# Optimizing a Trainium2 kernel written in Bass

```python
import jax
import jax.numpy as jnp
from jax import lax
import numpy as np
import jax, jax.numpy as jnp

D_MODEL = 1024
BATCH = 1
SEQ = 256
DEPTH = 2

CHUNK = 64
HEAD_DIM = 64
QBLOCK = 128
ROPE_THETA = 10000.0
EPS = 1e-6
NEG = -1e30

A_HEADS = 8
IDX_HEADS = 4
IDX_DIM = 64
IDX_TOPK_MAX = 256
B_HEADS = 8
B_PAST_CHUNKS = 8
B_REL_CLIP = 256
C_HEADS = 8
D_HEADS = 8
D_KV_HEADS = 2
D_GROUP = D_HEADS // D_KV_HEADS
D_WINDOW = 128
D_WINDOW_CHUNKS = -(-D_WINDOW // CHUNK)
D_FF = 2816
CONV_WIDTH = 3

N_EVEN = (DEPTH + 1) // 2
N_ODD = DEPTH // 2

EVEN_SPLITS = (A_HEADS * HEAD_DIM, A_HEADS * HEAD_DIM, A_HEADS * HEAD_DIM,
               IDX_HEADS * IDX_DIM, IDX_DIM, IDX_HEADS,
               B_HEADS * HEAD_DIM, B_HEADS * HEAD_DIM, B_HEADS * HEAD_DIM)
ODD_SPLITS = (C_HEADS * HEAD_DIM, C_HEADS * HEAD_DIM, C_HEADS * HEAD_DIM, C_HEADS,
              D_HEADS * HEAD_DIM, D_KV_HEADS * HEAD_DIM, D_KV_HEADS * HEAD_DIM)
EVEN_IN = sum(EVEN_SPLITS)
ODD_IN = sum(ODD_SPLITS)
EVEN_OUT = (A_HEADS + B_HEADS) * HEAD_DIM
ODD_OUT = (C_HEADS + D_HEADS) * HEAD_DIM


def _split(t, sizes):
    return jnp.split(t, np.cumsum(sizes)[:-1].tolist(), axis=-1)

def rms_norm(x, g):
    xf = x.astype(jnp.float32)
    y = xf * lax.rsqrt(jnp.mean(xf * xf, axis=-1, keepdims=True) + EPS)
    return (y * g.astype(jnp.float32)).astype(x.dtype)

def layer_norm(x, g, b):
    xf = x.astype(jnp.float32)
    xc = xf - jnp.mean(xf, axis=-1, keepdims=True)
    y = xc * lax.rsqrt(jnp.mean(xc * xc, axis=-1, keepdims=True) + EPS)
    return (y * g.astype(jnp.float32) + b.astype(jnp.float32)).astype(x.dtype)

def rope_tables(seq, dim):
    inv = 1.0 / (ROPE_THETA ** (jnp.arange(0, dim, 2, dtype=jnp.float32) / dim))
    ang = jnp.arange(seq, dtype=jnp.float32)[:, None] * inv[None, :]
    return jnp.cos(ang), jnp.sin(ang)

def apply_rope(t, cos, sin):
    half = t.shape[-1] // 2
    shape = (1, t.shape[1]) + (1,) * (t.ndim - 3) + (half,)
    c = cos.reshape(shape)
    s = sin.reshape(shape)
    tf = t.astype(jnp.float32)
    t1, t2 = tf[..., :half], tf[..., half:]
    return jnp.concatenate([t1 * c - t2 * s, t2 * c + t1 * s], axis=-1).astype(t.dtype)

def dsa_sparse_attention(q, k, v, q_idx, k_idx, w_idx):
    bsz, seq, nh, dh = q.shape
    topk = min(IDX_TOPK_MAX, seq // 4)
    key_chunk = jnp.arange(seq) // CHUNK
    scale = dh ** -0.5

    def block(i):
        start = i * QBLOCK
        qb = lax.dynamic_slice_in_dim(q, start, QBLOCK, 1)
        qib = lax.dynamic_slice_in_dim(q_idx, start, QBLOCK, 1)
        wib = lax.dynamic_slice_in_dim(w_idx, start, QBLOCK, 1).astype(jnp.float32)
        q_chunk = (start + jnp.arange(QBLOCK)) // CHUNK
        admissible = key_chunk[None, :] <= q_chunk[:, None]
        rel = jax.nn.relu(jnp.einsum('bqhd,bsd->bqhs', qib, k_idx).astype(jnp.float32))
        score = jnp.einsum('bqhs,bqh->bqs', rel, wib)
        score = jnp.where(admissible[None], score, NEG)
        _, idx = lax.top_k(score, topk)
        valid = key_chunk[idx] <= q_chunk[None, :, None]
        k_sel = jax.vmap(lambda kb, ib: kb[ib])(k, idx)
        v_sel = jax.vmap(lambda vb, ib: vb[ib])(v, idx)
        logits = jnp.einsum('bqhd,bqkhd->bhqk', qb, k_sel).astype(jnp.float32) * scale
        logits = jnp.where(valid[:, None], logits, NEG)
        p = jax.nn.softmax(logits, axis=-1).astype(v.dtype)
        return jnp.einsum('bhqk,bqkhd->bqhd', p, v_sel)

    out = lax.map(block, jnp.arange(seq // QBLOCK))
    return jnp.moveaxis(out, 0, 1).reshape(bsz, seq, nh, dh)

def chunked_relpos_attention(q, k, v, rel_bias):
    bsz, seq, nh, dh = q.shape
    pad = B_PAST_CHUNKS * CHUNK
    band = pad + CHUNK
    kp = jnp.pad(k, ((0, 0), (pad, 0), (0, 0), (0, 0)))
    vp = jnp.pad(v, ((0, 0), (pad, 0), (0, 0), (0, 0)))
    kj = jnp.arange(band)
    dist = jnp.arange(CHUNK)[:, None] + pad - kj[None, :]
    bias = rel_bias[:, jnp.clip(dist, -B_REL_CLIP, B_REL_CLIP) + B_REL_CLIP].astype(jnp.float32)
    scale = dh ** -0.5

    def chunk(c):
        start = c * CHUNK
        qc = lax.dynamic_slice_in_dim(q, start, CHUNK, 1)
        kc = lax.dynamic_slice_in_dim(kp, start, band, 1)
        vc = lax.dynamic_slice_in_dim(vp, start, band, 1)
        valid = kj >= pad - start
        logits = jnp.einsum('bqhd,bshd->bhqs', qc, kc).astype(jnp.float32) * scale + bias[None]
        logits = jnp.where(valid, logits, NEG)
        p = jax.nn.softmax(logits, axis=-1).astype(v.dtype)
        return jnp.einsum('bhqs,bshd->bqhd', p, vc)

    out = lax.map(chunk, jnp.arange(seq // CHUNK))
    return jnp.moveaxis(out, 0, 1).reshape(bsz, seq, nh, dh)

def forgetting_attention(q, k, v, log_f):
    bsz, seq, nh, dh = q.shape
    f_cum = jnp.moveaxis(lax.cumsum(log_f, axis=1), 1, 2)
    pos = jnp.arange(seq)
    scale = dh ** -0.5

    def block(i):
        start = i * QBLOCK
        qb = lax.dynamic_slice_in_dim(q, start, QBLOCK, 1)
        fq = lax.dynamic_slice_in_dim(f_cum, start, QBLOCK, 2)
        causal = pos[None, :] <= (start + jnp.arange(QBLOCK))[:, None]
        logits = (jnp.einsum('bqhd,bshd->bhqs', qb, k).astype(jnp.float32) * scale
                  + fq[..., None] - f_cum[:, :, None, :])
        logits = jnp.where(causal, logits, NEG)
        p = jax.nn.softmax(logits, axis=-1).astype(v.dtype)
        return jnp.einsum('bhqs,bshd->bqhd', p, v)

    out = lax.map(block, jnp.arange(seq // QBLOCK))
    return jnp.moveaxis(out, 0, 1).reshape(bsz, seq, nh, dh)

def sink_window_gqa(q, k, v, sinks):
    bsz, seq, nh, dh = q.shape
    nb = seq // QBLOCK
    qb = q.reshape(bsz, nb, QBLOCK, D_KV_HEADS, D_GROUP, dh)
    kb = k.reshape(bsz, nb, QBLOCK, D_KV_HEADS, dh)
    vb = v.reshape(bsz, nb, QBLOCK, D_KV_HEADS, dh)
    kprev = jnp.pad(kb, ((0, 0), (1, 0), (0, 0), (0, 0), (0, 0)))[:, :-1]
    vprev = jnp.pad(vb, ((0, 0), (1, 0), (0, 0), (0, 0), (0, 0)))[:, :-1]
    kband = jnp.concatenate([kprev, kb], axis=2)
    vband = jnp.concatenate([vprev, vb], axis=2)
    sk = jnp.arange(2 * QBLOCK) - QBLOCK
    cdiff = jnp.arange(QBLOCK)[:, None] // CHUNK - sk[None, :] // CHUNK
    band_mask = (cdiff >= 0) & (cdiff <= D_WINDOW_CHUNKS)
    mask = band_mask[None] & ((jnp.arange(nb)[:, None, None] > 0) | (sk >= 0)[None, None, :])
    logits = jnp.einsum('bnqkgd,bnskd->bnkgqs', qb, kband).astype(jnp.float32) * (dh ** -0.5)
    logits = jnp.where(mask[None, :, None, None], logits, NEG)
    sink_col = jnp.broadcast_to(
        sinks.reshape(D_KV_HEADS, D_GROUP).astype(jnp.float32)[None, None, :, :, None, None],
        logits.shape[:-1] + (1,))
    p = jax.nn.softmax(jnp.concatenate([logits, sink_col], axis=-1), axis=-1)[..., :-1]
    out = jnp.einsum('bnkgqs,bnskd->bnqkgd', p.astype(v.dtype), vband)
    return out.reshape(bsz, seq, nh, dh)

def conv_gated_ffn(x, w_up, conv_w, conv_b, w_down):
    h = x @ w_up
    c = h.shape[-1]
    h = lax.conv_general_dilated(
        h, conv_w.reshape(CONV_WIDTH, 1, c).astype(h.dtype), window_strides=(1,),
        padding=[(CONV_WIDTH - 1, 0)], dimension_numbers=('NWC', 'WIO', 'NWC'),
        feature_group_count=c) + conv_b.astype(h.dtype)
    g, u = jnp.split(h, 2, axis=-1)
    return (jax.nn.silu(g) * u) @ w_down

def even_mixer(xn, w_in, w_out, k_ln_g, k_ln_b, rel_bias, rope_h, rope_i):
    bsz, seq, _ = xn.shape
    qa, ka, va, qi, ki, wi, qb, kb, vb = _split(xn @ w_in, EVEN_SPLITS)
    heads = lambda t, n: t.reshape(bsz, seq, n, HEAD_DIM)
    qa = apply_rope(heads(qa, A_HEADS), *rope_h)
    ka = apply_rope(heads(ka, A_HEADS), *rope_h)
    qi = apply_rope(qi.reshape(bsz, seq, IDX_HEADS, IDX_DIM), *rope_i)
    ki = apply_rope(layer_norm(ki, k_ln_g, k_ln_b), *rope_i)
    ya = dsa_sparse_attention(qa, ka, heads(va, A_HEADS), qi, ki, wi)
    yb = chunked_relpos_attention(heads(qb, B_HEADS), heads(kb, B_HEADS), heads(vb, B_HEADS), rel_bias)
    y = jnp.concatenate([ya.reshape(bsz, seq, -1), yb.reshape(bsz, seq, -1)], axis=-1)
    return y @ w_out

def odd_mixer(xn, w_in, w_out, forget_b, sinks, rope_h):
    bsz, seq, _ = xn.shape
    qc, kc, vc, fc, qd, kd, vd = _split(xn @ w_in, ODD_SPLITS)
    heads = lambda t, n: t.reshape(bsz, seq, n, HEAD_DIM)
    log_f = jax.nn.log_sigmoid(fc.astype(jnp.float32) + forget_b.astype(jnp.float32))
    yc = forgetting_attention(heads(qc, C_HEADS), heads(kc, C_HEADS), heads(vc, C_HEADS), log_f)
    yd = sink_window_gqa(apply_rope(heads(qd, D_HEADS), *rope_h),
                         apply_rope(heads(kd, D_KV_HEADS), *rope_h),
                         heads(vd, D_KV_HEADS), sinks)
    y = jnp.concatenate([yc.reshape(bsz, seq, -1), yd.reshape(bsz, seq, -1)], axis=-1)
    return y @ w_out

def first_inputs(seed: int = 0) -> dict:
    key = jax.random.key(seed)
    ks = jax.random.split(key, 17)
    f32 = jnp.float32
    nrm = lambda k, shape, s: jax.random.normal(k, shape, f32) * s
    return {
        'x': nrm(ks[0], (BATCH, SEQ, D_MODEL), 1.0),
        'norm_mix_g': 1.0 + nrm(ks[1], (DEPTH, D_MODEL), 0.1),
        'norm_ffn_g': 1.0 + nrm(ks[2], (DEPTH, D_MODEL), 0.1),
        'norm_out_g': 1.0 + nrm(ks[3], (D_MODEL,), 0.1),
        'even_w_in': nrm(ks[4], (N_EVEN, D_MODEL, EVEN_IN), D_MODEL ** -0.5),
        'even_w_out': nrm(ks[5], (N_EVEN, EVEN_OUT, D_MODEL), EVEN_OUT ** -0.5),
        'idx_k_ln_g': 1.0 + nrm(ks[6], (N_EVEN, IDX_DIM), 0.1),
        'idx_k_ln_b': nrm(ks[7], (N_EVEN, IDX_DIM), 0.02),
        'rel_bias': nrm(ks[8], (N_EVEN, B_HEADS, 2 * B_REL_CLIP + 1), 0.5),
        'odd_w_in': nrm(ks[9], (N_ODD, D_MODEL, ODD_IN), D_MODEL ** -0.5),
        'odd_w_out': nrm(ks[10], (N_ODD, ODD_OUT, D_MODEL), ODD_OUT ** -0.5),
        'forget_b': jax.random.uniform(ks[11], (N_ODD, C_HEADS), f32, 1.0, 5.0),
        'sinks': nrm(ks[12], (N_ODD, D_HEADS), 1.0),
        'ffn_w_up': nrm(ks[13], (DEPTH, D_MODEL, 2 * D_FF), D_MODEL ** -0.5),
        'ffn_conv_w': nrm(ks[14], (DEPTH, CONV_WIDTH, 2 * D_FF), CONV_WIDTH ** -0.5),
        'ffn_conv_b': nrm(ks[15], (DEPTH, 2 * D_FF), 0.02),
        'ffn_w_down': nrm(ks[16], (DEPTH, D_FF, D_MODEL), D_FF ** -0.5),
    }

def first_block(x, norm_mix_g, norm_ffn_g, norm_out_g, even_w_in, even_w_out, idx_k_ln_g, idx_k_ln_b,
              rel_bias, odd_w_in, odd_w_out, forget_b, sinks, ffn_w_up, ffn_conv_w, ffn_conv_b, ffn_w_down):
    seq = x.shape[1]
    rope_h = rope_tables(seq, HEAD_DIM)
    rope_i = rope_tables(seq, IDX_DIM)
    h = x
    for layer in range(DEPTH):
        j = layer // 2
        xn = rms_norm(h, norm_mix_g[layer])
        if layer % 2 == 0:
            mix = even_mixer(xn, even_w_in[j], even_w_out[j], idx_k_ln_g[j], idx_k_ln_b[j],
                             rel_bias[j], rope_h, rope_i)
        else:
            mix = odd_mixer(xn, odd_w_in[j], odd_w_out[j], forget_b[j], sinks[j], rope_h)
        h = h + mix
        h = h + conv_gated_ffn(rms_norm(h, norm_ffn_g[layer]), ffn_w_up[layer], ffn_conv_w[layer],
                               ffn_conv_b[layer], ffn_w_down[layer])
    return rms_norm(h, norm_out_g)


DEPTH_2 = 1

CONV_CH = D_MODEL
CONV_K = 31
HEAD_DIM_2 = 128
N_HEADS = D_MODEL // HEAD_DIM_2
DELTA_W = N_HEADS * HEAD_DIM_2
SHORT_CONV = 5
N_DIR = 2
D_FF_2 = -(-8 * D_MODEL // (3 * 256)) * 256
PLE_DIM = 256
NORM_EPS = 1e-6
LN_EPS = 1e-5
IN_SIZES = (CONV_CH, CONV_CH, DELTA_W, DELTA_W, DELTA_W, DELTA_W,
            N_DIR * N_HEADS, N_DIR * N_HEADS, D_MODEL, D_MODEL)
IN_TOTAL = sum(IN_SIZES)


def rms_norm_2(x, g):
    xf = x.astype(jnp.float32)
    y = xf * lax.rsqrt(jnp.mean(xf * xf, axis=-1, keepdims=True) + NORM_EPS)
    return (y * g.astype(jnp.float32)).astype(x.dtype)

def layer_norm_2(x, g, b):
    xf = x.astype(jnp.float32)
    mu = jnp.mean(xf, axis=-1, keepdims=True)
    xc = xf - mu
    y = xc * lax.rsqrt(jnp.mean(xc * xc, axis=-1, keepdims=True) + LN_EPS)
    return (y * g.astype(jnp.float32) + b.astype(jnp.float32)).astype(x.dtype)

def l2_norm(x):
    xf = x.astype(jnp.float32)
    return xf * lax.rsqrt(jnp.sum(xf * xf, axis=-1, keepdims=True) + NORM_EPS)

def depthwise_conv(x, w):
    k = w.shape[0]
    return lax.conv_general_dilated(
        x, w[:, None, :].astype(x.dtype), window_strides=(1,),
        padding=[(k // 2, k // 2)], dimension_numbers=("NWC", "WIO", "NWC"),
        feature_group_count=x.shape[-1])

def split_cols(t, sizes):
    out, start = [], 0
    for s in sizes:
        out.append(t[..., start:start + s])
        start += s
    return out

def gated_delta_rule(q, k, v, g, beta):
    out_dtype = v.dtype
    bsz, t_len, n_h, _ = q.shape
    n_blk = t_len // CHUNK

    def blocks(t):
        t = t.astype(jnp.float32).reshape((bsz, n_blk, CHUNK, n_h) + t.shape[3:])
        return jnp.moveaxis(t, 3, 1)

    q, k, v, g, beta = (blocks(t) for t in (q, k, v, g, beta))
    g = jnp.cumsum(g, axis=-1)
    idx = jnp.arange(CHUNK)
    tri_incl = idx[:, None] >= idx[None, :]
    tri_strict = idx[:, None] > idx[None, :]
    decay = jnp.exp(jnp.where(tri_incl, g[..., :, None] - g[..., None, :], -jnp.inf))
    k_beta = k * beta[..., None]
    lower = jnp.where(tri_strict, jnp.einsum('bhncd,bhnsd->bhncs', k_beta, k) * decay, 0.0)
    dv = v.shape[-1]
    rhs = jnp.concatenate([v * beta[..., None], k_beta * jnp.exp(g)[..., None]], axis=-1)
    sol = lax.linalg.triangular_solve(lower, rhs, left_side=True, lower=True, unit_diagonal=True)
    u, w = sol[..., :dv], sol[..., dv:]
    qk = jnp.einsum('bhncd,bhnsd->bhncs', q, k) * decay
    g_last = g[..., -1]
    q_dec = q * jnp.exp(g)[..., None]
    k_tail = k * jnp.exp(g_last[..., None] - g)[..., None]

    def step(state, xs):
        qd, kt, ui, wi, qki, gl = xs
        v_new = ui - jnp.einsum('bhck,bhkv->bhcv', wi, state)
        o = jnp.einsum('bhck,bhkv->bhcv', qd, state) + jnp.einsum('bhcs,bhsv->bhcv', qki, v_new)
        state = state * jnp.exp(gl)[..., None, None] + jnp.einsum('bhck,bhcv->bhkv', kt, v_new)
        return state, o

    xs = tuple(jnp.moveaxis(t, 2, 0) for t in (q_dec, k_tail, u, w, qk, g_last))
    s0 = jnp.zeros((bsz, n_h, q.shape[-1], dv), jnp.float32)
    _, o = lax.scan(step, s0, xs)
    o = jnp.transpose(o, (1, 0, 3, 2, 4)).reshape(bsz, t_len, n_h, dv)
    return o.astype(out_dtype)

def second_inputs(seed: int = 0) -> dict:
    key = jax.random.key(seed)
    ks = jax.random.split(key, 32)
    f32 = jnp.float32

    def nrm(k, shape, fan_in):
        return jax.random.normal(k, shape, f32) * (fan_in ** -0.5)

    def gain(k, shape):
        return 1.0 + 0.05 * jax.random.normal(k, shape, f32)

    def small(k, shape):
        return 0.01 * jax.random.normal(k, shape, f32)

    a_log = jnp.log(jax.random.uniform(ks[10], (DEPTH_2, N_DIR, N_HEADS), f32, 1.0, 16.0))
    dt = jnp.exp(jax.random.uniform(ks[11], (DEPTH_2, N_DIR, N_HEADS), f32,
                                    float(np.log(1e-3)), float(np.log(1e-1))))
    dt_bias = dt + jnp.log(-jnp.expm1(-dt))
    return {
        "x": jax.random.normal(ks[0], (BATCH, SEQ, D_MODEL), f32),
        "p": jax.random.normal(ks[1], (DEPTH_2, BATCH, SEQ, PLE_DIM), f32),
        "g_mix": gain(ks[2], (DEPTH_2, D_MODEL)),
        "w_in": nrm(ks[3], (DEPTH_2, D_MODEL, IN_TOTAL), D_MODEL),
        "conv_dw_w": nrm(ks[4], (DEPTH_2, CONV_K, CONV_CH), CONV_K),
        "conv_dw_b": small(ks[5], (DEPTH_2, CONV_CH)),
        "conv_ln_g": gain(ks[6], (DEPTH_2, CONV_CH)),
        "conv_ln_b": small(ks[7], (DEPTH_2, CONV_CH)),
        "w_conv_out": nrm(ks[8], (DEPTH_2, CONV_CH, D_MODEL), CONV_CH),
        "qkv_conv_w": nrm(ks[9], (DEPTH_2, SHORT_CONV, 3 * DELTA_W), SHORT_CONV),
        "a_log": a_log,
        "dt_bias": dt_bias,
        "delta_norm_g": gain(ks[12], (DEPTH_2, HEAD_DIM_2)),
        "w_delta_out": nrm(ks[13], (DEPTH_2, DELTA_W, D_MODEL), DELTA_W),
        "w_o": nrm(ks[14], (DEPTH_2, D_MODEL, D_MODEL), D_MODEL),
        "g_ffn": gain(ks[15], (DEPTH_2, D_MODEL)),
        "w_gate_up": nrm(ks[16], (DEPTH_2, D_MODEL, 2 * D_FF_2), D_MODEL),
        "w_down": nrm(ks[17], (DEPTH_2, D_FF_2, D_MODEL), D_FF_2),
        "g_pl": gain(ks[18], (DEPTH_2, D_MODEL)),
        "w_pl_gate": nrm(ks[19], (DEPTH_2, D_MODEL, D_MODEL), D_MODEL),
        "w_pl_proj": nrm(ks[20], (DEPTH_2, PLE_DIM, D_MODEL), PLE_DIM),
        "g_pl_proj": gain(ks[21], (DEPTH_2, D_MODEL)),
        "g_final": gain(ks[22], (D_MODEL,)),
    }

def second_block(x, p, g_mix, w_in, conv_dw_w, conv_dw_b, conv_ln_g, conv_ln_b, w_conv_out,
              qkv_conv_w, a_log, dt_bias, delta_norm_g, w_delta_out, w_o, g_ffn,
              w_gate_up, w_down, g_pl, w_pl_gate, w_pl_proj, g_pl_proj, g_final):
    bsz, t_len, _ = x.shape
    for i in range(DEPTH_2):
        h = rms_norm_2(x, g_mix[i])
        proj = h @ w_in[i]
        glu_a, glu_b, q, k, v, z, a_in, b_in, gate_a, gate_b = split_cols(proj, IN_SIZES)

        c = glu_a * jax.nn.sigmoid(glu_b)
        c = depthwise_conv(c, conv_dw_w[i]) + conv_dw_b[i]
        c = jax.nn.silu(layer_norm_2(c, conv_ln_g[i], conv_ln_b[i]))
        y_conv = c @ w_conv_out[i]

        qkv = jax.nn.silu(depthwise_conv(jnp.concatenate([q, k, v], axis=-1), qkv_conv_w[i]))
        q, k, v = split_cols(qkv, (DELTA_W, DELTA_W, DELTA_W))
        q = l2_norm(q.reshape(bsz, t_len, N_HEADS, HEAD_DIM_2)) * (HEAD_DIM_2 ** -0.5)
        k = l2_norm(k.reshape(bsz, t_len, N_HEADS, HEAD_DIM_2))
        v = v.reshape(bsz, t_len, N_HEADS, HEAD_DIM_2)
        a_in = a_in.astype(jnp.float32).reshape(bsz, t_len, N_DIR, N_HEADS)
        b_in = b_in.astype(jnp.float32).reshape(bsz, t_len, N_DIR, N_HEADS)
        g = -jnp.exp(a_log[i].astype(jnp.float32)) * jax.nn.softplus(a_in + dt_bias[i].astype(jnp.float32))
        beta = jax.nn.sigmoid(b_in)
        o_fwd = gated_delta_rule(q, k, v, g[:, :, 0], beta[:, :, 0])
        rev = lambda t: jnp.flip(t, axis=1)
        o_bwd = rev(gated_delta_rule(rev(q), rev(k), rev(v), rev(g[:, :, 1]), rev(beta[:, :, 1])))
        o = rms_norm_2(o_fwd + o_bwd, delta_norm_g[i]) * jax.nn.silu(z.reshape(bsz, t_len, N_HEADS, HEAD_DIM_2))
        y_delta = o.reshape(bsz, t_len, DELTA_W).astype(x.dtype) @ w_delta_out[i]

        y = jax.nn.sigmoid(gate_a) * y_conv + jax.nn.sigmoid(gate_b) * y_delta
        x = x + y @ w_o[i]

        h = rms_norm_2(x, g_ffn[i])
        gt, up = split_cols(h @ w_gate_up[i], (D_FF_2, D_FF_2))
        x = x + (jax.nn.silu(gt) * up) @ w_down[i]

        pl = rms_norm_2(p[i] @ w_pl_proj[i], g_pl_proj[i])
        x = x + jax.nn.sigmoid(rms_norm_2(x, g_pl[i]) @ w_pl_gate[i]) * pl
    return rms_norm_2(x, g_final)


def setup_inputs(seed=0):
    out = dict(first_inputs(seed))
    for name, value in second_inputs(seed + 1).items():
        if name != "x":
            out[name + "_2"] = value
    return out


def reference(
    x, norm_mix_g, norm_ffn_g, norm_out_g, even_w_in, even_w_out, idx_k_ln_g, idx_k_ln_b,
    rel_bias, odd_w_in, odd_w_out, forget_b, sinks, ffn_w_up, ffn_conv_w, ffn_conv_b,
    ffn_w_down, p_2, g_mix_2, w_in_2, conv_dw_w_2, conv_dw_b_2, conv_ln_g_2, conv_ln_b_2,
    w_conv_out_2, qkv_conv_w_2, a_log_2, dt_bias_2, delta_norm_g_2, w_delta_out_2, w_o_2,
    g_ffn_2, w_gate_up_2, w_down_2, g_pl_2, w_pl_gate_2, w_pl_proj_2, g_pl_proj_2, g_final_2,
):
    x = first_block(
        x, norm_mix_g, norm_ffn_g, norm_out_g, even_w_in, even_w_out, idx_k_ln_g, idx_k_ln_b,
        rel_bias, odd_w_in, odd_w_out, forget_b, sinks, ffn_w_up, ffn_conv_w, ffn_conv_b,
        ffn_w_down,
    )
    return second_block(
        x, p_2, g_mix_2, w_in_2, conv_dw_w_2, conv_dw_b_2, conv_ln_g_2, conv_ln_b_2,
        w_conv_out_2, qkv_conv_w_2, a_log_2, dt_bias_2, delta_norm_g_2, w_delta_out_2, w_o_2,
        g_ffn_2, w_gate_up_2, w_down_2, g_pl_2, w_pl_gate_2, w_pl_proj_2, g_pl_proj_2,
        g_final_2,
    )


_drawn_inputs = setup_inputs


def setup_inputs(seed=0):
    import zlib

    import numpy as np

    out = dict(_drawn_inputs(seed))
    spreads = {}
    factors = {'sinks': 8.0,
     'conv_dw_b_2': 8.0,
     'conv_ln_g_2': 3.172,
     'conv_ln_b_2': 26.839,
     'delta_norm_g_2': 3.784,
     'g_pl_2': 23.722,
     'g_pl_proj_2': 9.739,
     'g_ffn_2': 2.715}
    for name, (base, spread) in spreads.items():
        noise = np.random.default_rng([zlib.crc32(name.encode()), seed]).standard_normal(out[name].shape)
        drawn = base * np.exp(spread * noise) if base else spread * noise
        out[name] = jnp.asarray(drawn.astype(out[name].dtype))
    for name, factor in factors.items():
        out[name] = (out[name] * factor).astype(out[name].dtype)
    return out
```

```python
from contextlib import ExitStack

import numpy as np

import concourse.bass as bass
from concourse import mybir

ALU = mybir.AluOpType
ACT = mybir.ActivationFunctionType
AX = mybir.AxisListType
F32 = mybir.dt.float32
F32R = mybir.dt.float32r

P = 128
TOK = 256
TT = TOK // P
D = 1024
KT = D // P
HD = 64
FF = 2816
FT = FF // P
EPS = 1e-6
SLOT = 2048
RAW = 3
RING = 3
AHEAD = RING - 1
MASKED = -8e30
TAKEN = -3e38



def stream_plan():
    plan = []

    def rows_major(key, weight, pieces):
        for half in range(2):
            plan.append(("columns", key, weight, pieces, half))

    def pair(key, weight, a, b):
        plan.append(("pair", key, weight, a, b))

    def down(key, weight, tiles):
        for i in range(tiles // 2):
            plan.append(("down", (key, i), weight, i))

    for key, a, n in EVEN_BLOCKS:
        rows_major(("even", key), ("even_w_in", 0), [(a, n)])
    down("even_out", ("even_w_out", 0), KT)
    for layer in range(2):
        if layer == 1:
            for key, pieces in ODD_BLOCKS:
                rows_major(("odd", key), ("odd_w_in", 0), pieces)
            down("odd_out", ("odd_w_out", 0), KT)
        for j in range(FT):
            pair((f"up{layer}", j), ("ffn_w_up", layer), j * P, FF + j * P)
        down(f"down{layer}", ("ffn_w_down", layer), FT)
    plan.append(("narrow", "ab", ("w_in_2", 0), 6144, 32))
    for round_ in ROUNDS:
        for key, weight, a, b in round_:
            pair(key, (weight, 0), a, b)
    for i in range(KT // 2):
        pair(("delta_out", i), ("w_delta_out_2", 0), 2 * i * P, (2 * i + 1) * P)
    down("mix_out", ("w_o_2", 0), KT)
    for j in range(FT):
        pair(("up2", j), ("w_gate_up_2", 0), j * P, FF + j * P)
    down("down2", ("w_down_2", 0), FT)
    down("pl_proj", ("w_pl_proj_2", 0), 2)
    for i in range(2):
        rows_major(("gate", i), ("w_pl_gate_2", 0), [(i * 512, 512)])
    return plan


def rounds():
    glu = [(("glu", j), "w_in_2", j * P, 1024 + j * P) for j in range(KT)]
    gates = [(("gates", j), "w_in_2", 6176 + j * P, 7200 + j * P) for j in range(KT)]
    z = [(("z", j), "w_in_2", 5120 + 2 * j * P, 5120 + (2 * j + 1) * P) for j in range(KT // 2)]
    out = [(("conv_out", i), "w_conv_out_2", 2 * i * P, (2 * i + 1) * P) for i in range(KT // 2)]
    other = [glu[0:2], [z[0]] + glu[2:4], [glu[4], z[1]], [z[2], glu[5], z[3]], [glu[6], gates[0]],
             [glu[7]] + gates[1:3], gates[3:5], gates[5:8]]
    made = []
    for r in range(HEADS):
        slots = [(("qk", r), "w_in_2", 2048 + r * P, 3072 + r * P)]
        if r % 2 == 0:
            slots.append((("v", r // 2), "w_in_2", 4096 + r * P, 4096 + (r + 1) * P))
        made.append(slots + other[r])
    return made + [[], out]


HEADS = 8
CHUNK = 64
LEVELS = [2, 4, 8, 16, 32]
TICKS = 8
ROUNDS = rounds()


EVEN_BLOCKS = [("idx", 1536, 324), ("qa", 0, 512), ("ka", 512, 512), ("va", 1024, 512),
               ("qb", 1860, 512), ("kb", 2372, 512), ("vb", 2884, 512)]
ODD_BLOCKS = [("kvf", [(2056, 256), (1536, 8)]), ("qd", [(1544, 512)]), ("qc", [(0, 512)]),
              ("kc", [(512, 512)]), ("vc", [(1024, 512)])]


def pack_stream(inputs):
    plan = stream_plan()
    out = np.zeros((len(plan), P, SLOT), np.float32)
    for n, (kind, _, (name, i), *args) in enumerate(plan):
        w = inputs[name][i]
        if kind == "columns":
            pieces, half = args
            view = out[n].reshape(P, 4, 512)
            at = 0
            for a, c in pieces:
                view[:, :, at:at + c] = w[half * 512:(half + 1) * 512, a:a + c].reshape(4, P, c).transpose(1, 0, 2)
                at += c
        elif kind == "pair":
            view = out[n].reshape(P, KT, 2, P)
            for m, a in enumerate(args):
                view[:, :, m, :] = w[:, a:a + P].reshape(KT, P, P).transpose(1, 0, 2)
        elif kind == "narrow":
            a, c = args
            out[n].reshape(P, KT, 256)[:, :, 0:c] = w[:, a:a + c].reshape(KT, P, c).transpose(1, 0, 2)
        elif kind == "down":
            view = out[n].reshape(P, 2, D)
            view[:] = w[args[0] * 256:args[0] * 256 + 256].reshape(2, P, D).transpose(1, 0, 2)
    return out


class Packer:

    def __init__(self):
        self.at, self.parts, self.n = {}, [], 0

    def add(self, name, a):
        a = np.ascontiguousarray(a, np.float32).reshape(P, -1)
        self.at[name] = (self.n, a.shape[1])
        self.n += a.shape[1]
        self.parts.append(a)

    def packed(self):
        return np.concatenate(self.parts, 1), self.at


def constants_1():
    c = Packer()
    p = np.arange(P)[:, None]
    s = np.arange(TOK)[None, :]
    causal, window = [], []
    for t in range(TT):
        w = P * (t + 1)
        q = t * P + p
        causal.append(np.where(s[:, :w] <= q, 0.0, MASKED))
        near = q // 64 - s[:, :w] // 64
        window.append(np.where((near >= 0) & (near <= 2), 0.0, MASKED))
    c.add("causal", np.concatenate(causal, 1))
    c.add("window", np.concatenate(window, 1))
    c.add("upto", np.stack([(t * P + p <= s) for t in range(TT)], 1))
    half = np.arange(0, HD, 2, dtype=np.float32)
    inv = (np.float32(1.0) / (np.float32(10000.0) ** (half / np.float32(HD)))).astype(np.float32)
    ang = (np.arange(TOK, dtype=np.float32)[:, None] * inv[None]).astype(np.float32).astype(np.float64)
    cos, sin = np.cos(ang), np.sin(ang)
    tiled = lambda a: a.reshape(TT, P, HD).transpose(1, 0, 2)
    c.add("cos", tiled(np.concatenate([cos, cos], 1)))
    c.add("sin", tiled(np.concatenate([-sin, sin], 1)))
    return c.packed()


def constants_2():
    c = Packer()
    k = np.arange(P)[:, None]
    m = np.arange(P)[None, :]
    same = k // CHUNK == m // CHUNK
    both = lambda forward, backward: np.stack([forward, backward], 1).astype(np.float32)
    c.add("cum", both(same & (k <= m), same & (k >= m)))
    c.add("tail", both(same & (k > m), same & (k < m)))
    c.add("off", np.where(both(same & (k <= m), same & (k >= m)) > 0, 0.0, -1e30))
    c.add("strict", both(same & (k < m), same & (k > m)))
    for b in [1] + LEVELS:
        joined = (k // (2 * b) == m // (2 * b)) & (k // b != m // b)
        c.add(f"join{b}", both(joined & (k < m), joined & (k > m)))
    c.add("half", np.concatenate([k // CHUNK == 0, k // CHUNK == 1], 1))
    c.add("mean", np.full((P, 1), 1.0 / D))
    return c.packed()


def pack_params_1(inputs):
    c = Packer()
    for layer in range(2):
        c.add(f"conv_w{layer}", inputs["ffn_conv_w"][layer].reshape(3, 2 * FT, P).transpose(2, 0, 1))
        c.add(f"conv_b{layer}", inputs["ffn_conv_b"][layer].reshape(2 * FT, P).T)
    return c.packed()


def pack_params_2(inputs):
    c = Packer()
    c.add("taps5", inputs["qkv_conv_w_2"][0].reshape(5, 3 * HEADS, P).transpose(2, 0, 1))
    c.add("taps31", inputs["conv_dw_w_2"][0].reshape(31, KT, P).transpose(2, 0, 1))
    for name in ("conv_dw_b_2", "conv_ln_g_2", "conv_ln_b_2"):
        c.add(name, inputs[name][0].reshape(KT, P).T)
    return c.packed()


GAINS = [("norm_mix_g", 0), ("norm_ffn_g", 0), ("norm_mix_g", 1), ("norm_ffn_g", 1), ("norm_out_g", None),
         ("g_mix_2", 0), ("g_ffn_2", 0), ("g_pl_2", 0), ("g_final_2", None), ("g_pl_proj_2", 0)]
ROWS = [("idx_k_ln_g", 0, 64), ("idx_k_ln_b", 0, 64), ("forget_b", 0, 8), ("sinks", 0, 8),
        ("a_log_2", 0, 16), ("dt_bias_2", 0, 16), ("delta_norm_g_2", 0, 128)]


def pack_gains(inputs):
    return np.stack([inputs[n] if i is None else inputs[n][i] for n, i in GAINS])


def pack_rows(inputs):
    return np.concatenate([inputs[n][i].reshape(-1) for n, i, _ in ROWS])[None]


def param_places():
    shapes = {"ffn_conv_w": (2, 3, 2 * FF), "ffn_conv_b": (2, 2 * FF), "qkv_conv_w_2": (1, 5, 3 * D), "conv_dw_w_2": (1, 31, D),
              "conv_dw_b_2": (1, D), "conv_ln_g_2": (1, D), "conv_ln_b_2": (1, D)}
    empty = {name: np.zeros(shape, np.float32) for name, shape in shapes.items()}
    return pack_params_1(empty)[1], pack_params_2(empty)[1]


PARAM1_AT, PARAM2_AT = param_places()



class Event:

    def __init__(self, sem, counted):
        self.sem, self.counted, self.values = sem, counted, {}

    def one(self, key=0):
        self.values[key] = len(self.values) + 1
        return self.sem, 1

    def at(self, key=0):
        return self.sem, self.counted[key] if self.counted else 1


EVENTS = {
    "weights_high": "slot n's rounded weights are written",
    "weights_low": "slot n's remainders are written, its raw weights no longer needed",
    "weights_used": "TensorE is done with slot n",
    "squared": "sum of squares of x, (k, t)",
    "rstd_ready": "both tiles' reciprocal deviations, k",
    "normed": "xn written, (k, t)",
    "norm_turned": "half of a tile of xn feature-major in its bank, (k, t, half)",
    "norm_high": "the same rounded into xhi",
    "norm_low": "the same's remainders in xlo",
    "x_added": "the residual is added to x, (k of the norm after it, t, half)",
    "rope_read": "rope has read a block's bank, (layer, b, t)",
    "rotated": "rope's result is written, (layer, b, t)",
    "copied": "a block that needs no rope is copied from its bank, (layer, b, t)",
    "block_turned": "a block is feature-major in its bank, (layer, b, t)",
    "turned_copied": "and copied to fm or fmi",
    "key_squares": "sum of squares of the centred keys, t",
    "key_rstd_ready": "their reciprocal deviations",
    "index_product": "queries times keys, u",
    "index_relu": "relu of the product, u",
    "index_sum": "and added to the score",
    "bias_ready": "half of the bias by distance is scaled and masked",
    "gate_abs": "absolute value of the forget gate's input",
    "gate_exp": "exp of minus that",
    "gate_ln": "ln(1 + that)",
    "gate_ready": "minus eight times the gate's logarithm",
    "nsink_ready": "minus the sinks",
    "forget_sum": "running sum of head h in its bank",
    "forget_bias": "bias of head h",
    "products": "queries times keys",
    "logits": "minus the logits, and the least of them",
    "exps": "exponentials and their sum",
    "sinks_done": "the sink's exponential, u",
    "probs": "probabilities",
    "probs_turned": "probabilities with the keys in the rows, in their bank",
    "probs_copied": "and copied to probT",
    "values_done": "probabilities times values",
    "mixed_high": "a pair of heads rounded into xhi, (layer, pair)",
    "mixed_low": "the pair's remainders in xlo",
    "conv_started": "newest tap and bias of gate or up channels, (layer, j, m)",
    "tap_one": "middle tap",
    "taps_done": "oldest tap",
    "gated": "silu of the gate channels",
    "hidden": "silu times up",
    "hidden_high": "the same rounded",
    "hidden_low": "the same's remainders",
    "ab_abs": "absolute value of the decay's input, all of ab read from its bank",
    "act_step": "exp of minus the absolute value; exp(a_log)",
    "ab_ln": "ln(1 + exp)",
    "beta_tanh": "tanh of half of beta's input",
    "decay_ready": "log decays",
    "beta_ready": "beta and minus beta",
    "decay_summed": "running sums, rests and totals of the log decays in bank 7",
    "exp_sums": "their exponentials",
    "neg_sum_made": "minus the running sums",
    "half_g_made": "scaled parameters of the convolution",
    "identr_made": "identity in the rounded type",
    "conv_begun": "middle tap, (key, m)",
    "tap5": "a tap of five, (key, k, m)",
    "taps5": "the last tap, (key, m)",
    "tanh_made": "tanh for a silu or sigmoid, by name",
    "conv_gated": "silu, doubled",
    "qk_turned": "q and k token-major in bank 2, h",
    "qk_squared": "sum of squares, (h, 2 * m + t)",
    "qk_rstd_ready": "reciprocal lengths, h",
    "qk_scaled": "normalized q or k, (h, 2 * m + t)",
    "qk_back": "q and k feature-major in bank 3, h",
    "qk_feat_made": "and copied",
    "v_turned": "v of heads 2i and 2i + 1 token-major in bank 2",
    "v_made": "and copied",
    "sums_spread": "running sums in every row of bank 2, h",
    "ratio_started": "and masked, h",
    "ratio_made": "ratio of decays, (h, y)",
    "qk_products": "keys times keys and queries in bank 3, h",
    "upper_made": "triangle of the systems, and q k times ratio, h",
    "inverse_begun": "inverse of the 2 x 2 blocks, transposed, h",
    "inverse_turned": "and not transposed in bank 4, h",
    "inverse_first": "and copied",
    "joint_made": "the part that joins the blocks of level i, (h, i)",
    "join_product": "it times the inverse in bank 4",
    "prod_made": "minus that, copied",
    "joined": "the next level's inverse transposed in bank 5, its change in bank 4",
    "inverse_t": "the inverse of level i - 1 transposed, copied",
    "inverse_done": "the inverse of level i",
    "from_one_made": "one minus the inverse, h",
    "check_product": "triangle times inverse in bank 4, h",
    "residual": "one minus the inverse's product, h",
    "correction": "refinement in bank 5, h",
    "solution_sum": "refined inverse, transposed, h",
    "solution": "solved values in bank 4 and keys in bank 5, h",
    "q_decayed_made": "queries times decay, (h, y)",
    "q_decayed_turned": "and feature-major in bank 3, h",
    "q_feat_made": "and copied",
    "k_decayed_made": "keys times decay, (h, y)",
    "k_rest_made": "keys times the decay after them, (h, y)",
    "values_made": "solved values times beta, (h, y)",
    "w_feat_made": "solved keys, feature-major, h",
    "recalled": "solved keys times state",
    "values_new": "new values",
    "o_product": "outputs of the chunk",
    "state_product": "keys times new values",
    "state_made": "state after the chunk",
    "o_added": "outputs copied or added",
    "o_squared": "sum of squares of the outputs, (h, t)",
    "o_rstd_ready": "their reciprocal deviations, h",
    "o_final": "outputs normalized and gated in xn, (h, t)",
    "glu_cleared": "zeros around glu's channels",
    "tanh_used": "the doubled product with the sigmoid is written",
    "z_made": "z's silu times the gain in xn, pair of heads",
    "slot_read_act": "tanh of both gates is written",
    "taps31": "a tap of channel tile j, (j, k)",
    "conv_mean": "mean in bank 2",
    "conv_centered": "mean subtracted",
    "conv_squared": "squares, q",
    "conv_square_used": "and their mean, q",
    "conv_var": "variance and epsilon",
    "conv_rstd": "reciprocal deviation",
    "conv_scaled": "times that, q",
    "conv_affine": "times gain plus bias, channel tile",
    "conv_tanh": "tanh of half, q",
    "conv_silu": "silu, doubled, q",
    "conv_high": "the same rounded into xhi",
    "conv_low": "the same's remainders in xlo",
    "conv_out_read": "product with the gate, of conv_out or delta_out, key of the slot",
    "mix_made": "sum of the two, q",
    "mix_high": "the same rounded into xhi",
    "mix_low": "the same's remainders in xlo",
    "p_turned": "p feature-major in bank 0",
    "p_high": "rounded",
    "p_low": "remainders",
    "pl_copied": "its projection, t",
    "pl_squared": "sum of squares, t",
    "pl_rstd_ready": "reciprocal deviations",
    "pl_made": "normalized, t",
    "gate_tanh_made": "tanh of half of the gate's input, (b, t)",
    "gate_tanh_used": "and added to x, (b, t)",
}


LAYERS = [("even", [(key, n) for key, _, n in EVEN_BLOCKS]),
          ("odd", [(key, sum(c for _, c in pieces)) for key, pieces in ODD_BLOCKS])]
ROTATED = {"idx", "qa", "ka", "kvf", "qd"}
TURNED = {"idx": 3, "qa": 4, "ka": 4, "qb": 4, "kb": 4, "kvf": 2, "qd": 4, "qc": 4, "kc": 4}
UNITS = {layer: [(kind, h, t) for kind in kinds for h in range(8) for t in range(TT)]
         for layer, kinds in (("even", "BA"), ("odd", "DC"))}
PAIR_OF = {kt: kt - 4 if kt >= 4 else kt + 4 for kt in range(KT)}
SLOT_OF_PAIR = {pair: kt for kt, pair in PAIR_OF.items()}
NORMS = len(GAINS) - 1


MIX_SLOTS = [("ab", -1, 0)] + [(slot[0], r, 2 * i) for r, slots in enumerate(ROUNDS) for i, slot in enumerate(slots)] \
    + [(("delta_out", i), len(ROUNDS), 0) for i in range(KT // 2)]
ORDINAL = {key: n for n, (key, _, _) in enumerate(MIX_SLOTS)}
READ_BY_ACT = {"gates"}
CONST1_AT, CONST2_AT = constants_1()[1], constants_2()[1]


CONVS = [key for key, _, _ in MIX_SLOTS if key[0] in ("qk", "v")]
ORDINAL_OF_CONV = {key: n for n, key in enumerate(CONVS)}


def tanh_order():
    order = []
    for r, slots in enumerate(ROUNDS):
        for i in range(TICKS):
            if r < HEADS and i == 2:
                order.append(("conv", ("qk", r)))
            if r < HEADS and r % 2 == 0 and i == 4:
                order.append(("conv", ("v", r // 2)))
            if i % 2 == 1 and i // 2 < len(slots) and slots[i // 2][0][0] in ("glu", "z"):
                order.append(slots[i // 2][0])
    return ({name: n % 2 for n, name in enumerate(order)},
            {name: order[n - 2] if n >= 2 else None for n, name in enumerate(order)},
            {n % 2: name for n, name in enumerate(order)})


TANH_OF, TANH_BEFORE, LAST_TANH = tanh_order()


def tap_schedule():
    ready = {key[1]: r * TICKS + tick + 1 for key, r, tick in MIX_SLOTS if key[0] == "glu"}
    ticks, todo, n = {}, [(j, k) for j in range(KT) for k in range(31)], 0
    for tick in range(TICKS * 8):
        left = TICKS * 8 - tick
        most = -(-len(todo) // left) + 1
        while todo and most and ready[todo[0][0]] < tick:
            ticks.setdefault(tick, []).append(todo.pop(0))
            most -= 1
    assert not todo
    return ticks


TAPS = tap_schedule()


def build(nc, dram, counted, stop=None):
    plan = stream_plan()
    const1_at, const2_at = CONST1_AT, CONST2_AT
    param1_at, param2_at = PARAM1_AT, PARAM2_AT
    slot_of = {}
    for n, entry in enumerate(plan):
        slot_of[(entry[1], entry[4]) if entry[0] == "columns" else entry[1]] = n
    ctx = ExitStack()
    with ctx:
        S = {name: Event(ctx.enter_context(nc.semaphore(name)), counted.get(name)) for name in EVENTS}
        x_loaded, ident_loaded, consts_loaded, params_loaded, rows_loaded, bias_loaded, gain_loaded, consts2_loaded, \
            params2_loaded, p_loaded, stored = [ctx.enter_context(nc.semaphore(name)) for name in (
                "x_loaded", "ident_loaded", "consts_loaded", "params_loaded", "rows_loaded", "bias_loaded", "gain_loaded",
                "consts2_loaded", "params2_loaded", "p_loaded", "stored")]
        weights_loaded = [ctx.enter_context(nc.semaphore(f"weights_loaded{i}")) for i in range(RAW)]
        dve_step, pool_step = [ctx.enter_context(nc.semaphore(name)) for name in ("dve_step", "pool_step")]

        def sb(name, shape, dt=F32, where=ctx):
            return where.enter_context(nc.sbuf_tensor(name, shape, dt))

        raw = sb("raw", [P, RAW, SLOT])
        whi = sb("whi", [P, RING, SLOT], F32R)
        wlo = sb("wlo", [P, RING, SLOT], F32R)
        x = sb("x", [P, TT, D])
        xn = sb("xn", [P, TT, D])
        xhi = sb("xhi", [P, KT, TOK], F32R)
        xlo = sb("xlo", [P, KT, TOK], F32R)
        gain = sb("gain", [P, D])
        ident = sb("ident", [P, P])[:, :]
        rows = sb("rows", [P, dram["rows"].shape[1]])
        sumsq = sb("sumsq", [P, TT])
        rstd = sb("rstd", [P, TT])
        half_power = sb("half_power", [P, 4])

        first = ExitStack()
        cst1 = sb("cst1", [P, dram["consts1"].shape[1]], F32, first)
        par1 = sb("par1", [P, dram["params1"].shape[1]], F32, first)
        with ExitStack() as area:
            hhi = sb("hhi", [P, FT, TOK], F32R, area)
            hlo = sb("hlo", [P, FT, TOK], F32R, area)
            cv = sb("cv", [P, 2, 2, TOK], F32, area)
            sg = sb("sg", [P, 2, TOK], F32, area)
            hf = sb("hf", [P, 2, TOK], F32, area)
        with ExitStack() as area:
            temp = sb("temp", [P, 2, TT, 512], F32, area)
            rope_a = sb("rope_a", [P, 512], F32, area)
            rope_b = sb("rope_b", [P, 512], F32, area)
            v0 = sb("v0", [P, TT, 512], F32, area)
            v1 = sb("v1", [P, TT, 512], F32, area)
            fm = sb("fm", [P, 4, 4, TOK], F32, area)
            fmi = sb("fmi", [P, 3, TOK], F32, area)
            bias = sb("bias", [P, 8, 384], F32, area)
            picked = sb("picked", [P, TT, TOK], F32, area)
            score = sb("score", [P, TT, TOK], F32, area)
            rel = sb("rel", [P, 2, TOK], F32, area)
            prob = sb("prob", [P, 3, TOK], F32, area)
            probT = sb("probT", [P, 2, TOK], F32, area)
            ks = sb("ks", [P, 3, TT, 64], F32, area)
            key_mean = sb("key_mean", [P, TT], F32, area)
            key_var = sb("key_var", [P, TT], F32, area)
            key_rstd = sb("key_rstd", [P, TT], F32, area)
            index_w = sb("index_w", [P, TT, 4], F32, area)
            top8 = sb("top8", [P, 8], F32, area)
            gate = sb("gate", [P, 4, TT * 8], F32, area)
            lowest = sb("lowest", [P, 4], F32, area)
            total = sb("total", [P, 4], F32, area)
            sunk = sb("sunk", [P, 4], F32, area)
            inverse = sb("inverse", [P, 4], F32, area)
            nsink = sb("nsink", [P, 8], F32, area)
        first.close()
        with ExitStack() as area:
            cst2 = sb("cst2", [P, dram["consts2"].shape[1]], F32, area)
            par2 = sb("par2", [P, dram["params2"].shape[1]], F32, area)
            twice_b = sb("twice_b", [P, KT], F32, area)
            half_g = sb("half_g", [P, KT], F32, area)
            ab = sb("ab", [P, 5, TT, 32], F32, area)
            neg_rate = sb("neg_rate", [P, 16], F32, area)
            decay = sb("decay", [P, TT, 16], F32, area)
            beta = sb("beta", [P, TT, 16], F32, area)
            neg_beta = sb("neg_beta", [P, TT, 16], F32, area)
            neg_sum = sb("neg_sum", [P, TT, 16], F32, area)
            exp_sum = sb("exp_sum", [P, P], F32, area)
            conv = sb("conv", [P, 2, 2, TOK], F32, area)
            tanh = sb("tanh", [P, 2, 512], F32, area)
            qk_tok = sb("qk_tok", [P, 2, 2, TT, P], F32, area)
            v_tok = sb("v_tok", [P, 4, TT, P], F32, area)
            qk_sq = sb("qk_sq", [P, 4], F32, area)
            qk_rstd = sb("qk_rstd", [P, 4], F32, area)
            qk_feat = sb("qk_feat", [P, 2, TOK], F32, area)
            ratio = sb("ratio", [P, 4, P], F32, area)
            upper = sb("upper", [P, 4, P], F32, area)
            qk_ratio = sb("qk_ratio", [P, 2, 4, P], F32, area)
            joint = sb("joint", [P, 2, 4, P], F32R, area)
            inv_t = sb("inv_t", [P, 4, P], F32R, area)
            inv = sb("inv", [P, 4, P], F32R, area)
            identr = sb("identr", [P, P], F32R, area)
            prod = sb("prod", [P, 4, P], F32R, area)
            from_one = sb("from_one", [P, 4, P], F32, area)
            solved = sb("solved", [P, 4, P], F32, area)
            k_decayed = sb("k_decayed", [P, 4, P], F32, area)
            k_rest = sb("k_rest", [P, 2, 4, P], F32, area)
            q_feat = sb("q_feat", [P, 2, 4, P], F32, area)
            values = sb("values", [P, 4, P], F32, area)
            w_feat = sb("w_feat", [P, 4, P], F32, area)
            state = sb("state", [P, 2, P], F32, area)
            o_tok = sb("o_tok", [P, TT, P], F32, area)
            o_sq = sb("o_sq", [P, 2 * TT], F32, area)
            o_rstd = sb("o_rstd", [P, TT], F32, area)
            glu_in = sb("glu_in", [P, 3, TOK + 30], F32, area)
            cacc = sb("cacc", [P, KT, TOK], F32, area)
            gts = sb("gts", [P, 2, KT, TOK], F32, area)
        q_decayed = from_one
        with ExitStack() as area:
            hhi2 = sb("hhi2", [P, FT, TOK], F32R, area)
            hlo2 = sb("hlo2", [P, FT, TOK], F32R, area)
            sg2 = sb("sg2", [P, 2, TOK], F32, area)
            hf2 = sb("hf2", [P, 2, TOK], F32, area)
            p_tok = sb("p_tok", [P, TT, TOK], F32, area)
            phi = sb("phi", [P, 2, TOK], F32R, area)
            plo = sb("plo", [P, 2, TOK], F32R, area)
            pl = sb("pl", [P, TT, D], F32, area)
            pl_junk = sb("pl_junk", [P, TT, D], F32, area)
            pl_gain = sb("pl_gain", [P, D], F32, area)
            pl_sq = sb("pl_sq", [P, TT], F32, area)
            pl_rstd = sb("pl_rstd", [P, TT], F32, area)
            gate_tanh = sb("gate_tanh", [P, 2, 512], F32, area)

        ps = ctx.enter_context(nc.psum_tensor("ps", [P, 8, 512], F32))
        block = ctx.enter_context(nc.Block())

        def C(name):
            if name in const1_at:
                a, n = const1_at[name]
                return cst1[:, a:a + n]
            a, n = const2_at[name]
            return cst2[:, a:a + n]

        def pair_of(name, r):
            return C(name)[:, r * P:(r + 1) * P]

        def systems(name):
            return C(name).rearrange("p (r c) -> p r c", r=2).unsqueeze(2).broadcast_to([P, 2, TT, P])

        def four(ap):
            return ap.rearrange("p (r t) c -> p r t c", r=2)

        def par_at(name, i, n=1):
            if name in param1_at:
                return par1[:, param1_at[name][0] + i:param1_at[name][0] + i + n]
            return par2[:, param2_at[name][0] + i:param2_at[name][0] + i + n]

        def slot_at(r, i):
            return ROUNDS[r][i // 2][0] if i // 2 < len(ROUNDS[r]) else None

        def chunk_of(step, r):
            c = step if r == 0 else 3 - step
            return c // 2, (c % 2) * CHUNK

        row_at, r = {}, 0
        for n, _, w in ROWS:
            row_at[n] = rows[:, r:r + w]
            r += w
        def used(ring, n):
            entry = plan[n]
            at = ring[:, n % ring.shape[1], :]
            if entry[0] == "columns":
                return at.rearrange("p (k c) -> p k c", k=4)[:, :, 0:sum(c for _, c in entry[3])]
            if entry[0] == "narrow":
                return at.rearrange("p (k c) -> p k c", k=KT)[:, :, 0:entry[4]]
            return at

        def logit_bias(kind, h, t):
            w = P * (t + 1)
            if kind in "BC":
                return bias[:, h, P * t:P * t + w]
            if kind == "A":
                return picked[:, t, 0:w]
            return C("window")[:, P * t:P * t + w]

        def base(h):
            return (h % 2) * HD

        def qk_of(kind, h, t):
            w = P * (t + 1)
            rows_ = slice(base(h), base(h) + HD)
            q = {"A": 0, "B": 2, "D": 0, "C": 1}[kind]
            query = fm[rows_, q, h // 2, t * P:(t + 1) * P]
            if kind == "D":
                return query, fmi[rows_, h // 4, 0:w]
            return query, fm[rows_, {"A": 1, "B": 3, "C": 2}[kind], h // 2, 0:w]

        def v_of(kind, h, s):
            if kind == "D":
                return v1[:, s, (h // 4) * HD:(h // 4 + 1) * HD]
            return (v1 if kind == "B" else v0)[:, s, h * HD:(h + 1) * HD]

        def slot_read(key):
            if key == "ab":
                return S["ab_abs"].at()
            if key[0] in ("qk", "v"):
                return S["taps5"].at((key, 1))
            if key[0] == "gates":
                return S["slot_read_act"].at(key)
            if key[0] in ("glu", "z"):
                return S["tanh_used"].at(key)
            return S["conv_out_read"].at(key)

        def tanh_free(name):
            return S["conv_gated"].at(name[1]) if name[0] == "conv" else S["tanh_used"].at(name)

        def channel_tile(key, m):
            return m * HEADS + key[1] if key[0] == "qk" else 2 * HEADS + 2 * key[1] + m

        o_junk = ab[:, 3:5, :, :].rearrange("p a t c -> p (a t c)")
        k_before = {1: 0, 3: 1, 4: 3}

        @block.sync
        def _(sp):
            for n in range(len(plan)):
                if n >= RAW:
                    sp.wait_ge(*S["weights_low"].at(n - RAW))
                sp.dma_start(raw[:, n % RAW, :], dram["stream"][n]).then_inc(weights_loaded[n % RAW], 16)
            sp.wait_ge(*S["normed"].at((NORMS - 1, TT - 1)))
            sp.dma_start(dram["out"].rearrange("(t p) d -> p t d", p=P), xn[:, :, :]).then_inc(stored, 16)
            sp.wait_ge(stored, 16)

        @block.gpsimd
        def _(pool):
            steps = [0]

            def link(ins):
                steps[0] += 1
                ins.then_inc(pool_step, 1)
                pool.wait_ge(pool_step, steps[0])

            def load_gain(k):
                if k >= 1:
                    pool.wait_ge(*S["normed"].at((k - 1, TT - 1)))
                pool.dma_start(gain[:, :], dram["gains"][k:k + 1, :].broadcast_to([P, D]))\
                    .then_inc(gain_loaded, 16)

            def rstd_of(out, mean, scale, eps):
                link(pool.tensor_scalar(mean, mean, scale, eps, ALU.mult, ALU.add))
                return pool.tensor_tensor(out, mean, half_power[:, 0:out.shape[1]], ALU.pow)

            def norm(k):
                pool.wait_ge(*S["squared"].at((k, TT - 1)))
                if k:
                    pool.wait_ge(*S["normed"].at((k - 1, TT - 1)))
                rstd_of(rstd[:, :], sumsq[:, :], 1.0 / D, EPS).then_inc(*S["rstd_ready"].one(k))

            pool.dma_start(x[:, :, :], dram["x"].rearrange("(t p) d -> p t d", p=P)).then_inc(x_loaded, 16)
            pool.dma_start(ident, dram["ident"]).then_inc(ident_loaded, 16)
            pool.dma_start(cst1[:, :], dram["consts1"]).then_inc(consts_loaded, 16)
            load_gain(0)
            pool.dma_start(par1[:, :], dram["params1"]).then_inc(params_loaded, 16)
            pool.dma_start(rows[:, :], dram["rows"].broadcast_to([P, rows.shape[1]])).then_inc(rows_loaded, 16)
            pool.dma_start(bias[:, :, :], dram["rel"].rearrange("p (h c) -> p h c", h=8)).then_inc(bias_loaded, 16)
            link(pool.memset(half_power[:, :], -0.5))
            norm(0)
            pool.wait_ge(bias_loaded, 16)
            link(pool.tensor_scalar(bias[:, :, :], bias[:, :, :], 8.0, None, ALU.mult))
            pool.memset(bias[0:64, :, 64:128], MASKED).then_inc(*S["bias_ready"].one(0))
            pool.memset(bias[0:64, :, P + 192:P + 256], MASKED).then_inc(*S["bias_ready"].one(1))
            pool.wait_ge(*S["key_squares"].at(TT - 1))
            rstd_of(key_rstd[:, :], key_var[:, :], 1.0 / HD, EPS).then_inc(*S["key_rstd_ready"].one())
            for k in range(1, 6):
                load_gain(k)
                if k == 4:
                    pool.wait_ge(*S["x_added"].at((4, TT - 1, 1)))
                    pool.dma_start(cst2[:, :], dram["consts2"]).then_inc(consts2_loaded, 16)
                    pool.dma_start(par2[:, :], dram["params2"]).then_inc(params2_loaded, 16)
                norm(k)

            pool.memset(glu_in[:, :, :], 0.0).then_inc(*S["glu_cleared"].one())
            pool.wait_ge(consts2_loaded, 16)

            def prepare(h, i):
                if h >= HEADS:
                    return
                if i == 4:
                    pool.wait_ge(*S["qk_squared"].at((h, 3)))
                    link(pool.tensor_scalar(qk_sq[:, :], qk_sq[:, :], 0.25, EPS, ALU.mult, ALU.add))
                    pool.tensor_tensor(qk_rstd[:, :], qk_sq[:, :], half_power[:, 0:4], ALU.pow)\
                        .then_inc(*S["qk_rstd_ready"].one(h))
                if i == 7:
                    pool.wait_ge(*S["upper_made"].at(h))
                    link(pool.tensor_tensor(four(upper[:, :, :]), four(upper[:, :, :]), systems("strict"), ALU.mult))
                    link(pool.tensor_tensor(four(joint[:, 0, :, :]), four(upper[:, :, :]), systems("join1"), ALU.mult))
                    if h:
                        pool.wait_ge(*S["solution"].at(h - 1))
                    pool.tensor_tensor(inv_t[:, :, :], ident.unsqueeze(1).broadcast_to([P, 4, P]),
                                       joint[:, 0, :, :].bitcast(F32), ALU.subtract).then_inc(*S["inverse_begun"].one(h))

            def level(h, i):
                if not 0 <= h < HEADS:
                    return
                if i < 5:
                    if i == 0:
                        pool.wait_ge(*S["inverse_begun"].at(h))
                    if i >= 2:
                        pool.wait_ge(*S["prod_made"].at((h, i - 1)))
                    pool.tensor_tensor(four(joint[:, (i + 1) % 2, :, :]), four(upper[:, :, :]),
                                       systems(f"join{LEVELS[i]}"), ALU.mult).then_inc(*S["joint_made"].one((h, i + 1)))
                if i == 5:
                    pool.wait_ge(*S["inverse_done"].at((h, 5)))
                    pool.wait_ge(*S["q_feat_made"].at(h))
                    pool.tensor_tensor(from_one[:, :, :], ident.unsqueeze(1).broadcast_to([P, 4, P]),
                                       inv[:, :, :].bitcast(F32), ALU.subtract).then_inc(*S["from_one_made"].one(h))

            def finish(h, i):
                if not 0 <= h < HEADS:
                    return
                if i == 4:
                    pool.wait_ge(*S["o_squared"].at((h, TT - 1)))
                    link(pool.tensor_scalar(o_sq[:, 0:TT], o_sq[:, 0:TT], 1.0 / P, EPS, ALU.mult, ALU.add))
                    pool.tensor_tensor(o_rstd[:, :], o_sq[:, 0:TT], half_power[:, 0:TT], ALU.pow)\
                        .then_inc(*S["o_rstd_ready"].one(h))

            for r in range(len(ROUNDS)):
                for i in range(TICKS):
                    level(r - 1, i)
                    prepare(r, i)
                    finish(r - 2, i)
                    if r == 8 and i == 2:
                        pool.wait_ge(*S["conv_var"].at())
                        v = glu_in[:, 0, 0:TOK]
                        pool.tensor_tensor(v, v, half_power[:, 0:1].broadcast_to([P, TOK]), ALU.pow)\
                            .then_inc(*S["conv_rstd"].one())

            load_gain(6)
            pool.wait_ge(*S["x_added"].at((6, TT - 1, 1)))
            pool.dma_start(p_tok[:, :, :], dram["p"].rearrange("(t p) d -> p t d", p=P)).then_inc(p_loaded, 16)
            pool.dma_start(pl_gain[:, :], dram["gains"][NORMS:NORMS + 1, :].broadcast_to([P, D])).then_inc(p_loaded, 16)
            norm(6)
            load_gain(7)
            pool.wait_ge(*S["pl_squared"].at(TT - 1))
            rstd_of(pl_rstd[:, :], pl_sq[:, :], 1.0 / D, EPS).then_inc(*S["pl_rstd_ready"].one())
            norm(7)
            load_gain(8)
            norm(8)

        @block.tensor
        def _(pe):
            def three(out, a_hi, a_lo, b_hi, b_lo, start, stop):
                nc.tensor.matmul(out, a_hi, b_hi, start=start, stop=False)
                nc.tensor.matmul(out, a_hi, b_lo, start=False, stop=False)
                return nc.tensor.matmul(out, a_lo, b_hi, start=False, stop=stop)

            def norm(k):
                for t in range(TT):
                    pe.wait_ge(*S["normed"].at((k, t)))
                    for half in range(2):
                        for i in range(4):
                            last = nc.tensor.transpose(ps[:, 4 + 2 * t + half, i * P:(i + 1) * P],
                                                       xn[:, t, (4 * half + i) * P:(4 * half + i + 1) * P], ident)
                        last.then_inc(*S["norm_turned"].one((k, t, half)))

            def norm_split_done(k):
                for t in range(TT):
                    for half in range(2):
                        pe.wait_ge(*S["norm_low"].at((k, t, half)))

            def columns(layer, blocks, b):
                key, width = blocks[b]
                for half in range(2):
                    n = slot_of[((layer, key), half)]
                    pe.wait_ge(*S["weights_low"].at(n))
                    wh, wl = used(whi, n), used(wlo, n)
                    for k in range(4):
                        for t in range(TT):
                            kt = 4 * half + k
                            last = three(ps[:, 2 * (b % 2) + t, 0:width], xhi[:, kt, t * P:(t + 1) * P],
                                         xlo[:, kt, t * P:(t + 1) * P], wh[:, k, :], wl[:, k, :],
                                         kt == 0, kt == KT - 1)
                    last.then_inc(*S["weights_used"].one(n))

            def block_read(layer, blocks, b):
                rotated = blocks[b][0] in ROTATED
                for t in range(TT):
                    pe.wait_ge(*(S["rope_read"] if rotated else S["copied"]).at((layer, b, t)))

            def turn_block(layer, blocks, b, before):
                key = blocks[b][0]
                for t in range(TT):
                    pe.wait_ge(*(S["rotated"] if key in ROTATED else S["copied"]).at((layer, b, t)))
                    if before is not None:
                        pe.wait_ge(*S["turned_copied"].at((layer, before, t)))
                    for i in range(TURNED[key]):
                        last = nc.tensor.transpose(ps[:, 4 + t, i * P:(i + 1) * P],
                                                   temp[:, b % 2, t, i * P:(i + 1) * P], ident)
                    last.then_inc(*S["block_turned"].one((layer, b, t)))

            def index_scores():
                pe.wait_ge(*S["turned_copied"].at(("even", 0, 0)))
                pe.wait_ge(*S["turned_copied"].at(("even", 0, 1)))
                for u in range(8):
                    h, t = u // 2, u % 2
                    if u >= 2:
                        pe.wait_ge(*S["index_relu"].at(u - 2))
                    r = slice(base(h), base(h) + HD)
                    nc.tensor.matmul(ps[:, 6 + u % 2, 0:P * (t + 1)], fmi[r, h // 2, t * P:(t + 1) * P],
                                     fmi[r, 2, 0:P * (t + 1)], start=True, stop=True)\
                        .then_inc(*S["index_product"].one(u))

            def forget_sums():
                pe.wait_ge(*S["gate_ready"].at())
                for h in range(8):
                    if h >= 2:
                        pe.wait_ge(*S["forget_bias"].at(h - 2))
                    for s in range(TT):
                        last = nc.tensor.matmul(ps[:, 6 + h % 2, 0:TOK],
                                                gate[:, 3, s * 8 + h:s * 8 + h + 1].broadcast_to([P, P]),
                                                C("upto")[:, s * TOK:(s + 1) * TOK], start=(s == 0), stop=(s == 1))
                    last.then_inc(*S["forget_sum"].one(h))

            def attend(layer, blocks):
                units = UNITS[layer]
                n = len(units)
                for b, (key, _) in enumerate(blocks):
                    for t in range(TT):
                        if key in TURNED:
                            pe.wait_ge(*S["turned_copied"].at((layer, b, t)))
                        else:
                            pe.wait_ge(*S["copied"].at((layer, b, t)))
                block_read(layer, blocks, len(blocks) - 2)
                block_read(layer, blocks, len(blocks) - 1)
                for u in range(n + 3):
                    if u < n:
                        kind, h, t = units[u]
                        if u >= 2:
                            pe.wait_ge(*S["logits"].at((layer, u - 2)))
                        q, k = qk_of(kind, h, t)
                        nc.tensor.matmul(ps[:, u % 2, 0:P * (t + 1)], q, k, start=True, stop=True)\
                            .then_inc(*S["products"].one((layer, u)))
                    if 2 <= u < n + 2:
                        v = u - 2
                        kind, h, t = units[v]
                        pe.wait_ge(*S["probs"].at((layer, v)))
                        if v >= 2:
                            pe.wait_ge(*S["probs_copied"].at((layer, v - 2)))
                        for s in range(t + 1):
                            last = nc.tensor.transpose(ps[:, 2 + v % 2, s * P:(s + 1) * P],
                                                       prob[:, v % 3, s * P:(s + 1) * P], ident)
                        last.then_inc(*S["probs_turned"].one((layer, v)))
                    if u >= 3:
                        v = u - 3
                        kind, h, t = units[v]
                        pair = v // 4
                        pe.wait_ge(*S["probs_copied"].at((layer, v)))
                        if v % 4 == 0 and pair >= 2:
                            pe.wait_ge(*S["mixed_low"].at((layer, pair - 2)))
                        for s in range(t + 1):
                            last = nc.tensor.matmul(ps[base(h):base(h) + HD, 4 + pair % 2, t * P:(t + 1) * P],
                                                    v_of(kind, h, s), probT[:, v % 2, s * P:(s + 1) * P],
                                                    start=(s == 0), stop=(s == t))
                        last.then_inc(*S["values_done"].one((layer, v)))

            def down(key, tiles, a_hi, a_lo, ready):
                for i in range(tiles // 2):
                    n = slot_of[(key, i)]
                    pe.wait_ge(*S["weights_low"].at(n))
                    wh = used(whi, n).rearrange("p (k c) -> p k c", k=2)
                    wl = used(wlo, n).rearrange("p (k c) -> p k c", k=2)
                    for k in range(2):
                        kt = 2 * i + k
                        ready(kt)
                        for t in range(TT):
                            for half in range(2):
                                c = slice(half * 512, (half + 1) * 512)
                                last = three(ps[:, 4 + 2 * t + half, :], a_hi[:, kt, t * P:(t + 1) * P],
                                             a_lo[:, kt, t * P:(t + 1) * P], wh[:, k, c], wl[:, k, c],
                                             kt == 0, kt == tiles - 1)
                    last.then_inc(*S["weights_used"].one(n))

            def half_slot(key, m):
                n, o = slot_of[key], ORDINAL[key]
                if m == 0:
                    pe.wait_ge(*S["weights_low"].at(n))
                    if o >= 2:
                        pe.wait_ge(*slot_read(MIX_SLOTS[o - 2][0]))
                if key == "ab":
                    wh, wl = used(whi, n), used(wlo, n)
                elif key[0] == "z":
                    wh = used(whi, n).rearrange("p (k c) -> p k c", k=KT)
                    wl = used(wlo, n).rearrange("p (k c) -> p k c", k=KT)
                else:
                    wh = used(whi, n).rearrange("p (k m c) -> p k m c", k=KT, m=2)[:, :, m, :]
                    wl = used(wlo, n).rearrange("p (k m c) -> p k m c", k=KT, m=2)[:, :, m, :]
                for kt in range(KT):
                    if key == "ab" or key[0] == "z":
                        width = wh.shape[2]
                        last = three(ps[:, o % 2, m * width:(m + 1) * width], xhi[:, kt, m * P:(m + 1) * P],
                                     xlo[:, kt, m * P:(m + 1) * P], wh[:, kt, :], wl[:, kt, :], kt == 0, kt == KT - 1)
                    else:
                        last = three(ps[:, o % 2, m * TOK:(m + 1) * TOK], wh[:, kt, :], wl[:, kt, :],
                                     xhi[:, kt, :], xlo[:, kt, :], kt == 0, kt == KT - 1)
                if m == 1:
                    last.then_inc(*S["weights_used"].one(n))

            def decay_sums():
                pe.wait_ge(consts2_loaded, 16)
                pe.wait_ge(*S["decay_ready"].at())
                for t in range(TT):
                    for r in range(2):
                        g = decay[:, t, r * 8:r * 8 + 8]
                        c = t * 16 + r * 8
                        nc.tensor.matmul(ps[:, 7, c:c + 8], pair_of("cum", r), g, start=True, stop=True)
                        nc.tensor.matmul(ps[:, 7, 32 + c:40 + c], pair_of("tail", r), g, start=True, stop=True)
                    for q in range(2):
                        c = 64 + (2 * t + q) * 16
                        last = nc.tensor.matmul(ps[:, 7, c:c + 16], C("half")[:, q:q + 1].broadcast_to([P, P]), decay[:, t, :], start=True, stop=True)
                last.then_inc(*S["decay_summed"].one())

            def prepare(h, i):
                if h >= HEADS:
                    return
                if i == 3:
                    c = ORDINAL_OF_CONV[("qk", h)]
                    pe.wait_ge(*S["conv_gated"].at(("qk", h)))
                    if h:
                        pe.wait_ge(*S["ratio_started"].at(h - 1))
                    for m in range(2):
                        for t in range(TT):
                            last = nc.tensor.transpose(ps[:, 2, (2 * m + t) * P:(2 * m + t + 1) * P],
                                                       conv[:, c % 2, m, t * P:(t + 1) * P], ident)
                    last.then_inc(*S["qk_turned"].one(h))
                if i == 5:
                    pe.wait_ge(*S["qk_scaled"].at((h, 3)))
                    if h:
                        pe.wait_ge(*S["q_feat_made"].at(h - 1))
                    for m in range(2):
                        for t in range(TT):
                            last = nc.tensor.transpose(ps[:, 3, (2 * m + t) * P:(2 * m + t + 1) * P],
                                                       qk_tok[:, h % 2, m, t, :], ident)
                    last.then_inc(*S["qk_back"].one(h))
                    if h % 2 == 0:
                        c = ORDINAL_OF_CONV[("v", h // 2)]
                        pe.wait_ge(*S["conv_gated"].at(("v", h // 2)))
                        for m in range(2):
                            for t in range(TT):
                                last = nc.tensor.transpose(ps[:, 2, (2 * m + t) * P:(2 * m + t + 1) * P],
                                                           conv[:, c % 2, m, t * P:(t + 1) * P], ident)
                        last.then_inc(*S["v_turned"].one(h // 2))
                if i == 6:
                    if h % 2 == 0:
                        pe.wait_ge(*S["v_made"].at(h // 2))
                    for r in range(2):
                        for t in range(TT):
                            col = decay[:, t, r * 8 + h:r * 8 + h + 1]
                            last = nc.tensor.matmul(ps[:, 2, (2 * r + t) * P:(2 * r + t + 1) * P], col.broadcast_to([P, P]),
                                                    pair_of("cum", r), start=True, stop=True)
                    last.then_inc(*S["sums_spread"].one(h))
                    pe.wait_ge(*S["qk_feat_made"].at(h))
                    for m in range(2):
                        for t in range(TT):
                            last = nc.tensor.matmul(ps[:, 3, (2 * m + t) * P:(2 * m + t + 1) * P],
                                                    qk_feat[:, 1, t * P:(t + 1) * P], qk_feat[:, 1 - m, t * P:(t + 1) * P],
                                                    start=True, stop=True)
                    last.then_inc(*S["qk_products"].one(h))

            def level_first(h, i):
                if not 0 <= h < HEADS:
                    return
                if i == 0:
                    pe.wait_ge(*S["inverse_begun"].at(h))
                    if h:
                        pe.wait_ge(*S["values_made"].at((h - 1, 3)))
                    for y in range(4):
                        last = nc.tensor.transpose(ps[:, 4, y * P:(y + 1) * P], inv_t[:, y, :].bitcast(F32), ident)
                    last.then_inc(*S["inverse_turned"].one(h))
                if 1 <= i <= 5:
                    pe.wait_ge(*S["joint_made"].at((h, i)))
                    pe.wait_ge(*(S["inverse_done"].at((h, i - 1)) if i > 1 else S["inverse_first"].at(h)))
                    for y in range(4):
                        last = nc.tensor.matmul(ps[:, 4, y * P:(y + 1) * P], joint[:, i % 2, y, :], inv[:, y, :],
                                                start=True, stop=True)
                    last.then_inc(*S["join_product"].one((h, i)))
                if i == 2:
                    pe.wait_ge(*S["q_decayed_made"].at((h, 3)))
                    pe.wait_ge(*S["upper_made"].at(h))
                    for y in range(4):
                        last = nc.tensor.transpose(ps[:, 3, y * P:(y + 1) * P], q_decayed[:, y, :], ident)
                    last.then_inc(*S["q_decayed_turned"].one(h))
                if i == 6:
                    pe.wait_ge(*S["inverse_done"].at((h, 5)))
                    for y in range(4):
                        last = nc.tensor.matmul(ps[:, 4, y * P:(y + 1) * P], upper[:, y, :], inv[:, y, :].bitcast(F32),
                                                start=True, stop=True)
                    last.then_inc(*S["check_product"].one(h))
                if i == 7:
                    pe.wait_ge(*S["solution_sum"].at(h))
                    pe.wait_ge(*S["k_decayed_made"].at((h, 3)))
                    for y in range(4):
                        nc.tensor.matmul(ps[:, 4, y * P:(y + 1) * P], solved[:, y, :], v_tok[:, h % 4, y % 2, :],
                                         start=True, stop=True)
                    for y in range(4):
                        last = nc.tensor.matmul(ps[:, 5, y * P:(y + 1) * P], k_decayed[:, y, :], solved[:, y, :],
                                                start=True, stop=True)
                    last.then_inc(*S["solution"].one(h))

            def level_second(h, i):
                if not 0 <= h < HEADS:
                    return
                if 1 <= i <= 5:
                    pe.wait_ge(*S["prod_made"].at((h, i)))
                    if i == 1 and h:
                        pe.wait_ge(*S["w_feat_made"].at(h - 1))
                    pe.wait_ge(*S["identr_made"].at())
                    for y in range(4):
                        nc.tensor.matmul(ps[:, 5, y * P:(y + 1) * P], identr[:, :], inv_t[:, y, :], start=True, stop=False)
                        nc.tensor.matmul(ps[:, 5, y * P:(y + 1) * P], prod[:, y, :], inv_t[:, y, :], start=False, stop=True)
                    for y in range(4):
                        last = nc.tensor.matmul(ps[:, 4, y * P:(y + 1) * P], inv_t[:, y, :], prod[:, y, :],
                                                start=True, stop=True)
                    last.then_inc(*S["joined"].one((h, i)))
                if i == 6:
                    pe.wait_ge(*S["residual"].at(h))
                    pe.wait_ge(*S["inverse_t"].at((h, 6)))
                    for y in range(4):
                        last = nc.tensor.matmul(ps[:, 5, y * P:(y + 1) * P], prod[:, y, :], inv_t[:, y, :],
                                                start=True, stop=True)
                    last.then_inc(*S["correction"].one(h))

            def chain_first(h, i):
                if not (0 <= h < HEADS and 1 <= i < 4):
                    return
                for r in range(2):
                    t, b = chunk_of(i, r)
                    pe.wait_ge(*S["state_made"].at((h, i - 1, r)))
                    pe.wait_ge(*S["o_added"].at((h, i - 1, r)))
                    nc.tensor.matmul(ps[b:b + CHUNK, 6 + r, 0:P], w_feat[:, 2 * r + t, b:b + CHUNK], state[:, r, :],
                                     start=True, stop=True).then_inc(*S["recalled"].one((h, i, r)))

            def chain_second(h, i):
                if not (0 <= h < HEADS and i < 4):
                    return
                for r in range(2):
                    t, b = chunk_of(i, r)
                    y = 2 * r + t
                    if i:
                        pe.wait_ge(*S["values_new"].at((h, i, r)))
                    else:
                        pe.wait_ge(*S["values_made"].at((h, 3)))
                        pe.wait_ge(*S["w_feat_made"].at(h))
                        if h:
                            pe.wait_ge(*S["o_added"].at((h - 1, 3, r)))
                        elif r == 1:
                            pe.wait_ge(*S["exp_sums"].at())
                    out = ps[b:b + CHUNK, 6 + r, P:2 * P]
                    if i:
                        nc.tensor.matmul(out, q_feat[:, h % 2, y, b:b + CHUNK], state[:, r, :], start=True, stop=False)
                    nc.tensor.matmul(out, qk_ratio[:, h % 2, y, b:b + CHUNK], values[:, y, :], start=(i == 0), stop=True)\
                        .then_inc(*S["o_product"].one((h, i, r)))
                    if i < 3:
                        nc.tensor.matmul(ps[:, 6 + r, 2 * P:3 * P], k_rest[b:b + CHUNK, h % 2, y, :],
                                         values[b:b + CHUNK, y, :], start=True, stop=True)\
                            .then_inc(*S["state_product"].one((h, i, r)))

            def conv_norm(i):
                if i == 0:
                    pe.wait_ge(*S["taps31"].at((KT - 1, 30)))
                    for j in range(KT):
                        last = nc.tensor.matmul(ps[:, 2, 0:TOK], C("mean").broadcast_to([P, P]), cacc[:, j, :], start=(j == 0), stop=(j == KT - 1))
                    last.then_inc(*S["conv_mean"].one())
                if i == 1:
                    for q in range(4):
                        pe.wait_ge(*S["conv_squared"].at(q))
                        for j in range(2):
                            last = nc.tensor.matmul(ps[:, 2, TOK:2 * TOK], C("mean").broadcast_to([P, P]), tanh[:, q % 2, j * TOK:(j + 1) * TOK],
                                                    start=(q == 0 and j == 0), stop=(q == 3 and j == 1))
                        last.then_inc(*S["conv_square_used"].one(q))

            def turn_o():
                for t in range(TT):
                    pe.wait_ge(*S["o_final"].at((HEADS - 1, t)))
                    for half in range(2):
                        for i in range(4):
                            last = nc.tensor.transpose(ps[:, 4 + 2 * t + half, i * P:(i + 1) * P],
                                                       xn[:, t, (4 * half + i) * P:(4 * half + i + 1) * P], ident)
                        last.then_inc(*S["norm_turned"].one(("o", t, half)))

            def up(layer, li):
                for j in range(FT):
                    n = slot_of[(f"up{li}", j)]
                    pe.wait_ge(*S["weights_low"].at(n))
                    if j >= 4:
                        pe.wait_ge(*(S["hidden"].at((li, j - 4)) if li == 2 else S["taps_done"].at((li, j - 4, 1))))
                    wh = used(whi, n).rearrange("p (k m c) -> p k m c", k=KT, m=2)
                    wl = used(wlo, n).rearrange("p (k m c) -> p k m c", k=KT, m=2)
                    for m in range(2):
                        for kt in range(KT):
                            last = three(ps[:, j % 4, m * TOK:(m + 1) * TOK], wh[:, kt, m, :], wl[:, kt, m, :],
                                         xhi[:, kt, :], xlo[:, kt, :], kt == 0, kt == KT - 1)
                    last.then_inc(*S["weights_used"].one(n))

            pe.wait_ge(ident_loaded, 16)
            pe.wait_ge(consts_loaded, 16)
            norm(0)
            for li, (layer, blocks) in enumerate(LAYERS):
                norm_split_done(2 * li)
                before = None
                for b in range(len(blocks)):
                    if b >= 2:
                        block_read(layer, blocks, b - 2)
                    columns(layer, blocks, b)
                    if b >= 1 and blocks[b - 1][0] in TURNED:
                        turn_block(layer, blocks, b - 1, before)
                        before = b - 1
                    if layer == "even" and b == 2:
                        index_scores()
                    if layer == "odd" and b == 2:
                        forget_sums()
                if blocks[-1][0] in TURNED:
                    turn_block(layer, blocks, len(blocks) - 1, before)
                attend(layer, blocks)
                for h in range(2):
                    if layer == "even":
                        pe.wait_ge(*S["index_relu"].at(6 + h))
                    else:
                        pe.wait_ge(*S["forget_bias"].at(6 + h))
                for pair in range(8):
                    pe.wait_ge(*S["mixed_low"].at((layer, pair)))
                down(f"{layer}_out", KT, xhi, xlo, lambda kt: None)
                norm(2 * li + 1)
                norm_split_done(2 * li + 1)
                up(layer, li)
                down(f"down{li}", FT, hhi, hlo, lambda kt: pe.wait_ge(*S["hidden_low"].at((li, kt))))
                if li == 0:
                    norm(2)

            norm(5)
            norm_split_done(5)
            for m in range(2):
                half_slot("ab", m)
            decay_sums()
            for r in range(len(ROUNDS)):
                for i in range(TICKS):
                    chain_first(r - 2, i)
                    level_first(r - 1, i)
                    if slot_at(r, i):
                        if r == 9 and i == 0:
                            for q in range(4):
                                pe.wait_ge(*S["conv_low"].at(q))
                        half_slot(slot_at(r, i), i % 2)
                    chain_second(r - 2, i)
                    level_second(r - 1, i)
                    prepare(r, i)
                    if r == 8:
                        conv_norm(i)
            turn_o()
            norm_split_done("o")
            for i in range(KT // 2):
                for m in range(2):
                    half_slot(("delta_out", i), m)
            for q in range(4):
                pe.wait_ge(*S["mix_low"].at(q))
            down("mix_out", KT, xhi, xlo, lambda kt: None)
            norm(6)
            norm_split_done(6)
            up("", 2)
            pe.wait_ge(p_loaded, 32)
            pe.wait_ge(*S["hidden"].at((2, FT - 1)))
            for kt in range(2):
                for t in range(TT):
                    last = nc.tensor.transpose(ps[:, 0, kt * TOK + t * P:kt * TOK + (t + 1) * P],
                                               p_tok[:, t, kt * P:(kt + 1) * P], ident)
            last.then_inc(*S["p_turned"].one())
            down("down2", FT, hhi2, hlo2, lambda kt: pe.wait_ge(*S["hidden_low"].at((2, kt))))
            pe.wait_ge(*S["p_low"].at())
            n = slot_of[("pl_proj", 0)]
            pe.wait_ge(*S["weights_low"].at(n))
            wh = used(whi, n).rearrange("p (k c) -> p k c", k=2)
            wl = used(wlo, n).rearrange("p (k c) -> p k c", k=2)
            for t in range(TT):
                for half in range(2):
                    for kt in range(2):
                        c = slice(half * 512, (half + 1) * 512)
                        last = three(ps[:, 2 * t + half, :], phi[:, kt, t * P:(t + 1) * P], plo[:, kt, t * P:(t + 1) * P],
                                     wh[:, kt, c], wl[:, kt, c], kt == 0, kt == 1)
            last.then_inc(*S["weights_used"].one(n))
            norm(7)
            norm_split_done(7)
            for t in range(TT):
                pe.wait_ge(*S["pl_copied"].at(t))
            columns("gate", [(0, 512), (1, 512)], 0)
            columns("gate", [(0, 512), (1, 512)], 1)

        @block.scalar
        def _(act):
            split_to = [0]

            def split(last):
                while split_to[0] <= min(last, len(plan) - 1):
                    n = split_to[0]
                    act.wait_ge(weights_loaded[n % RAW], 16 * (n // RAW + 1))
                    if n >= RING:
                        act.wait_ge(*S["weights_used"].at(n - RING))
                    act.activation(used(whi, n), used(raw, n), ACT.Copy).then_inc(*S["weights_high"].one(n))
                    split_to[0] += 1

            def norm(k, turned=True):
                for t in range(TT):
                    if k == 0:
                        act.wait_ge(x_loaded, 16)
                    elif k == 5:
                        act.wait_ge(*S["normed"].at((4, t)))
                    else:
                        act.wait_ge(*S["x_added"].at((k, t, 1)))
                        if t == 0:
                            act.wait_ge(*S["rstd_ready"].at(k - 1))
                            for tt in range(TT):
                                act.wait_ge(*S["norm_turned"].at(("o" if k == 6 else k - 1, tt, 1)))
                    act.activation(xn[:, t, :], x[:, t, :], ACT.Square, accum_out=sumsq[:, t:t + 1])\
                        .then_inc(*S["squared"].one((k, t)))
                if turned:
                    round_turned(k)

            def round_turned(k):
                for t in range(TT):
                    for half in range(2):
                        act.wait_ge(*S["norm_turned"].at((k, t, half)))
                        act.activation(xhi[:, 4 * half:4 * half + 4, t * P:(t + 1) * P],
                                       ps[:, 4 + 2 * t + half, :].rearrange("p (i c) -> p i c", i=4), ACT.Copy)\
                            .then_inc(*S["norm_high"].one((k, t, half)))

            def copy_block(layer, blocks, b):
                key = blocks[b][0]
                n = slot_of[((layer, key), 1)]
                act.wait_ge(*S["weights_used"].at(n))
                for t in range(TT):
                    if key in TURNED:
                        dst = temp[:, b % 2, t, :]
                        if b >= 2 and blocks[b - 2][0] in TURNED:
                            act.wait_ge(*S["block_turned"].at((layer, b - 2, t)))
                    else:
                        dst = (v1 if key == "vb" else v0)[:, t, :]
                    act.activation(dst, ps[:, 2 * (b % 2) + t, :], ACT.Copy).then_inc(*S["copied"].one((layer, b, t)))

            def copy_turned(layer, blocks, b):
                key = blocks[b][0]
                tiles = TURNED[key]
                dst = fmi if key in ("idx", "kvf") else fm[:, FM_OF[key], :, :]
                for t in range(TT):
                    act.wait_ge(*S["block_turned"].at((layer, b, t)))
                    act.activation(dst[:, 0:tiles, t * P:(t + 1) * P],
                                   ps[:, 4 + t, 0:tiles * P].rearrange("p (i c) -> p i c", i=tiles), ACT.Copy)\
                        .then_inc(*S["turned_copied"].one((layer, b, t)))

            def index_relus():
                for u in range(8):
                    t = u % 2
                    act.wait_ge(*S["index_product"].at(u))
                    if u >= 2:
                        act.wait_ge(*S["index_sum"].at(u - 2))
                    act.activation(rel[:, u % 2, 0:P * (t + 1)], ps[:, 6 + u % 2, 0:P * (t + 1)], ACT.Relu)\
                        .then_inc(*S["index_relu"].one(u))

            def gate_logs():
                act.wait_ge(*S["gate_abs"].at())
                act.activation(gate[:, 2, :], gate[:, 1, :], ACT.Exp, scale=-1.0).then_inc(*S["gate_exp"].one())
                act.wait_ge(*S["gate_exp"].at())
                act.activation(gate[:, 3, :], gate[:, 2, :], ACT.Ln, bias=1.0).then_inc(*S["gate_ln"].one())

            def attend(layer):
                units = UNITS[layer]
                n = len(units)
                for u in range(n + 5):
                    if u < n:
                        kind, h, t = units[u]
                        act.wait_ge(*S["logits"].at((layer, u)))
                        act.activation(prob[:, u % 3, 0:P * (t + 1)], prob[:, u % 3, 0:P * (t + 1)], ACT.Exp,
                                       bias=lowest[:, u % 4:u % 4 + 1], scale=-1.0, accum_out=total[:, u % 4:u % 4 + 1])\
                            .then_inc(*S["exps"].one((layer, u)))
                        if kind == "D":
                            act.activation(sunk[:, u % 4:u % 4 + 1], nsink[:, h:h + 1], ACT.Exp,
                                           bias=lowest[:, u % 4:u % 4 + 1], scale=-1.0).then_inc(*S["sinks_done"].one(u))
                    if 2 <= u < n + 2:
                        v = u - 2
                        t = units[v][2]
                        act.wait_ge(*S["probs_turned"].at((layer, v)))
                        if v >= 2:
                            act.wait_ge(*S["values_done"].at((layer, v - 2)))
                        act.activation(probT[:, v % 2, 0:P * (t + 1)], ps[:, 2 + v % 2, 0:P * (t + 1)], ACT.Copy)\
                            .then_inc(*S["probs_copied"].one((layer, v)))
                    if u >= 4 and (u - 4) % 4 == 3:
                        pair = (u - 4) // 4
                        act.wait_ge(*S["values_done"].at((layer, u - 4)))
                        act.activation(xhi[:, SLOT_OF_PAIR[pair], :], ps[:, 4 + pair % 2, 0:TOK], ACT.Copy)\
                            .then_inc(*S["mixed_high"].one((layer, pair)))

            def up(li):
                for j in range(FT + 2):
                    if j < FT:
                        n = slot_of[(f"up{li}", j)]
                        split(n + AHEAD)
                        act.wait_ge(*S["weights_used"].at(n))
                        if j >= 2:
                            act.wait_ge(*S["hidden"].at((li, j - 2)))
                        for m in range(2):
                            c = m * FT + j
                            act.activation(cv[:, j % 2, m, :], ps[:, j % 4, m * TOK:(m + 1) * TOK], ACT.Identity,
                                           bias=par_at(f"conv_b{li}", c), scale=par_at(f"conv_w{li}", 2 * 2 * FT + c))\
                                .then_inc(*S["conv_started"].one((li, j, m)))
                    if 1 <= j < FT + 1:
                        i = j - 1
                        act.wait_ge(*S["taps_done"].at((li, i, 0)))
                        act.activation(sg[:, i % 2, :], cv[:, i % 2, 0, :], ACT.Silu).then_inc(*S["gated"].one((li, i)))
                    if j >= 2:
                        i = j - 2
                        act.wait_ge(*S["hidden"].at((li, i)))
                        act.activation(hhi[:, i, :], hf[:, i % 2, :], ACT.Copy).then_inc(*S["hidden_high"].one((li, i)))

            def up2():
                for j in range(FT + 1):
                    if j < FT:
                        n = slot_of[("up2", j)]
                        split(n + AHEAD)
                        act.wait_ge(*S["weights_used"].at(n))
                        if j >= 2:
                            act.wait_ge(*S["hidden"].at((2, j - 2)))
                        act.activation(sg2[:, j % 2, :], ps[:, j % 4, 0:TOK], ACT.Silu).then_inc(*S["gated"].one((2, j)))
                    if j >= 1:
                        i = j - 1
                        act.wait_ge(*S["hidden"].at((2, i)))
                        act.activation(hhi2[:, i, :], hf2[:, i % 2, :], ACT.Copy).then_inc(*S["hidden_high"].one((2, i)))

            def evacuate(key):
                o, n = ORDINAL[key], slot_of[key]
                act.wait_ge(*S["weights_used"].at(n))
                src = ps[:, o % 2, :]
                if key[0] in ("qk", "v"):
                    c = ORDINAL_OF_CONV[key]
                    for m in range(2):
                        if c >= 2:
                            old = CONVS[c - 2]
                            act.wait_ge(*(S["qk_turned"] if old[0] == "qk" else S["v_turned"]).at(old[1]))
                        act.activation(conv[:, c % 2, m, :], src[:, m * TOK:(m + 1) * TOK], ACT.Copy,
                                       scale=par_at("taps5", 2 * 3 * HEADS + channel_tile(key, m)))\
                            .then_inc(*S["conv_begun"].one((key, m)))
                elif key[0] in ("glu", "z"):
                    if TANH_BEFORE[key]:
                        act.wait_ge(*tanh_free(TANH_BEFORE[key]))
                    if key[0] == "glu":
                        act.activation(tanh[:, TANH_OF[key], 0:TOK], src[:, TOK:2 * TOK], ACT.Tanh, scale=0.5)\
                            .then_inc(*S["tanh_made"].one(key))
                    else:
                        act.activation(tanh[:, TANH_OF[key], :], src, ACT.Tanh, scale=0.5).then_inc(*S["tanh_made"].one(key))
                elif key[0] == "gates":
                    act.activation(gts[:, :, key[1], :], src.rearrange("p (m c) -> p m c", m=2), ACT.Tanh, scale=0.5)\
                        .then_inc(*S["slot_read_act"].one(key))

            def conv_tanh(key):
                c = ORDINAL_OF_CONV[key]
                act.wait_ge(*S["taps5"].at((key, 1)))
                name = ("conv", key)
                if TANH_BEFORE[name]:
                    act.wait_ge(*tanh_free(TANH_BEFORE[name]))
                act.activation(tanh[:, TANH_OF[name], :].rearrange("p (m c) -> p m c", m=2), conv[:, c % 2, :, :], ACT.Tanh,
                               scale=0.5).then_inc(*S["tanh_made"].one(name))

            def prepare(h, i):
                if h >= HEADS:
                    return
                if i == 3:
                    act.wait_ge(*S["qk_turned"].at(h))
                    if h:
                        act.wait_ge(*S["qk_scaled"].at((h - 1, 3)))
                    for y in range(4):
                        if y == 0 and h:
                            act.wait_ge(*S["upper_made"].at(h - 1))
                        act.activation(ratio[:, y, :], ps[:, 2, y * P:(y + 1) * P], ACT.Square,
                                       accum_out=qk_sq[:, y:y + 1]).then_inc(*S["qk_squared"].one((h, y)))
                if i == 5:
                    act.wait_ge(*S["qk_back"].at(h))
                    if h:
                        act.wait_ge(*S["qk_products"].at(h - 1))
                    act.activation(qk_feat[:, :, :], ps[:, 3, :].rearrange("p (m c) -> p m c", m=2), ACT.Copy)\
                        .then_inc(*S["qk_feat_made"].one(h))
                    if h % 2 == 0:
                        act.wait_ge(*S["v_turned"].at(h // 2))
                        if h >= 4:
                            act.wait_ge(*S["solution"].at(h - 3))
                        act.activation(v_tok[:, h % 4:h % 4 + 2, :, :],
                                       ps[:, 2, :].rearrange("p (m t c) -> p m t c", m=2, t=2), ACT.Copy, scale=0.5)\
                            .then_inc(*S["v_made"].one(h // 2))
                if i == 6:
                    act.wait_ge(*S["ratio_started"].at(h))
                    for y in range(4):
                        r, t = y // 2, y % 2
                        act.activation(ratio[:, y, :], ratio[:, y, :], ACT.Exp,
                                       bias=neg_sum[:, t, r * 8 + h:r * 8 + h + 1]).then_inc(*S["ratio_made"].one((h, y)))

            def level(h, i):
                if not 0 <= h < HEADS:
                    return
                if i == 0:
                    act.wait_ge(*S["inverse_turned"].at(h))
                    act.activation(inv[:, :, :], ps[:, 4, :].rearrange("p (y c) -> p y c", y=4), ACT.Copy)\
                        .then_inc(*S["inverse_first"].one(h))
                if 1 <= i <= 5:
                    act.wait_ge(*S["join_product"].at((h, i)))
                    if i == 1 and h:
                        act.wait_ge(*S["correction"].at(h - 1))
                    act.activation(prod[:, :, :], ps[:, 4, :].rearrange("p (y c) -> p y c", y=4), ACT.Copy, scale=-1.0)\
                        .then_inc(*S["prod_made"].one((h, i)))

            def level_late(h, i):
                if not 0 <= h < HEADS:
                    return
                if i in (0, 1, 3):
                    for y in range(4):
                        r, t = y // 2, y % 2
                        column = t * 16 + r * 8 + h
                        if i == 0:
                            if y == 0 and h:
                                act.wait_ge(*S["residual"].at(h - 1))
                            act.activation(q_decayed[:, y, :], qk_tok[:, h % 2, 0, t, :], ACT.Copy,
                                           scale=exp_sum[:, column:column + 1]).then_inc(*S["q_decayed_made"].one((h, y)))
                        if i == 1:
                            act.activation(k_decayed[:, y, :], qk_tok[:, h % 2, 1, t, :], ACT.Copy,
                                           scale=exp_sum[:, column:column + 1]).then_inc(*S["k_decayed_made"].one((h, y)))
                        if i == 3:
                            act.activation(k_rest[:, h % 2, y, :], qk_tok[:, h % 2, 1, t, :], ACT.Copy,
                                           scale=exp_sum[:, 32 + column:33 + column])\
                                .then_inc(*S["k_rest_made"].one((h, y)))
                if i == 2:
                    act.wait_ge(*S["q_decayed_turned"].at(h))
                    act.activation(q_feat[:, h % 2, :, :], ps[:, 3, :].rearrange("p (y c) -> p y c", y=4), ACT.Copy)\
                        .then_inc(*S["q_feat_made"].one(h))
                if 1 <= i <= 5:
                    act.wait_ge(*S["joined"].at((h, i)))
                    act.activation(inv_t[:, :, :], ps[:, 5, :].rearrange("p (y c) -> p y c", y=4), ACT.Copy)\
                        .then_inc(*S["inverse_t"].one((h, i + 1)))
                if i == 7:
                    act.wait_ge(*S["solution"].at(h))
                    if h:
                        act.wait_ge(*S["o_product"].at((h - 1, 3, 1)))
                    for y in range(4):
                        r, t = y // 2, y % 2
                        act.activation(values[:, y, :], ps[:, 4, y * P:(y + 1) * P], ACT.Copy,
                                       scale=beta[:, t, r * 8 + h:r * 8 + h + 1]).then_inc(*S["values_made"].one((h, y)))
                    act.activation(w_feat[:, :, :], ps[:, 5, :].rearrange("p (y c) -> p y c", y=4), ACT.Copy)\
                        .then_inc(*S["w_feat_made"].one(h))

            def finish(h, i):
                if not 0 <= h < HEADS:
                    return
                if i == 4:
                    act.wait_ge(*S["o_added"].at((h, 3, 1)))
                    for t in range(TT):
                        if h or t:
                            act.wait_ge(*S["o_squared"].at((h, t - 1) if t else (h - 1, TT - 1)))
                        act.activation(o_junk, o_tok[:, t, :], ACT.Square, accum_out=o_sq[:, t:t + 1])\
                            .then_inc(*S["o_squared"].one((h, t)))

            def conv_norm(i):
                if i == 1:
                    act.wait_ge(*S["conv_centered"].at())
                    for q in range(4):
                        act.wait_ge(*(S["conv_square_used"].at(q - 2) if q >= 2 else tanh_free(LAST_TANH[q])))
                        act.activation(tanh[:, q % 2, :].rearrange("p (m c) -> p m c", m=2), cacc[:, 2 * q:2 * q + 2, :],
                                       ACT.Square).then_inc(*S["conv_squared"].one(q))
                if i == 3:
                    for q in range(4):
                        act.wait_ge(*S["conv_scaled"].at(q))
                        if q >= 2:
                            act.wait_ge(*S["conv_silu"].at(q - 2))
                        else:
                            act.wait_ge(*S["conv_square_used"].at(q + 2))
                        for m in range(2):
                            j = 2 * q + m
                            act.activation(cacc[:, j, :], cacc[:, j, :], ACT.Identity, scale=half_g[:, j:j + 1],
                                           bias=par_at("conv_ln_b_2", j)).then_inc(*S["conv_affine"].one(j))
                        act.wait_ge(*S["conv_affine"].at(2 * q + 1))
                        act.activation(tanh[:, q % 2, :].rearrange("p (m c) -> p m c", m=2), cacc[:, 2 * q:2 * q + 2, :],
                                       ACT.Tanh, scale=0.5).then_inc(*S["conv_tanh"].one(q))
                        if q >= 1:
                            round_conv(q - 1)
                    round_conv(3)

            def round_conv(q):
                act.wait_ge(*S["conv_silu"].at(q))
                if q == 0:
                    act.wait_ge(*S["weights_used"].at(slot_of[("gates", KT - 1)]))
                act.activation(xhi[:, 2 * q:2 * q + 2, :], cacc[:, 2 * q:2 * q + 2, :], ACT.Copy).then_inc(*S["conv_high"].one(q))

            act.wait_ge(params_loaded, 16)
            norm(0)
            split(AHEAD)
            for li, (layer, blocks) in enumerate(LAYERS):
                for b in range(len(blocks)):
                    split(slot_of[((layer, blocks[b][0]), 1)] + AHEAD)
                    if layer == "odd" and b == 0:
                        gate_logs()
                    if blocks[b][0] not in ROTATED:
                        copy_block(layer, blocks, b)
                    if b >= 1 and blocks[b - 1][0] in TURNED:
                        copy_turned(layer, blocks, b - 1)
                    if layer == "even" and b == 2:
                        index_relus()
                if blocks[-1][0] in TURNED:
                    copy_turned(layer, blocks, len(blocks) - 1)
                attend(layer)
                for i in range(KT // 2):
                    split(slot_of[(f"{layer}_out", i)] + AHEAD)
                norm(2 * li + 1)
                up(li)
                for i in range(FT // 2):
                    split(slot_of[(f"down{li}", i)] + AHEAD)
                norm(2 * li + 2, turned=(li == 0))

            norm(5)
            split(slot_of["ab"] + AHEAD)
            act.wait_ge(*S["ab_abs"].at())
            act.activation(ab[:, 2, :, 0:16], ab[:, 1, :, 0:16], ACT.Exp, scale=-1.0).then_inc(*S["act_step"].one(0))
            act.activation(neg_rate[:, :], row_at["a_log_2"], ACT.Exp).then_inc(*S["act_step"].one(1))
            act.wait_ge(*S["act_step"].at(0))
            act.activation(ab[:, 3, :, 0:16], ab[:, 2, :, 0:16], ACT.Ln, bias=1.0).then_inc(*S["ab_ln"].one())
            act.activation(ab[:, 3, :, 16:32], ab[:, 0, :, 16:32], ACT.Tanh, scale=0.5).then_inc(*S["beta_tanh"].one())
            act.wait_ge(*S["decay_summed"].at())
            act.activation(exp_sum[:, :], ps[:, 7, 0:P], ACT.Exp).then_inc(*S["exp_sums"].one())
            act.wait_ge(*S["exp_sums"].at())
            act.wait_ge(*S["beta_ready"].at())
            for r in range(len(ROUNDS)):
                for i in range(TICKS):
                    level(r - 1, i)
                    if slot_at(r, i) and i % 2 == 0:
                        split(slot_of[slot_at(r, i)] + AHEAD)
                    level_late(r - 1, i)
                    if r < HEADS and i == 2:
                        conv_tanh(("qk", r))
                    if r < HEADS and r % 2 == 0 and i == 4:
                        conv_tanh(("v", r // 2))
                    prepare(r, i)
                    finish(r - 2, i)
                    if r == 8:
                        conv_norm(i)
                    if slot_at(r, i) and i % 2 == 1:
                        evacuate(slot_at(r, i))
            act.wait_ge(*S["weights_used"].at(slot_of[("conv_out", 3)]))
            round_turned("o")
            for i in range(KT // 2):
                split(slot_of[("delta_out", i)] + AHEAD)
            for q in range(4):
                act.wait_ge(*S["mix_made"].at(q))
                act.wait_ge(*S["weights_used"].at(slot_of[("delta_out", 3)]))
                act.activation(xhi[:, 2 * q:2 * q + 2, :], gts[:, 0, 2 * q:2 * q + 2, :], ACT.Copy).then_inc(*S["mix_high"].one(q))
            for i in range(KT // 2):
                split(slot_of[("mix_out", i)] + AHEAD)
            norm(6)
            up2()
            act.wait_ge(*S["p_turned"].at())
            act.activation(phi[:, :, :], ps[:, 0, :].rearrange("p (k c) -> p k c", k=2), ACT.Copy).then_inc(*S["p_high"].one())
            for i in range(FT // 2):
                split(slot_of[("down2", i)] + AHEAD)
            act.wait_ge(*S["weights_used"].at(slot_of[("pl_proj", 0)]))
            for t in range(TT):
                act.activation(pl[:, t, :], ps[:, 2 * t:2 * t + 2, :].rearrange("p a b -> p (a b)"), ACT.Copy)\
                    .then_inc(*S["pl_copied"].one(t))
            for t in range(TT):
                act.wait_ge(*S["pl_copied"].at(t))
                act.activation(pl_junk[:, t, :], pl[:, t, :], ACT.Square, accum_out=pl_sq[:, t:t + 1])\
                    .then_inc(*S["pl_squared"].one(t))
            norm(7)
            for b in range(2):
                split(slot_of[(("gate", b), 1)] + AHEAD)
                act.wait_ge(*S["weights_used"].at(slot_of[(("gate", b), 1)]))
                for t in range(TT):
                    if b:
                        act.wait_ge(*S["gate_tanh_used"].at((b - 1, t)))
                    act.activation(gate_tanh[:, t, :], ps[:, 2 * b + t, :], ACT.Tanh, scale=0.5)\
                        .then_inc(*S["gate_tanh_made"].one((b, t)))
            norm(8, turned=False)

        @block.vector
        def _(dve):
            steps, split_to = [0], [0]

            def link(ins):
                steps[0] += 1
                ins.then_inc(dve_step, 1)
                dve.wait_ge(dve_step, steps[0])

            def split(last):
                while split_to[0] <= min(last, len(plan) - 1):
                    n = split_to[0]
                    dve.wait_ge(*S["weights_high"].at(n))
                    dve.tensor_tensor(used(wlo, n), used(raw, n), used(whi, n).bitcast(F32), ALU.subtract)\
                        .then_inc(*S["weights_low"].one(n))
                    split_to[0] += 1

            def normalize(k):
                dve.wait_ge(*S["rstd_ready"].at(k))
                dve.wait_ge(gain_loaded, 16 * (k + 1))
                for t in range(TT):
                    dve.scalar_tensor_tensor((x if k == 4 else xn)[:, t, :], x[:, t, :], rstd[:, t:t + 1],
                                             gain[:, :], ALU.mult, ALU.mult).then_inc(*S["normed"].one((k, t)))

            def norm(k):
                normalize(k)
                lows(k)

            def lows(k):
                for t in range(TT):
                    for half in range(2):
                        dve.wait_ge(*S["norm_high"].at((k, t, half)))
                        at = (slice(None), slice(4 * half, 4 * half + 4), slice(t * P, (t + 1) * P))
                        dve.tensor_tensor(xlo[at], ps[:, 4 + 2 * t + half, :].rearrange("p (i c) -> p i c", i=4),
                                          xhi[at].bitcast(F32), ALU.subtract).then_inc(*S["norm_low"].one((k, t, half)))

            def add_quarter_to_x(k, n):
                dve.wait_ge(*S["weights_used"].at(n))
                for t in range(TT):
                    for half in range(2):
                        c = slice(half * 512, (half + 1) * 512)
                        dve.scalar_tensor_tensor(x[:, t, c], ps[:, 4 + 2 * t + half, :], 0.25, x[:, t, c], ALU.mult, ALU.add)\
                            .then_inc(*S["x_added"].one((k, t, half)))

            def add_to_x(k, n):
                dve.wait_ge(*S["weights_used"].at(n))
                for t in range(TT):
                    for half in range(2):
                        c = slice(half * 512, (half + 1) * 512)
                        dve.tensor_tensor(x[:, t, c], ps[:, 4 + 2 * t + half, :], x[:, t, c], ALU.add)\
                            .then_inc(*S["x_added"].one((k, t, half)))

            def rope(src, heads, t, dsts, read, done):
                cos = C("cos")[:, t * HD:(t + 1) * HD].unsqueeze(1)
                sin = C("sin")[:, t * HD:(t + 1) * HD].unsqueeze(1)
                a = rope_a[:, 0:heads * HD].rearrange("p (h d) -> p h d", h=heads)
                b = rope_b[:, 0:heads * HD].rearrange("p (h d) -> p h d", h=heads)
                dve.tensor_tensor(a, src, cos.broadcast_to([P, heads, HD]), ALU.mult)
                dve.tensor_tensor(b[:, :, 0:32], src[:, :, 32:64], sin[:, :, 0:32].broadcast_to([P, heads, 32]), ALU.mult)
                last = dve.tensor_tensor(b[:, :, 32:64], src[:, :, 0:32], sin[:, :, 32:64].broadcast_to([P, heads, 32]),
                                         ALU.mult)
                if read:
                    last.then_inc(*S["rope_read"].one(read))
                    dve.wait_ge(*S["rope_read"].at(read))
                else:
                    link(last)
                for i, dst in enumerate(dsts):
                    last = dve.tensor_tensor(dst, a, b, ALU.add)
                    if i < len(dsts) - 1 or not done:
                        link(last)
                    else:
                        last.then_inc(*S["rotated"].one(done))
                        dve.wait_ge(*S["rotated"].at(done))

            def heads_of(ap, n):
                return ap.rearrange("p (h d) -> p h d", h=n)

            def rope_block(layer, blocks, b):
                key = blocks[b][0]
                dve.wait_ge(*S["weights_used"].at(slot_of[((layer, key), 1)]))
                for t in range(TT):
                    src = ps[:, 2 * (b % 2) + t, :]
                    dst = temp[:, b % 2, t, :]
                    if b >= 2 and blocks[b - 2][0] in TURNED:
                        dve.wait_ge(*S["block_turned"].at((layer, b - 2, t)))
                    if key == "idx":
                        dve.tensor_copy(ks[:, 0, t, :], src[:, 256:320])
                        link(dve.tensor_copy(index_w[:, t, :], src[:, 320:324]))
                        rope(heads_of(src[:, 0:256], 4), 4, t, [heads_of(dst[:, 0:256], 4)], (layer, b, t), None)
                        link(dve.tensor_reduce(key_mean[:, t:t + 1], ks[:, 0, t, :], AX.X, ALU.add))
                        link(dve.tensor_scalar(key_mean[:, t:t + 1], key_mean[:, t:t + 1], 1.0 / HD, None, ALU.mult))
                        link(dve.tensor_scalar(ks[:, 1, t, :], ks[:, 0, t, :], key_mean[:, t:t + 1], None, ALU.subtract))
                        dve.tensor_tensor_reduce(ks[:, 2, t, :], ks[:, 1, t, :], ks[:, 1, t, :], 1.0, 0.0, ALU.mult,
                                                 ALU.add, key_var[:, t:t + 1]).then_inc(*S["key_squares"].one(t))
                    elif key == "kvf":
                        dve.tensor_copy(v1[:, t, 0:P], src[:, P:2 * P])
                        dve.tensor_tensor(gate[:, 0, t * 8:t * 8 + 8], src[:, 256:264], row_at["forget_b"], ALU.add)
                        four = dst[:, 0:256].rearrange("p (g c d) -> p g c d", g=2, c=2)
                        rope(heads_of(src[:, 0:P], 2), 2, t, [four[:, :, 0, :], four[:, :, 1, :]], (layer, b, t), (layer, b, t))
                    else:
                        rope(heads_of(src, 8), 8, t, [heads_of(dst, 8)], (layer, b, t), (layer, b, t))
                if key == "idx":
                    dve.wait_ge(*S["key_rstd_ready"].at())
                    for t in range(TT):
                        dst = temp[:, b % 2, t, :]
                        link(dve.scalar_tensor_tensor(ks[:, 0, t, :], ks[:, 1, t, :], key_rstd[:, t:t + 1],
                                                      row_at["idx_k_ln_g"], ALU.mult, ALU.mult))
                        link(dve.tensor_tensor(ks[:, 1, t, :], ks[:, 0, t, :], row_at["idx_k_ln_b"], ALU.add))
                        rope(heads_of(ks[:, 1, t, :], 1), 1, t, [heads_of(dst[:, 256:320], 1), heads_of(dst[:, 320:384], 1)],
                             None, (layer, b, t))
                if key == "kvf":
                    link(dve.tensor_scalar(gate[:, 1, :], gate[:, 0, :], -1.0, None, ALU.mult))
                    dve.tensor_tensor(gate[:, 1, :], gate[:, 0, :], gate[:, 1, :], ALU.max).then_inc(*S["gate_abs"].one())

            def gate_finish():
                dve.wait_ge(*S["gate_ln"].at())
                link(dve.scalar_tensor_tensor(gate[:, 2, :], gate[:, 0, :], 0.0, gate[:, 3, :], ALU.min, ALU.subtract))
                dve.tensor_scalar(gate[:, 3, :], gate[:, 2, :], -8.0, None, ALU.mult).then_inc(*S["gate_ready"].one())
                dve.tensor_scalar(nsink[:, :], row_at["sinks"], -1.0, None, ALU.mult).then_inc(*S["nsink_ready"].one())

            def forget_biases():
                for h in range(8):
                    dve.wait_ge(*S["forget_sum"].at(h))
                    dve.tensor_tensor(bias[:, h, 0:P], ps[:, 6 + h % 2, 0:P], C("causal")[:, 0:P], ALU.add)
                    dve.tensor_tensor(bias[:, h, P:3 * P], ps[:, 6 + h % 2, 0:TOK], C("causal")[:, P:3 * P], ALU.add)\
                        .then_inc(*S["forget_bias"].one(h))
                dve.wait_ge(*S["forget_bias"].at(7))

            def index_sums():
                for u in range(8):
                    h, t = u // 2, u % 2
                    w = P * (t + 1)
                    dve.wait_ge(*S["index_relu"].at(u))
                    if h == 0:
                        last = dve.tensor_scalar(score[:, t, 0:w], rel[:, u % 2, 0:w], index_w[:, t, h:h + 1], None, ALU.mult)
                    else:
                        dve.wait_ge(*S["index_sum"].at(u - 2))
                        last = dve.scalar_tensor_tensor(score[:, t, 0:w], rel[:, u % 2, 0:w], index_w[:, t, h:h + 1],
                                                        score[:, t, 0:w], ALU.mult, ALU.add)
                    last.then_inc(*S["index_sum"].one(u))
                dve.wait_ge(*S["index_sum"].at(7))
                dve.memset(score[0:64, 0, 64:128], -1e30)
                link(dve.memset(score[0:64, 1, 192:256], -1e30))

            def take_top(rounds):
                for t in range(TT):
                    w = P * (t + 1)
                    for _ in range(rounds):
                        link(dve.max(top8[:, :], score[:, t, 0:w]))
                        link(dve.match_replace(score[:, t, 0:w], top8[:, :], score[:, t, 0:w], TAKEN))

            def pick():
                for t in range(TT):
                    w = P * (t + 1)
                    link(dve.tensor_scalar(picked[:, t, 0:w], score[:, t, 0:w], -2e38, MASKED, ALU.is_gt, ALU.mult))

            def attend(layer):
                units = UNITS[layer]
                n = len(units)
                for u in range(n + 5):
                    if u < n:
                        kind, h, t = units[u]
                        w = P * (t + 1)
                        dve.wait_ge(*S["products"].at((layer, u)))
                        if u >= 3:
                            dve.wait_ge(*S["probs_turned"].at((layer, u - 3)))
                        if kind == "B" and u < 2:
                            dve.wait_ge(*S["bias_ready"].at(1))
                        first = nsink[:, h:h + 1] if kind == "D" else 3e38
                        dve.tensor_tensor_reduce(prob[:, u % 3, 0:w], ps[:, u % 2, 0:w], logit_bias(kind, h, t),
                                                 -0.125, first, ALU.add, ALU.min, lowest[:, u % 4:u % 4 + 1])\
                            .then_inc(*S["logits"].one((layer, u)))
                    if 1 <= u < n + 1:
                        v = u - 1
                        kind, h, t = units[v]
                        w = P * (t + 1)
                        sum_ = total[:, v % 4:v % 4 + 1]
                        dve.wait_ge(*S["exps"].at((layer, v)))
                        if kind == "D":
                            dve.wait_ge(*S["sinks_done"].at(v))
                            link(dve.tensor_tensor(sum_, sum_, sunk[:, v % 4:v % 4 + 1], ALU.add))
                        link(dve.reciprocal(inverse[:, v % 4:v % 4 + 1], sum_))
                        dve.tensor_scalar(prob[:, v % 3, 0:w], prob[:, v % 3, 0:w], inverse[:, v % 4:v % 4 + 1], None,
                                          ALU.mult).then_inc(*S["probs"].one((layer, v)))
                    if u >= 4 and (u - 4) % 4 == 3:
                        pair = (u - 4) // 4
                        kt = SLOT_OF_PAIR[pair]
                        dve.wait_ge(*S["mixed_high"].at((layer, pair)))
                        dve.tensor_tensor(xlo[:, kt, :], ps[:, 4 + pair % 2, 0:TOK], xhi[:, kt, :].bitcast(F32),
                                          ALU.subtract).then_inc(*S["mixed_low"].one((layer, pair)))

            def up(li):
                for j in range(FT + 2):
                    if j < FT:
                        split(slot_of[(f"up{li}", j)] + AHEAD)
                        for m in range(2):
                            dve.wait_ge(*S["conv_started"].at((li, j, 1)))
                            dve.scalar_tensor_tensor(cv[:, j % 2, m, 1:TOK], ps[:, j % 4, m * TOK:(m + 1) * TOK - 1],
                                                     par_at(f"conv_w{li}", 2 * FT + m * FT + j), cv[:, j % 2, m, 1:TOK],
                                                     ALU.mult, ALU.add).then_inc(*S["tap_one"].one((li, j, m)))
                        for m in range(2):
                            dve.wait_ge(*S["tap_one"].at((li, j, m)))
                            dve.scalar_tensor_tensor(cv[:, j % 2, m, 2:TOK], ps[:, j % 4, m * TOK:(m + 1) * TOK - 2],
                                                     par_at(f"conv_w{li}", m * FT + j), cv[:, j % 2, m, 2:TOK],
                                                     ALU.mult, ALU.add).then_inc(*S["taps_done"].one((li, j, m)))
                    if 1 <= j < FT + 1:
                        i = j - 1
                        dve.wait_ge(*S["gated"].at((li, i)))
                        dve.wait_ge(*S["taps_done"].at((li, i, 1)))
                        if i >= 2:
                            dve.wait_ge(*S["hidden_low"].at((li, i - 2)))
                        dve.tensor_tensor(hf[:, i % 2, :], sg[:, i % 2, :], cv[:, i % 2, 1, :], ALU.mult)\
                            .then_inc(*S["hidden"].one((li, i)))
                    if j >= 2:
                        i = j - 2
                        dve.wait_ge(*S["hidden_high"].at((li, i)))
                        dve.tensor_tensor(hlo[:, i, :], hf[:, i % 2, :], hhi[:, i, :].bitcast(F32), ALU.subtract)\
                            .then_inc(*S["hidden_low"].one((li, i)))

            dve.wait_ge(x_loaded, 16)
            def up2():
                for j in range(FT + 1):
                    if j < FT:
                        split(slot_of[("up2", j)] + AHEAD)
                        dve.wait_ge(*S["gated"].at((2, j)))
                        if j >= 2:
                            dve.wait_ge(*S["hidden_low"].at((2, j - 2)))
                        dve.tensor_tensor(hf2[:, j % 2, :], sg2[:, j % 2, :], ps[:, j % 4, TOK:2 * TOK], ALU.mult)\
                            .then_inc(*S["hidden"].one((2, j)))
                    if j >= 1:
                        i = j - 1
                        dve.wait_ge(*S["hidden_high"].at((2, i)))
                        dve.tensor_tensor(hlo2[:, i, :], hf2[:, i % 2, :], hhi2[:, i, :].bitcast(F32), ALU.subtract)\
                            .then_inc(*S["hidden_low"].one((2, i)))

            def decays():
                dve.wait_ge(*S["weights_used"].at(slot_of["ab"]))
                dve.wait_ge(params2_loaded, 16)
                link(dve.tensor_copy(ab[:, 0, :, :], ps[:, 0, 0:64].rearrange("p (t c) -> p t c", t=2)))
                dt = row_at["dt_bias_2"].unsqueeze(1).broadcast_to([P, TT, 16])
                link(dve.tensor_tensor(ab[:, 0, :, 0:16], ab[:, 0, :, 0:16], dt, ALU.add))
                link(dve.tensor_scalar(ab[:, 1, :, 0:16], ab[:, 0, :, 0:16], -1.0, None, ALU.mult))
                dve.tensor_tensor(ab[:, 1, :, 0:16], ab[:, 1, :, 0:16], ab[:, 0, :, 0:16], ALU.max).then_inc(*S["ab_abs"].one())
                dve.tensor_scalar(twice_b[:, :], par_at("conv_dw_b_2", 0, KT), 2.0, None, ALU.mult)
                dve.tensor_scalar(half_g[:, :], par_at("conv_ln_g_2", 0, KT), 0.5, None, ALU.mult)\
                    .then_inc(*S["half_g_made"].one())
                link(dve.tensor_copy(identr[:, :], ident))
                dve.tensor_copy(identr[:, :], ident).then_inc(*S["identr_made"].one())
                dve.wait_ge(*S["ab_ln"].at())
                link(dve.scalar_tensor_tensor(ab[:, 4, :, 0:16], ab[:, 0, :, 0:16], 0.0, ab[:, 3, :, 0:16], ALU.max, ALU.add))
                rate = neg_rate[:, :].unsqueeze(1).broadcast_to([P, TT, 16])
                dve.wait_ge(*S["act_step"].at(1))
                dve.scalar_tensor_tensor(decay[:, :, :], ab[:, 4, :, 0:16], -1.0, rate, ALU.mult, ALU.mult)\
                    .then_inc(*S["decay_ready"].one())
                dve.wait_ge(*S["beta_tanh"].at())
                link(dve.tensor_scalar(beta[:, :, :], ab[:, 3, :, 16:32], 0.5, 0.5, ALU.mult, ALU.add))
                dve.tensor_scalar(neg_beta[:, :, :], beta[:, :, :], -1.0, None, ALU.mult).then_inc(*S["beta_ready"].one())
                dve.wait_ge(*S["beta_ready"].at())
                dve.wait_ge(*S["exp_sums"].at())
                dve.tensor_scalar(neg_sum[:, :, :], ps[:, 7, 0:32].rearrange("p (t c) -> p t c", t=2), -1.0, None, ALU.mult)\
                    .then_inc(*S["neg_sum_made"].one())
                dve.wait_ge(*S["neg_sum_made"].at())

            def evacuate(key):
                o = ORDINAL[key]
                src = ps[:, o % 2, :]
                if key[0] in ("qk", "v"):
                    c = ORDINAL_OF_CONV[key]
                    for k in (0, 1, 3, 4):
                        d = k - 2
                        for m in range(2):
                            if k == 0:
                                dve.wait_ge(*S["conv_begun"].at((key, 1)))
                            else:
                                dve.wait_ge(*S["tap5"].at((key, k_before[k], m)))
                            to, of = (slice(-d, TOK), slice(0, TOK + d)) if d < 0 else (slice(0, TOK - d), slice(d, TOK))
                            ins = dve.scalar_tensor_tensor(conv[:, c % 2, m, to], src[:, m * TOK:(m + 1) * TOK][:, of],
                                                           par_at("taps5", k * 3 * HEADS + channel_tile(key, m)),
                                                           conv[:, c % 2, m, to], ALU.mult, ALU.add)
                            ins.then_inc(*(S["taps5"].one((key, m)) if k == 4 else S["tap5"].one((key, k, m))))
                elif key[0] == "glu":
                    dve.wait_ge(*S["tanh_made"].at(key))
                    j = key[1]
                    if j == 0:
                        dve.wait_ge(*S["glu_cleared"].at())
                    if j >= 3:
                        dve.wait_ge(*S["taps31"].at((j - 3, 30)))
                    dve.scalar_tensor_tensor(glu_in[:, j % 3, 15:15 + TOK], tanh[:, TANH_OF[key], 0:TOK], 1.0, src[:, 0:TOK],
                                             ALU.add, ALU.mult).then_inc(*S["tanh_used"].one(key))
                elif key[0] == "z":
                    dve.wait_ge(*S["tanh_made"].at(key))
                    c = slice(key[1] * TOK, (key[1] + 1) * TOK)
                    dve.scalar_tensor_tensor(xn[:, :, c], tanh[:, TANH_OF[key], :].rearrange("p (t c) -> p t c", t=2), 1.0,
                                             src.rearrange("p (t c) -> p t c", t=2), ALU.add, ALU.mult)\
                        .then_inc(*S["tanh_used"].one(key))
                    dve.wait_ge(*S["tanh_used"].at(key))
                    view = xn[:, :, c].rearrange("p t (h c) -> p t h c", h=2)
                    for t in range(TT):
                        last = dve.tensor_tensor(view[:, t, :, :], view[:, t, :, :],
                                                 row_at["delta_norm_g_2"].unsqueeze(1).broadcast_to([P, 2, P]), ALU.mult)
                    last.then_inc(*S["z_made"].one(key[1]))
                elif key[0] == "conv_out":
                    dve.wait_ge(*S["weights_used"].at(slot_of[key]))
                    if key[1] == 0:
                        dve.wait_ge(*S["slot_read_act"].at(("gates", KT - 1)))
                    g = gts[:, 0, 2 * key[1]:2 * key[1] + 2, :]
                    dve.scalar_tensor_tensor(g, g, 1.0, src.rearrange("p (m c) -> p m c", m=2), ALU.add, ALU.mult)\
                        .then_inc(*S["conv_out_read"].one(key))
                elif key[0] == "delta_out":
                    dve.wait_ge(*S["weights_used"].at(slot_of[key]))
                    q = key[1]
                    g = gts[:, 1, 2 * q:2 * q + 2, :]
                    dve.scalar_tensor_tensor(g, g, 1.0, src.rearrange("p (m c) -> p m c", m=2), ALU.add, ALU.mult)\
                        .then_inc(*S["conv_out_read"].one(key))
                    dve.wait_ge(*S["conv_out_read"].at(key))
                    f = gts[:, 0, 2 * q:2 * q + 2, :]
                    dve.tensor_tensor(f, f, g, ALU.add).then_inc(*S["mix_made"].one(q))

            def conv_gate(key):
                c = ORDINAL_OF_CONV[key]
                name = ("conv", key)
                dve.wait_ge(*S["tanh_made"].at(name))
                dve.scalar_tensor_tensor(conv[:, c % 2, :, :], tanh[:, TANH_OF[name], :].rearrange("p (m c) -> p m c", m=2), 1.0,
                                         conv[:, c % 2, :, :], ALU.add, ALU.mult).then_inc(*S["conv_gated"].one(key))

            def long_taps(tick):
                for j, k in TAPS.get(tick, []):
                    src = glu_in[:, j % 3, k:k + TOK]
                    w = par_at("taps31", k * KT + j)
                    if k == 0:
                        dve.wait_ge(*S["tanh_used"].at(("glu", j)))
                        dve.tensor_scalar(cacc[:, j, :], src, w, twice_b[:, j:j + 1], ALU.mult, ALU.add)\
                            .then_inc(*S["taps31"].one((j, k)))
                    else:
                        dve.wait_ge(*S["taps31"].at((j, k - 1)))
                        dve.scalar_tensor_tensor(cacc[:, j, :], src, w, cacc[:, j, :], ALU.mult, ALU.add)\
                            .then_inc(*S["taps31"].one((j, k)))

            def prepare(h, i):
                if h >= HEADS:
                    return
                if i == 4:
                    dve.wait_ge(*S["qk_rstd_ready"].at(h))
                    for y in range(4):
                        scale = 0.5 * (P ** -0.5 if y < 2 else 1.0)
                        dve.tensor_scalar(qk_tok[:, h % 2, y // 2, y % 2, :], ps[:, 2, y * P:(y + 1) * P],
                                          qk_rstd[:, y:y + 1], scale, ALU.mult, ALU.mult).then_inc(*S["qk_scaled"].one((h, y)))
                if i == 6:
                    dve.wait_ge(*S["sums_spread"].at(h))
                    dve.tensor_tensor(four(ratio[:, :, :]), ps[:, 2, :].rearrange("p (r t c) -> p r t c", r=2, t=2),
                                      systems("off"), ALU.add).then_inc(*S["ratio_started"].one(h))
                if i == 7:
                    dve.wait_ge(*S["ratio_made"].at((h, 3)))
                    dve.wait_ge(*S["qk_products"].at(h))
                    kk = ps[:, 3, 0:TOK].rearrange("p (t c) -> p t c", t=2)
                    kq = ps[:, 3, TOK:2 * TOK].rearrange("p (t c) -> p t c", t=2)
                    for r in range(2):
                        dve.tensor_tensor(qk_ratio[:, h % 2, 2 * r:2 * r + 2, :], kq, ratio[:, 2 * r:2 * r + 2, :], ALU.mult)
                    if h:
                        dve.wait_ge(*S["check_product"].at(h - 1))
                    for y in range(4):
                        r, t = y // 2, y % 2
                        last = dve.scalar_tensor_tensor(upper[:, y, :], kk[:, t, :], beta[:, t, r * 8 + h:r * 8 + h + 1],
                                                        ratio[:, y, :], ALU.mult, ALU.mult)
                    last.then_inc(*S["upper_made"].one(h))

            def level_first(h, i):
                if not 0 <= h < HEADS:
                    return
                if i == 6:
                    dve.wait_ge(*S["check_product"].at(h))
                    dve.wait_ge(*S["from_one_made"].at(h))
                    dve.scalar_tensor_tensor(prod[:, :, :], ps[:, 4, :].rearrange("p (y c) -> p y c", y=4), -1.0,
                                             from_one[:, :, :], ALU.mult, ALU.add).then_inc(*S["residual"].one(h))

            def level_second(h, i):
                if not 0 <= h < HEADS:
                    return
                if 1 <= i <= 5:
                    dve.wait_ge(*S["joined"].at((h, i)))
                    dve.tensor_tensor(inv[:, :, :], ps[:, 4, :].rearrange("p (y c) -> p y c", y=4),
                                      inv[:, :, :].bitcast(F32), ALU.add).then_inc(*S["inverse_done"].one((h, i)))
                if i == 6:
                    dve.wait_ge(*S["correction"].at(h))
                    dve.wait_ge(*S["inverse_t"].at((h, 6)))
                    dve.tensor_tensor(solved[:, :, :], ps[:, 5, :].rearrange("p (y c) -> p y c", y=4),
                                      inv_t[:, :, :].bitcast(F32), ALU.add).then_inc(*S["solution_sum"].one(h))

            def chain_first(h, i):
                if not (0 <= h < HEADS and 1 <= i < 4):
                    return
                for r in range(2):
                    t, b = chunk_of(i, r)
                    y = 2 * r + t
                    dve.wait_ge(*S["recalled"].at((h, i, r)))
                    dve.wait_ge(*S["values_made"].at((h, y)))
                    dve.scalar_tensor_tensor(values[b:b + CHUNK, y, :], ps[b:b + CHUNK, 6 + r, 0:P],
                                             neg_beta[b:b + CHUNK, t, r * 8 + h:r * 8 + h + 1], values[b:b + CHUNK, y, :],
                                             ALU.mult, ALU.add).then_inc(*S["values_new"].one((h, i, r)))

            def chain_second(h, i):
                if not (0 <= h < HEADS and i < 4):
                    return
                for r in range(2):
                    t, b = chunk_of(i, r)
                    if i < 3:
                        dve.wait_ge(*S["state_product"].at((h, i, r)))
                        new = ps[:, 6 + r, 2 * P:3 * P]
                        if i == 0:
                            last = dve.tensor_copy(state[:, r, :], new)
                        else:
                            column = 64 + (2 * t + b // CHUNK) * 16 + r * 8 + h
                            dve.wait_ge(*S["state_made"].at((h, i - 1, r)))
                            last = dve.scalar_tensor_tensor(state[:, r, :], state[:, r, :], exp_sum[:, column:column + 1],
                                                            new, ALU.mult, ALU.add)
                        last.then_inc(*S["state_made"].one((h, i, r)))
                    else:
                        dve.wait_ge(*S["o_product"].at((h, i, r)))
                    out = o_tok[b:b + CHUNK, t, :]
                    got = ps[b:b + CHUNK, 6 + r, P:2 * P]
                    if i < 2:
                        last = dve.tensor_copy(out, got)
                    else:
                        dve.wait_ge(*S["o_added"].at((h, 3 - i, 1 - r)))
                        last = dve.tensor_tensor(out, got, out, ALU.add)
                    last.then_inc(*S["o_added"].one((h, i, r)))

            def finish(h, i):
                if not 0 <= h < HEADS:
                    return
                if i == 5:
                    dve.wait_ge(*S["o_rstd_ready"].at(h))
                    dve.wait_ge(*S["z_made"].at(h // 2))
                    for t in range(TT):
                        at = xn[:, t, h * P:(h + 1) * P]
                        dve.scalar_tensor_tensor(at, o_tok[:, t, :], o_rstd[:, t:t + 1], at, ALU.mult, ALU.mult)\
                            .then_inc(*S["o_final"].one((h, t)))

            def conv_norm(i):
                if i == 0:
                    dve.wait_ge(*S["conv_mean"].at())
                    mean = ps[:, 2, 0:TOK].unsqueeze(1).broadcast_to([P, KT, TOK])
                    dve.tensor_tensor(cacc[:, :, :], cacc[:, :, :], mean, ALU.subtract).then_inc(*S["conv_centered"].one())
                if i == 2:
                    dve.wait_ge(*S["conv_square_used"].at(3))
                    dve.tensor_scalar(glu_in[:, 0, 0:TOK], ps[:, 2, TOK:2 * TOK], 0.25, 1e-5, ALU.mult, ALU.add)\
                        .then_inc(*S["conv_var"].one())
                if i == 3:
                    dve.wait_ge(*S["conv_rstd"].at())
                    for q in range(4):
                        at = cacc[:, 2 * q:2 * q + 2, :]
                        dve.tensor_tensor(at, at, glu_in[:, 0, 0:TOK].unsqueeze(1).broadcast_to([P, 2, TOK]), ALU.mult)\
                            .then_inc(*S["conv_scaled"].one(q))
                    for q in range(4):
                        at = cacc[:, 2 * q:2 * q + 2, :]
                        dve.wait_ge(*S["conv_tanh"].at(q))
                        dve.scalar_tensor_tensor(at, tanh[:, q % 2, :].rearrange("p (m c) -> p m c", m=2), 1.0, at,
                                                 ALU.add, ALU.mult).then_inc(*S["conv_silu"].one(q))
                        if q:
                            low_conv(q - 1)
                    low_conv(3)

            def low_conv(q):
                dve.wait_ge(*S["conv_high"].at(q))
                at = (slice(None), slice(2 * q, 2 * q + 2), slice(None))
                dve.tensor_tensor(xlo[at], cacc[at], xhi[at].bitcast(F32), ALU.subtract).then_inc(*S["conv_low"].one(q))

            dve.wait_ge(consts_loaded, 16)
            dve.wait_ge(rows_loaded, 16)
            norm(0)
            for li, (layer, blocks) in enumerate(LAYERS):
                for b in range(len(blocks)):
                    split(slot_of[((layer, blocks[b][0]), 1)] + AHEAD)
                    if layer == "even" and b >= 3:
                        take_top(2)
                    if layer == "odd" and b == 1:
                        gate_finish()
                    if blocks[b][0] in ROTATED:
                        rope_block(layer, blocks, b)
                    if layer == "even" and b == 2:
                        index_sums()
                    if layer == "odd" and b == 2:
                        forget_biases()
                if layer == "even":
                    pick()
                else:
                    dve.wait_ge(*S["nsink_ready"].at())
                attend(layer)
                for i in range(KT // 2):
                    split(slot_of[(f"{layer}_out", i)] + AHEAD)
                add_to_x(2 * li + 1, slot_of[(f"{layer}_out", KT // 2 - 1)])
                norm(2 * li + 1)
                up(li)
                for i in range(FT // 2):
                    split(slot_of[(f"down{li}", i)] + AHEAD)
                add_to_x(2 * li + 2, slot_of[(f"down{li}", FT // 2 - 1)])
                if li == 0:
                    norm(2)
            normalize(4)
            norm(5)
            split(slot_of["ab"] + AHEAD)
            decays()
            for r in range(len(ROUNDS)):
                for i in range(TICKS):
                    chain_first(r - 2, i)
                    level_first(r - 1, i)
                    if slot_at(r, i) and i % 2 == 0:
                        split(slot_of[slot_at(r, i)] + AHEAD)
                    long_taps(r * TICKS + i)
                    chain_second(r - 2, i)
                    level_second(r - 1, i)
                    if r < HEADS and i == 2:
                        conv_gate(("qk", r))
                    if r < HEADS and r % 2 == 0 and i == 4:
                        conv_gate(("v", r // 2))
                    prepare(r, i)
                    finish(r - 2, i)
                    if r == 8:
                        conv_norm(i)
                    if slot_at(r, i) and i % 2 == 1:
                        evacuate(slot_at(r, i))
            lows("o")
            for i in range(KT // 2):
                split(slot_of[("delta_out", i)] + AHEAD)
                evacuate(("delta_out", i))
            for q in range(4):
                at = (slice(None), slice(2 * q, 2 * q + 2), slice(None))
                dve.wait_ge(*S["mix_high"].at(q))
                dve.tensor_tensor(xlo[at], gts[:, 0, 2 * q:2 * q + 2, :], xhi[at].bitcast(F32), ALU.subtract)\
                    .then_inc(*S["mix_low"].one(q))
            for i in range(KT // 2):
                split(slot_of[("mix_out", i)] + AHEAD)
            add_quarter_to_x(6, slot_of[("mix_out", KT // 2 - 1)])
            norm(6)
            up2()
            dve.wait_ge(*S["p_high"].at())
            dve.tensor_tensor(plo[:, :, :], ps[:, 0, :].rearrange("p (k c) -> p k c", k=2), phi[:, :, :].bitcast(F32),
                              ALU.subtract).then_inc(*S["p_low"].one())
            for i in range(FT // 2):
                split(slot_of[("down2", i)] + AHEAD)
            add_to_x(7, slot_of[("down2", FT // 2 - 1)])
            norm(7)
            dve.wait_ge(*S["pl_rstd_ready"].at())
            for t in range(TT):
                dve.scalar_tensor_tensor(pl[:, t, :], pl[:, t, :], pl_rstd[:, t:t + 1], pl_gain[:, :], ALU.mult, ALU.mult)\
                    .then_inc(*S["pl_made"].one(t))
            for b in range(2):
                split(slot_of[(("gate", b), 1)] + AHEAD)
                for t in range(TT):
                    c = slice(b * 512, (b + 1) * 512)
                    dve.wait_ge(*S["gate_tanh_made"].at((b, t)))
                    dve.wait_ge(*S["pl_made"].at(t))
                    g = gate_tanh[:, t, :]
                    link(dve.scalar_tensor_tensor(g, g, 1.0, pl[:, t, c], ALU.add, ALU.mult))
                    last = dve.scalar_tensor_tensor(x[:, t, c], g, 0.5, x[:, t, c], ALU.mult, ALU.add)
                    last.then_inc(*(S["x_added"].one((8, t, 1)) if b else S["gate_tanh_used"].one((b, t))))
            normalize(NORMS - 1)
        return {name: event.values for name, event in S.items()}


FM_OF = {"qa": 0, "ka": 1, "qb": 2, "kb": 3, "qd": 0, "qc": 1, "kc": 2}


def pack_distances(inputs):
    q = np.arange(P)[:, None]
    distance = np.concatenate([t * P + q - np.arange(P * (t + 1))[None] for t in range(TT)], 1)
    return inputs["rel_bias"][0][:, distance + 256].transpose(1, 0, 2).reshape(P, -1)


def arrays(inputs):
    return {
        "x": inputs["x"][0], "p": inputs["p_2"][0, 0], "stream": pack_stream(inputs), "ident": np.eye(P, dtype=np.float32),
        "consts1": constants_1()[0], "consts2": constants_2()[0],
        "params1": pack_params_1(inputs)[0], "params2": pack_params_2(inputs)[0],
        "gains": pack_gains(inputs), "rows": pack_rows(inputs),
        "rel": pack_distances(inputs),
    }


def kernel(**inputs):
    import concourse.bacc as bacc
    from concourse.bass_utils import run_bass_kernel_spmd

    data = arrays({name: np.asarray(a) for name, a in inputs.items()})

    def make(counted):
        nc = bacc.Bacc("TRN2", target_bir_lowering=False, num_devices=1)
        dram = {name: nc.dram_tensor(f"in_{name}", a.shape, F32, kind="ExternalInput").ap() for name, a in data.items()}
        dram["out"] = nc.dram_tensor("out", [TOK, D], F32, kind="ExternalOutput").ap()
        return nc, build(nc, dram, counted)

    _, counted = make({})
    nc, _ = make(counted)
    r = run_bass_kernel_spmd(nc, [{f"in_{name}": a for name, a in data.items()}], core_ids=[0])
    return r.results[0]["out"].reshape(1, TOK, D)
```

```python
from contextlib import ExitStack

import numpy as np

import concourse.bass as bass
from concourse import mybir

ALU = mybir.AluOpType
ACT = mybir.ActivationFunctionType
AX = mybir.AxisListType
F32 = mybir.dt.float32
F32R = mybir.dt.float32r

P = 128
TOK = 256
TT = TOK // P
D = 1024
KT = D // P
HD = 64
FF = 2816
FT = FF // P
EPS = 1e-6
SLOT = 2048
RAW = 3
RING = 3
AHEAD = RING - 1
MASKED = -8e30
TAKEN = -3e38



def stream_plan():
    plan = []

    def rows_major(key, weight, pieces):
        for half in range(2):
            plan.append(("columns", key, weight, pieces, half))

    def pair(key, weight, a, b):
        plan.append(("pair", key, weight, a, b))

    def down(key, weight, tiles):
        for i in range(tiles // 2):
            plan.append(("down", (key, i), weight, i))

    for key, a, n in EVEN_BLOCKS:
        rows_major(("even", key), ("even_w_in", 0), [(a, n)])
    down("even_out", ("even_w_out", 0), KT)
    for layer in range(2):
        if layer == 1:
            for key, pieces in ODD_BLOCKS:
                rows_major(("odd", key), ("odd_w_in", 0), pieces)
            down("odd_out", ("odd_w_out", 0), KT)
        for j in range(FT):
            pair((f"up{layer}", j), ("ffn_w_up", layer), j * P, FF + j * P)
        down(f"down{layer}", ("ffn_w_down", layer), FT)
    plan.append(("narrow", "ab", ("w_in_2", 0), 6144, 32))
    for round_ in ROUNDS:
        for key, weight, a, b in round_:
            pair(key, (weight, 0), a, b)
    for i in range(KT // 2):
        pair(("delta_out", i), ("w_delta_out_2", 0), 2 * i * P, (2 * i + 1) * P)
    down("mix_out", ("w_o_2", 0), KT)
    for j in range(FT):
        pair(("up2", j), ("w_gate_up_2", 0), j * P, FF + j * P)
    down("down2", ("w_down_2", 0), FT)
    down("pl_proj", ("w_pl_proj_2", 0), 2)
    for i in range(2):
        rows_major(("gate", i), ("w_pl_gate_2", 0), [(i * 512, 512)])
    return plan


def rounds():
    glu = [(("glu", j), "w_in_2", j * P, 1024 + j * P) for j in range(KT)]
    gates = [(("gates", j), "w_in_2", 6176 + j * P, 7200 + j * P) for j in range(KT)]
    z = [(("z", j), "w_in_2", 5120 + 2 * j * P, 5120 + (2 * j + 1) * P) for j in range(KT // 2)]
    out = [(("conv_out", i), "w_conv_out_2", 2 * i * P, (2 * i + 1) * P) for i in range(KT // 2)]
    other = [glu[0:2], [z[0]] + glu[2:4], [glu[4], z[1]], [z[2], glu[5], z[3]], [glu[6], gates[0]],
             [glu[7]] + gates[1:3], gates[3:4], gates[4:5]]
    made = []
    for r in range(HEADS):
        slots = [(("qk", r), "w_in_2", 2048 + r * P, 3072 + r * P)]
        if r % 2 == 0:
            slots.append((("v", r // 2), "w_in_2", 4096 + r * P, 4096 + (r + 1) * P))
        made.append(slots + other[r])
    return made + [gates[5:8], out]


HEADS = 8
CHUNK = 64
LEVELS = [2, 4, 8, 16, 32]
TICKS = 8
ROUNDS = rounds()


EVEN_BLOCKS = [("idx", 1536, 324), ("qa", 0, 512), ("ka", 512, 512), ("va", 1024, 512),
               ("qb", 1860, 512), ("kb", 2372, 512), ("vb", 2884, 512)]
ODD_BLOCKS = [("kvf", [(2056, 256), (1536, 8)]), ("qd", [(1544, 512)]), ("qc", [(0, 512)]),
              ("kc", [(512, 512)]), ("vc", [(1024, 512)])]


def pack_stream(inputs):
    plan = stream_plan()
    out = np.zeros((len(plan), P, SLOT), np.float32)
    for n, (kind, _, (name, i), *args) in enumerate(plan):
        w = inputs[name][i]
        if kind == "columns":
            pieces, half = args
            view = out[n].reshape(P, 4, 512)
            at = 0
            for a, c in pieces:
                view[:, :, at:at + c] = w[half * 512:(half + 1) * 512, a:a + c].reshape(4, P, c).transpose(1, 0, 2)
                at += c
        elif kind == "pair":
            view = out[n].reshape(P, KT, 2, P)
            for m, a in enumerate(args):
                view[:, :, m, :] = w[:, a:a + P].reshape(KT, P, P).transpose(1, 0, 2)
        elif kind == "narrow":
            a, c = args
            out[n].reshape(P, KT, 256)[:, :, 0:c] = w[:, a:a + c].reshape(KT, P, c).transpose(1, 0, 2)
        elif kind == "down":
            view = out[n].reshape(P, 2, D)
            view[:] = w[args[0] * 256:args[0] * 256 + 256].reshape(2, P, D).transpose(1, 0, 2)
    return out


class Packer:

    def __init__(self):
        self.at, self.parts, self.n = {}, [], 0

    def add(self, name, a):
        a = np.ascontiguousarray(a, np.float32).reshape(P, -1)
        self.at[name] = (self.n, a.shape[1])
        self.n += a.shape[1]
        self.parts.append(a)

    def packed(self):
        return np.concatenate(self.parts, 1), self.at


def constants_1():
    c = Packer()
    p = np.arange(P)[:, None]
    s = np.arange(TOK)[None, :]
    causal, window = [], []
    for t in range(TT):
        w = P * (t + 1)
        q = t * P + p
        causal.append(np.where(s[:, :w] <= q, 0.0, MASKED))
        near = q // 64 - s[:, :w] // 64
        window.append(np.where((near >= 0) & (near <= 2), 0.0, MASKED))
    c.add("causal", np.concatenate(causal, 1))
    c.add("window", np.concatenate(window, 1))
    c.add("upto", np.stack([(t * P + p <= s) for t in range(TT)], 1))
    half = np.arange(0, HD, 2, dtype=np.float32)
    inv = (np.float32(1.0) / (np.float32(10000.0) ** (half / np.float32(HD)))).astype(np.float32)
    ang = (np.arange(TOK, dtype=np.float32)[:, None] * inv[None]).astype(np.float32).astype(np.float64)
    cos, sin = np.cos(ang), np.sin(ang)
    tiled = lambda a: a.reshape(TT, P, HD).transpose(1, 0, 2)
    c.add("cos", tiled(np.concatenate([cos, cos], 1)))
    c.add("sin", tiled(np.concatenate([-sin, sin], 1)))
    return c.packed()


def constants_2():
    c = Packer()
    k = np.arange(P)[:, None]
    m = np.arange(P)[None, :]
    same = k // CHUNK == m // CHUNK
    both = lambda forward, backward: np.stack([forward, backward], 1).astype(np.float32)
    c.add("cum", both(same & (k <= m), same & (k >= m)))
    c.add("tail", both(same & (k > m), same & (k < m)))
    c.add("off", np.where(both(same & (k <= m), same & (k >= m)) > 0, 0.0, -1e30))
    c.add("strict", both(same & (k < m), same & (k > m)))
    for b in [1] + LEVELS:
        joined = (k // (2 * b) == m // (2 * b)) & (k // b != m // b)
        above, below = joined & (k < m), joined & (k > m)
        c.add(f"one_minus_join{b}", (k == m)[:, None, :] - (both(above, below) if b == 1 else both(below, above)))
    c.add("half", np.concatenate([k // CHUNK == 0, k // CHUNK == 1], 1))
    c.add("mean", np.full((P, 1), 1.0 / D))
    return c.packed()


def pack_params_1(inputs):
    c = Packer()
    for layer in range(2):
        c.add(f"conv_w{layer}", inputs["ffn_conv_w"][layer].reshape(3, 2 * FT, P).transpose(2, 0, 1))
        c.add(f"conv_b{layer}", inputs["ffn_conv_b"][layer].reshape(2 * FT, P).T)
    return c.packed()


def pack_params_2(inputs):
    c = Packer()
    c.add("taps5", inputs["qkv_conv_w_2"][0].reshape(5, 3 * HEADS, P).transpose(2, 0, 1))
    c.add("taps31", inputs["conv_dw_w_2"][0].reshape(31, KT, P).transpose(2, 0, 1))
    for name in ("conv_dw_b_2", "conv_ln_g_2", "conv_ln_b_2"):
        c.add(name, inputs[name][0].reshape(KT, P).T)
    return c.packed()


GAINS = [("norm_mix_g", 0), ("norm_ffn_g", 0), ("norm_mix_g", 1), ("norm_ffn_g", 1), ("norm_out_g", None),
         ("g_mix_2", 0), ("g_ffn_2", 0), ("g_pl_2", 0), ("g_final_2", None), ("g_pl_proj_2", 0)]
ROWS = [("idx_k_ln_g", 0, 64), ("idx_k_ln_b", 0, 64), ("forget_b", 0, 8), ("sinks", 0, 8),
        ("a_log_2", 0, 16), ("dt_bias_2", 0, 16), ("delta_norm_g_2", 0, 128)]


def pack_gains(inputs):
    return np.stack([inputs[n] if i is None else inputs[n][i] for n, i in GAINS])


def pack_rows(inputs):
    return np.concatenate([inputs[n][i].reshape(-1) for n, i, _ in ROWS])[None]


def param_places():
    shapes = {"ffn_conv_w": (2, 3, 2 * FF), "ffn_conv_b": (2, 2 * FF), "qkv_conv_w_2": (1, 5, 3 * D), "conv_dw_w_2": (1, 31, D),
              "conv_dw_b_2": (1, D), "conv_ln_g_2": (1, D), "conv_ln_b_2": (1, D)}
    empty = {name: np.zeros(shape, np.float32) for name, shape in shapes.items()}
    return pack_params_1(empty)[1], pack_params_2(empty)[1]


PARAM1_AT, PARAM2_AT = param_places()



class Event:

    def __init__(self, sem, counted):
        self.sem, self.counted, self.values = sem, counted, {}

    def one(self, key=0):
        self.values[key] = len(self.values) + 1
        return self.sem, 1

    def at(self, key=0):
        return self.sem, self.counted[key] if self.counted else 1


EVENTS = {
    "weights_high": "slot n's rounded weights are written",
    "weights_low": "slot n's remainders are written, its raw weights no longer needed",
    "pool_weights_low": "the same by Pool, (n, half)",
    "weights_used": "TensorE is done with slot n",
    "first_summed": "the first tile of tokens is summed up with slot n, the last one of a product",
    "squared": "sum of squares of x, (k, t)",
    "rstd_ready": "reciprocal deviations, (k, t)",
    "normed": "xn written, (k, t); before it its first half",
    "norm_turned": "half of a tile of xn feature-major in its bank, (k, t, half)",
    "norm_high": "the same rounded into xhi",
    "norm_low": "the same's remainders in xlo",
    "x_added": "the residual is added to x, (k of the norm after it, t, half)",
    "rope_read": "rope has read a block's bank, (layer, b, t)",
    "rotated": "rope's result is written, (layer, b, t)",
    "copied": "a block that needs no rope is copied from its bank, (layer, b, t)",
    "block_turned": "a block is feature-major in its bank, (layer, b, t)",
    "turned_copied": "and copied to fm or fmi",
    "key_squares": "sum of squares of the centred keys, t",
    "key_rstd_ready": "their reciprocal deviations",
    "index_product": "queries times keys, u",
    "index_relu": "relu of the product, u",
    "index_sum": "and added to the score",
    "bias_ready": "half of the bias by distance is scaled and masked",
    "gate_abs": "absolute value of the forget gate's input",
    "gate_exp": "exp of minus that",
    "gate_ln": "ln(1 + that)",
    "gate_ready": "minus eight times the gate's logarithm",
    "nsink_ready": "minus the sinks",
    "forget_sum": "running sum of head h in its bank",
    "forget_bias": "bias of head h",
    "products": "queries times keys",
    "logits": "minus the logits, and the least of them",
    "exps": "exponentials and their sum",
    "sinks_done": "the sink's exponential, u",
    "probs": "probabilities",
    "probs_turned": "probabilities with the keys in the rows, in their bank",
    "probs_copied": "and copied to probT",
    "values_done": "probabilities times values",
    "mixed_high": "a pair of heads rounded into xhi, (layer, pair)",
    "mixed_low": "the pair's remainders in xlo",
    "conv_started": "newest tap and bias of gate or up channels, (layer, j, m)",
    "tap_one": "middle tap",
    "taps_done": "oldest tap",
    "gated": "silu of the gate channels",
    "hidden": "silu times up",
    "hidden_high": "the same rounded",
    "hidden_low": "the same's remainders",
    "ab_copied": "decay and beta's input copied, feature-major",
    "ab_turned": "and token-major in bank 0",
    "ab_abs": "absolute value of the decay's input, all of ab read from its bank",
    "act_step": "exp of minus the absolute value; exp(a_log)",
    "ab_ln": "ln(1 + exp)",
    "beta_tanh": "tanh of half of beta's input",
    "decay_ready": "log decays",
    "beta_ready": "beta and minus beta",
    "decay_summed": "running sums, rests and totals of the log decays in bank 7",
    "exp_sums": "their exponentials",
    "neg_sum_made": "minus the running sums",
    "conv_begun": "middle tap, (key, m)",
    "tap5": "a tap of five, (key, k, m)",
    "taps5": "the last tap, (key, m)",
    "tanh_made": "tanh for a silu or sigmoid, by name",
    "conv_gated": "silu, doubled",
    "qk_turned": "q and k token-major in bank 2, h",
    "qk_squared": "sum of squares, (h, 2 * m + t)",
    "qk_rstd_ready": "reciprocal lengths, h",
    "qk_scaled": "normalized q or k, (h, 2 * m + t)",
    "qk_back": "q and k feature-major in bank 3, h",
    "qk_feat_made": "and copied",
    "v_turned": "v of heads 2i and 2i + 1 token-major in bank 2",
    "v_made": "and copied",
    "sums_spread": "running sums in every row of bank 2, h",
    "ratio_started": "and masked, h",
    "ratio_made": "ratio of decays, (h, y)",
    "qk_products": "keys times keys and queries in bank 3, h",
    "upper_made": "triangle of the systems, h",
    "qk_ratio_made": "q k times ratio, h",
    "inverse_begun": "inverse of the 2 x 2 blocks, transposed, h",
    "inverse_turned": "and not transposed in bank 4, h",
    "inverse_first": "and copied",
    "upper_rounded": "the triangle rounded, h",
    "strict_made": "the triangle without its diagonal, h",
    "triangle_made": "and with ones there, h",
    "join_product": "it times the inverse in bank 4",
    "prod_made": "minus that, copied",
    "joined": "the next level's inverse transposed in bank 5, its change in bank 4",
    "inverse_t": "the inverse of level i - 1 transposed, copied",
    "inverse_done": "the inverse of level i",
    "check_product": "triangle times inverse in bank 4, h",
    "residual": "one minus the inverse's product, h",
    "correction": "refinement in bank 5, h",
    "solution_sum": "refined inverse, transposed, h",
    "solution": "solved values in bank 4 and keys in bank 5, h",
    "q_decayed_made": "queries times decay, (h, y)",
    "q_decayed_turned": "and feature-major in bank 3, h",
    "q_feat_made": "and copied",
    "k_decayed_made": "keys times decay, (h, y)",
    "values_made": "solved values times beta, (h, y)",
    "w_feat_made": "solved keys, feature-major, h",
    "recalled": "solved keys times state",
    "values_new": "new values",
    "o_product": "outputs of the chunk",
    "state_product": "keys times new values",
    "state_made": "state after the chunk",
    "o_added": "outputs copied or added",
    "o_squared": "sum of squares of the outputs, (h, t)",
    "o_rstd_ready": "their reciprocal deviations, h",
    "o_final": "outputs normalized and gated in xn, (h, t)",
    "glu_cleared": "zeros around glu's channels",
    "tanh_used": "the doubled product with the sigmoid is written",
    "z_made": "z's silu times the gain in xn, pair of heads",
    "slot_read_act": "tanh of both gates is written",
    "taps31": "a tap of channel tile j, (j, k); k = 31: the sum of both sums",
    "conv_mean": "mean in bank 2",
    "conv_centered": "mean subtracted",
    "conv_squared": "squares, q",
    "conv_square_used": "and their mean, q",
    "conv_var": "variance and epsilon",
    "conv_rstd": "reciprocal deviation",
    "conv_rstd_spread": "and in every row of bank 2",
    "conv_scaled": "times that, q",
    "conv_affine": "times gain plus bias, channel tile",
    "conv_tanh": "tanh of half, q",
    "conv_silu": "silu, doubled, q",
    "conv_high": "the same rounded into xhi",
    "conv_low": "the same's remainders in xlo",
    "conv_out_read": "product with the gate, of conv_out or delta_out, key of the slot",
    "mix_made": "sum of the two, q",
    "mix_high": "the same rounded into xhi",
    "mix_low": "the same's remainders in xlo",
    "p_turned": "p feature-major in bank 0",
    "p_high": "rounded",
    "p_low": "remainders",
    "pl_copied": "its projection, t",
    "pl_squared": "sum of squares, t",
    "pl_rstd_ready": "reciprocal deviations",
    "pl_made": "normalized, t",
    "gate_tanh_made": "tanh of half of the gate's input, (b, t)",
    "gate_tanh_used": "and added to x, (b, t)",
}


LAYERS = [("even", [(key, n) for key, _, n in EVEN_BLOCKS]),
          ("odd", [(key, sum(c for _, c in pieces)) for key, pieces in ODD_BLOCKS])]
ROTATED = {"idx", "qa", "ka", "kvf", "qd"}
TURNED = {"idx": 3, "qa": 4, "ka": 4, "qb": 4, "kb": 4, "kvf": 2, "qd": 4, "qc": 4, "kc": 4}
TOP_ROUNDS = (3, 3, 2)


def turned_after(layer, b):
    if layer == "even" and b <= 2:
        return [0, 1] if b == 2 else []
    return [b - 1] if b and dict(LAYERS)[layer][b - 1][0] in TURNED else []


UNITS = {layer: [(kind, h, t) for kind in kinds for h in range(8) for t in range(TT)]
         for layer, kinds in (("even", "BA"), ("odd", "DC"))}
PAIR_OF = {kt: kt - 4 if kt >= 4 else kt + 4 for kt in range(KT)}
SLOT_OF_PAIR = {pair: kt for kt, pair in PAIR_OF.items()}
NORMS = len(GAINS) - 1
LOGIT_BANKS = (0, 1, 6)


MIX_SLOTS = [("ab", -1, 0)] + [(slot[0], r, 2 * i) for r, slots in enumerate(ROUNDS) for i, slot in enumerate(slots)] \
    + [(("delta_out", i), len(ROUNDS), 0) for i in range(KT // 2)]
ORDINAL = {key: n for n, (key, _, _) in enumerate(MIX_SLOTS)}
READ_BY_ACT = {"gates"}
CONST1_AT, CONST2_AT = constants_1()[1], constants_2()[1]


CONVS = [key for key, _, _ in MIX_SLOTS if key[0] in ("qk", "v")]
ORDINAL_OF_CONV = {key: n for n, key in enumerate(CONVS)}


def slot_at(r, i):
    return ROUNDS[r][i // 2][0] if i // 2 < len(ROUNDS[r]) else None


def finished_slot(r, i):
    if i % 2 or r + i == 0:
        return None
    return slot_at(r, i - 1) if i else slot_at(r - 1, TICKS - 1)


def tanh_order():
    order = []
    for r in range(len(ROUNDS)):
        for i in range(TICKS):
            key = finished_slot(r, i)
            if key and key[0] in ("glu", "z"):
                order.append(key)
            if r < HEADS and i == 3:
                order.append(("conv", ("qk", r)))
            if r < HEADS and r % 2 == 0 and i == 5:
                order.append(("conv", ("v", r // 2)))
    return ({name: n % 2 for n, name in enumerate(order)},
            {name: order[n - 2] if n >= 2 else None for n, name in enumerate(order)},
            {n % 2: name for n, name in enumerate(order)})


TANH_OF, TANH_BEFORE, LAST_TANH = tanh_order()


TAP_SHARE = [5, 6, 0, 5, 0, 2, 4, 1, 5, 5, 0, 5, 2, 4, 3, 1]


def tap_schedule():
    ready = {key[1]: r * TICKS + tick + 1 for key, r, tick in MIX_SLOTS if key[0] == "glu"}
    ticks, todo, n = {}, [(j, k) for j in range(KT) for k in range(31)], 0
    share = [TAP_SHARE[tick % (2 * TICKS)] for tick in range(TICKS * 8)]
    for tick in range(TICKS * 8):
        most = -(-len(todo) * share[tick] // max(sum(share[tick:]), 1)) + (1 if share[tick] else 0)
        while todo and most and ready[todo[0][0]] < tick:
            ticks.setdefault(tick, []).append(todo.pop(0))
            most -= 1
    assert not todo
    return ticks


TAPS = tap_schedule()


def build(nc, dram, counted, stop=None):
    plan = stream_plan()
    const1_at, const2_at = CONST1_AT, CONST2_AT
    param1_at, param2_at = PARAM1_AT, PARAM2_AT
    slot_of = {}
    for n, entry in enumerate(plan):
        slot_of[(entry[1], entry[4]) if entry[0] == "columns" else entry[1]] = n
    ctx = ExitStack()
    with ctx:
        S = {name: Event(ctx.enter_context(nc.semaphore(name)), counted.get(name)) for name in EVENTS}
        ident_loaded, consts_loaded, params_loaded, rows_loaded, bias_loaded, gain_loaded, consts2_loaded, \
            params2_loaded, p_loaded, stored = [ctx.enter_context(nc.semaphore(name)) for name in (
                "ident_loaded", "consts_loaded", "params_loaded", "rows_loaded", "bias_loaded", "gain_loaded",
                "consts2_loaded", "params2_loaded", "p_loaded", "stored")]
        gain_5_loaded = ctx.enter_context(nc.semaphore("gain_5_loaded"))
        x_loaded = [ctx.enter_context(nc.semaphore(f"x_loaded{t}")) for t in range(TT)]
        weights_loaded = [ctx.enter_context(nc.semaphore(f"weights_loaded{i}")) for i in range(RAW)]
        dve_step, pool_step = [ctx.enter_context(nc.semaphore(name)) for name in ("dve_step", "pool_step")]

        def sb(name, shape, dt=F32, where=ctx):
            return where.enter_context(nc.sbuf_tensor(name, shape, dt))

        raw = sb("raw", [P, RAW, SLOT])
        whi = sb("whi", [P, RING, SLOT], F32R)
        wlo = sb("wlo", [P, RING, SLOT], F32R)
        x = sb("x", [P, TT, D])
        xn = sb("xn", [P, TT, D])
        xhi = sb("xhi", [P, KT, TOK], F32R)
        xlo = sb("xlo", [P, KT, TOK], F32R)
        gain = sb("gain", [P, D])
        ident = sb("ident", [P, P])[:, :]
        rows = sb("rows", [P, dram["rows"].shape[1]])
        sumsq = sb("sumsq", [P, TT])
        rstd = sb("rstd", [P, TT])
        half_power = sb("half_power", [P, 4])

        first = ExitStack()
        cst1 = sb("cst1", [P, dram["consts1"].shape[1]], F32, first)
        par1 = sb("par1", [P, dram["params1"].shape[1]], F32, first)
        with ExitStack() as area:
            hhi = sb("hhi", [P, FT, TOK], F32R, area)
            hlo = sb("hlo", [P, FT, TOK], F32R, area)
            cv = sb("cv", [P, 2, 2, TOK], F32, area)
            sg = sb("sg", [P, 2, TOK], F32, area)
            hf = sb("hf", [P, 2, TOK], F32, area)
        with ExitStack() as area:
            temp = sb("temp", [P, 2, TT, 512], F32, area)
            rope_a = sb("rope_a", [P, 512], F32, area)
            rope_b = sb("rope_b", [P, 512], F32, area)
            v0 = sb("v0", [P, TT, 512], F32, area)
            v1 = sb("v1", [P, TT, 512], F32, area)
            fm = sb("fm", [P, 4, 4, TOK], F32, area)
            fmi = sb("fmi", [P, 3, TOK], F32, area)
            bias = sb("bias", [P, 8, 384], F32, area)
            picked = sb("picked", [P, TT, TOK], F32, area)
            score = sb("score", [P, TT, TOK], F32, area)
            rel = sb("rel", [P, 2, TOK], F32, area)
            prob = sb("prob", [P, 3, TOK], F32, area)
            probT = sb("probT", [P, 2, TOK], F32, area)
            ks = sb("ks", [P, 3, TT, 64], F32, area)
            key_mean = sb("key_mean", [P, TT], F32, area)
            key_var = sb("key_var", [P, TT], F32, area)
            key_rstd = sb("key_rstd", [P, TT], F32, area)
            index_w = sb("index_w", [P, TT, 4], F32, area)
            top8 = sb("top8", [P, 8], F32, area)
            gate = sb("gate", [P, 4, TT * 8], F32, area)
            lowest = sb("lowest", [P, 4], F32, area)
            total = sb("total", [P, 4], F32, area)
            sunk = sb("sunk", [P, 4], F32, area)
            inverse = sb("inverse", [P, 4], F32, area)
            nsink = sb("nsink", [P, 8], F32, area)
        first.close()
        with ExitStack() as area:
            cst2 = sb("cst2", [P, dram["consts2"].shape[1]], F32, area)
            par2 = sb("par2", [P, dram["params2"].shape[1]], F32, area)
            twice_b = sb("twice_b", [P, KT], F32, area)
            half_g = sb("half_g", [P, KT], F32, area)
            ab = sb("ab", [P, 5, TT, 32], F32, area)
            ab_feat = sb("ab_feat", [P, TOK], F32, area)
            neg_rate = sb("neg_rate", [P, 16], F32, area)
            decay = sb("decay", [P, TT, 16], F32, area)
            beta = sb("beta", [P, TT, 16], F32, area)
            neg_beta = sb("neg_beta", [P, TT, 16], F32, area)
            neg_sum = sb("neg_sum", [P, TT, 16], F32, area)
            exp_sum = sb("exp_sum", [P, P], F32, area)
            conv = sb("conv", [P, 2, 2, TOK], F32, area)
            tanh = sb("tanh", [P, 2, 512], F32, area)
            qk_tok = sb("qk_tok", [P, 2, 2, TT, P], F32, area)
            v_tok = sb("v_tok", [P, 4, TT, P], F32, area)
            qk_sq = sb("qk_sq", [P, 4], F32, area)
            qk_rstd = sb("qk_rstd", [P, 4], F32, area)
            qk_feat = sb("qk_feat", [P, 2, TOK], F32, area)
            ratio = sb("ratio", [P, 4, P], F32, area)
            upper = sb("upper", [P, 4, P], F32, area)
            qk_ratio = sb("qk_ratio", [P, 2, 4, P], F32, area)
            upper_r = sb("upper_r", [P, 4, P], F32R, area)
            inv_t = sb("inv_t", [P, 4, P], F32R, area)
            inv = sb("inv", [P, 4, P], F32R, area)
            prod = sb("prod", [P, 4, P], F32R, area)
            q_decayed = sb("q_decayed", [P, 4, P], F32, area)
            solved = sb("solved", [P, 4, P], F32, area)
            k_decayed = sb("k_decayed", [P, 4, P], F32, area)
            k_rest = sb("k_rest", [P, 2, 4, P], F32, area)
            q_feat = sb("q_feat", [P, 2, 4, P], F32, area)
            values = sb("values", [P, 4, P], F32, area)
            w_feat = sb("w_feat", [P, 4, P], F32, area)
            state = sb("state", [P, 2, P], F32, area)
            o_tok = sb("o_tok", [P, TT, P], F32, area)
            odd_taps = sb("odd_taps", [P, TOK], F32, area)
            conv_rsd = sb("conv_rsd", [P, TT], F32, area)
            o_sq = sb("o_sq", [P, 2 * TT], F32, area)
            o_rstd = sb("o_rstd", [P, TT], F32, area)
            glu_in = sb("glu_in", [P, 3, TOK + 30], F32, area)
            cacc = sb("cacc", [P, KT, TOK], F32, area)
            gts = sb("gts", [P, 2, KT, TOK], F32, area)
            gain_5 = cacc[:, 0:4, :].rearrange("p k c -> p (k c)")
        with ExitStack() as area:
            hhi2 = sb("hhi2", [P, FT, TOK], F32R, area)
            hlo2 = sb("hlo2", [P, FT, TOK], F32R, area)
            sg2 = sb("sg2", [P, 2, TOK], F32, area)
            hf2 = sb("hf2", [P, 2, TOK], F32, area)
            p_tok = sb("p_tok", [P, TT, TOK], F32, area)
            phi = sb("phi", [P, 2, TOK], F32R, area)
            plo = sb("plo", [P, 2, TOK], F32R, area)
            pl = sb("pl", [P, TT, D], F32, area)
            pl_junk = sb("pl_junk", [P, TT, D], F32, area)
            pl_gain = sb("pl_gain", [P, D], F32, area)
            pl_sq = sb("pl_sq", [P, TT], F32, area)
            pl_rstd = sb("pl_rstd", [P, TT], F32, area)
            gate_tanh = sb("gate_tanh", [P, 2, 512], F32, area)

        ps = ctx.enter_context(nc.psum_tensor("ps", [P, 8, 512], F32))
        block = ctx.enter_context(nc.Block())

        def C(name):
            if name in const1_at:
                a, n = const1_at[name]
                return cst1[:, a:a + n]
            a, n = const2_at[name]
            return cst2[:, a:a + n]

        def pair_of(name, r):
            return C(name)[:, r * P:(r + 1) * P]

        def systems(name):
            return C(name).rearrange("p (r c) -> p r c", r=2).unsqueeze(2).broadcast_to([P, 2, TT, P])

        def four(ap):
            return ap.rearrange("p (r t) c -> p r t c", r=2)

        def par_at(name, i, n=1):
            if name in param1_at:
                return par1[:, param1_at[name][0] + i:param1_at[name][0] + i + n]
            return par2[:, param2_at[name][0] + i:param2_at[name][0] + i + n]

        def chunk_of(step, r):
            c = step if r == 0 else 3 - step
            return c // 2, (c % 2) * CHUNK

        row_at, r = {}, 0
        for n, _, w in ROWS:
            row_at[n] = rows[:, r:r + w]
            r += w
        def used(ring, n):
            return weights_of(n, ring[:, n % ring.shape[1], :])

        def weights_of(n, at):
            entry = plan[n]
            if entry[0] == "columns":
                return at.rearrange("p (k c) -> p k c", k=4)[:, :, 0:sum(c for _, c in entry[3])]
            if entry[0] == "narrow":
                return at.rearrange("p (k c) -> p k c", k=KT)[:, :, 0:entry[4]]
            return at

        def logit_bias(kind, h, t):
            w = P * (t + 1)
            if kind in "BC":
                return bias[:, h, P * t:P * t + w]
            if kind == "A":
                return picked[:, t, 0:w]
            return C("window")[:, P * t:P * t + w]

        def base(h):
            return (h % 2) * HD

        def qk_of(kind, h, t):
            w = P * (t + 1)
            rows_ = slice(base(h), base(h) + HD)
            q = {"A": 0, "B": 2, "D": 0, "C": 1}[kind]
            query = fm[rows_, q, h // 2, t * P:(t + 1) * P]
            if kind == "D":
                return query, fmi[rows_, h // 4, 0:w]
            return query, fm[rows_, {"A": 1, "B": 3, "C": 2}[kind], h // 2, 0:w]

        def v_of(kind, h, s):
            if kind == "D":
                return v1[:, s, (h // 4) * HD:(h // 4 + 1) * HD]
            return (v1 if kind == "B" else v0)[:, s, h * HD:(h + 1) * HD]

        def weights_low(n):
            return S["pool_weights_low"].at((n, 1)) if n in POOL_SLOTS else S["weights_low"].at((n, 1))

        def summed(n, t):
            return S["weights_used"].at(n) if t else S["first_summed"].at(n)

        def slot_read(key):
            if key == "ab":
                return S["ab_abs"].at()
            if key[0] in ("qk", "v"):
                return S["taps5"].at((key, 1))
            if key[0] == "gates":
                return S["slot_read_act"].at(key)
            if key[0] in ("glu", "z"):
                return S["tanh_used"].at(key)
            return S["conv_out_read"].at(key)

        def tanh_free(name):
            return S["conv_gated"].at(name[1]) if name[0] == "conv" else S["tanh_used"].at(name)

        def channel_tile(key, m):
            return m * HEADS + key[1] if key[0] == "qk" else 2 * HEADS + 2 * key[1] + m

        POOL_SLOTS = [slot_of[key] + AHEAD for key, r, tick in MIX_SLOTS if r >= 0 and tick != 4 and r < len(ROUNDS)]
        POOL_SLOTS += [slot_of[((layer, key), 1)] for layer, blocks in LAYERS
                       for key, _ in blocks[2 if layer == "even" else 1:]]
        o_junk = ab[:, 3:5, :, :].rearrange("p a t c -> p (a t c)")
        k_before = {1: 0, 3: 1, 4: 3}

        @block.sync
        def _(sp):
            sp.dma_start(ident, dram["ident"]).then_inc(ident_loaded, 16)
            for t in range(TT):
                sp.dma_start(x[:, t, :], dram["x"][t * P:(t + 1) * P, :]).then_inc(x_loaded[t], 16)
            for n in range(len(plan)):
                if n >= RAW:
                    sp.wait_ge(*weights_low(n - RAW))
                sp.dma_start(used(raw, n), weights_of(n, dram["stream"][n])).then_inc(weights_loaded[n % RAW], 16)
            for t in range(TT):
                sp.wait_ge(*S["normed"].at((NORMS - 1, t)))
                sp.dma_start(dram["out"][t * P:(t + 1) * P, :], xn[:, t, :]).then_inc(stored, 16)
            sp.wait_ge(stored, 16 * TT)

        @block.gpsimd
        def _(pool):
            steps = [0]

            def link(ins):
                steps[0] += 1
                ins.then_inc(pool_step, 1)
                pool.wait_ge(pool_step, steps[0])

            def load_gain(k):
                if k >= 1:
                    pool.wait_ge(*S["normed"].at((k - 1, TT - 1)))
                pool.dma_start(gain[:, :], dram["gains"][k:k + 1, :].broadcast_to([P, D]))\
                    .then_inc(gain_loaded, 16)

            def rstd_of(out, mean, scale, eps):
                link(pool.tensor_scalar(mean, mean, scale, eps, ALU.mult, ALU.add))
                return pool.tensor_tensor(out, mean, half_power[:, 0:out.shape[1]], ALU.pow)

            def norm(k):
                for t in range(TT):
                    pool.wait_ge(*S["squared"].at((k, t)))
                    if k:
                        pool.wait_ge(*S["normed"].at((k - 1, t)))
                    rstd_of(rstd[:, t:t + 1], sumsq[:, t:t + 1], 1.0 / D, EPS).then_inc(*S["rstd_ready"].one((k, t)))

            def split(layer, b):
                n = slot_of[((layer, (EVEN_BLOCKS if layer == "even" else ODD_BLOCKS)[b][0]), 1)]
                pool.wait_ge(*S["weights_high"].at((n, 1)))
                pool.tensor_tensor(used(wlo, n), used(raw, n), used(whi, n).bitcast(F32), ALU.subtract)\
                    .then_inc(*S["pool_weights_low"].one((n, 1)))

            load_gain(0)
            link(pool.memset(half_power[:, :], -0.5))
            pool.dma_start(rows[:, :], dram["rows"].broadcast_to([P, rows.shape[1]])).then_inc(rows_loaded, 16)
            pool.dma_start(cst1[:, :], dram["consts1"]).then_inc(consts_loaded, 16)
            norm(0)
            pool.wait_ge(*S["key_squares"].at(TT - 1))
            rstd_of(key_rstd[:, :], key_var[:, :], 1.0 / HD, EPS).then_inc(*S["key_rstd_ready"].one())
            pool.dma_start(bias[:, :, :], dram["rel"].rearrange("p (h c) -> p h c", h=8)).then_inc(bias_loaded, 16)
            split("even", 2)
            pool.dma_start(par1[:, :], dram["params1"]).then_inc(params_loaded, 16)
            split("even", 3)
            pool.wait_ge(bias_loaded, 16)
            for half in range(2):
                link(pool.tensor_scalar(bias[:, 4 * half:4 * half + 4, :], bias[:, 4 * half:4 * half + 4, :], 8.0, None, ALU.mult))
                split("even", 4 + half)
            pool.memset(bias[0:64, :, 64:128], MASKED).then_inc(*S["bias_ready"].one(0))
            pool.memset(bias[0:64, :, P + 192:P + 256], MASKED).then_inc(*S["bias_ready"].one(1))
            split("even", 6)
            for k in range(1, 6):
                if k < 5:
                    load_gain(k)
                norm(k)
                if k == 4:
                    pool.dma_start(cst2[:, :], dram["consts2"]).then_inc(consts2_loaded, 16)
                    pool.dma_start(par2[:, :], dram["params2"]).then_inc(params2_loaded, 16)
                if k == 2:
                    for b in range(1, len(ODD_BLOCKS)):
                        split("odd", b)

            pool.memset(glu_in[:, :, :], 0.0).then_inc(*S["glu_cleared"].one())
            pool.wait_ge(consts2_loaded, 16)

            def prepare(h, i):
                if h >= HEADS:
                    return
                if i == 4:
                    pool.wait_ge(*S["qk_squared"].at((h, 3)))
                    link(pool.tensor_scalar(qk_sq[:, :], qk_sq[:, :], 0.25, EPS, ALU.mult, ALU.add))
                    pool.tensor_tensor(qk_rstd[:, :], qk_sq[:, :], half_power[:, 0:4], ALU.pow)\
                        .then_inc(*S["qk_rstd_ready"].one(h))
                if i == 7:
                    pool.wait_ge(*S["strict_made"].at(h))
                    pool.tensor_tensor(upper[:, :, :], upper[:, :, :], ident.unsqueeze(1).broadcast_to([P, 4, P]), ALU.add)\
                        .then_inc(*S["triangle_made"].one(h))
                    pool.wait_ge(*S["triangle_made"].at(h))
                    if h:
                        pool.wait_ge(*S["solution"].at(h - 1))
                    pool.tensor_tensor(four(inv_t[:, :, :]), four(upper[:, :, :]), systems("one_minus_join1"), ALU.mult)\
                        .then_inc(*S["inverse_begun"].one(h))

            def split_half(n, half):
                if n in POOL_SLOTS:
                    pool.wait_ge(*S["weights_high"].at((n, half)))
                    c = slice(half * SLOT // 2, (half + 1) * SLOT // 2)
                    pool.tensor_tensor(wlo[:, n % RING, c], raw[:, n % RAW, c], whi[:, n % RING, c].bitcast(F32),
                                       ALU.subtract).then_inc(*S["pool_weights_low"].one((n, half)))

            def finish(h, i):
                if not 0 <= h < HEADS:
                    return
                if i == 4:
                    pool.wait_ge(*S["o_squared"].at((h, TT - 1)))
                    link(pool.tensor_scalar(o_sq[:, 0:TT], o_sq[:, 0:TT], 1.0 / P, EPS, ALU.mult, ALU.add))
                    pool.tensor_tensor(o_rstd[:, :], o_sq[:, 0:TT], half_power[:, 0:TT], ALU.pow)\
                        .then_inc(*S["o_rstd_ready"].one(h))

            for r in range(len(ROUNDS)):
                for i in range(TICKS):
                    prepare(r, i)
                    finish(r - 2, i)
                    if r == 8 and i == 2:
                        pool.wait_ge(*S["conv_var"].at())
                        pool.tensor_tensor(conv_rsd[:, :], conv_rsd[:, :], half_power[:, 0:TT], ALU.pow)\
                            .then_inc(*S["conv_rstd"].one())
                    if slot_at(r, i):
                        split_half(slot_of[slot_at(r, i)] + AHEAD, i % 2)

            load_gain(6)
            pool.wait_ge(*S["x_added"].at((6, TT - 1, 1)))
            pool.dma_start(p_tok[:, :, :], dram["p"].rearrange("(t p) d -> p t d", p=P)).then_inc(p_loaded, 16)
            pool.dma_start(pl_gain[:, :], dram["gains"][NORMS:NORMS + 1, :].broadcast_to([P, D])).then_inc(p_loaded, 16)
            norm(6)
            load_gain(7)
            norm(7)
            pool.wait_ge(*S["pl_squared"].at(TT - 1))
            rstd_of(pl_rstd[:, :], pl_sq[:, :], 1.0 / D, EPS).then_inc(*S["pl_rstd_ready"].one())
            load_gain(8)
            norm(8)

        @block.tensor
        def _(pe):
            def three(out, a_hi, a_lo, b_hi, b_lo, start, stop):
                nc.tensor.matmul(out, a_hi, b_hi, start=start, stop=False)
                nc.tensor.matmul(out, a_hi, b_lo, start=False, stop=False)
                return nc.tensor.matmul(out, a_lo, b_hi, start=False, stop=stop)

            def norm(k):
                for t in range(TT):
                    for half in range(2):
                        pe.wait_ge(*S["normed"].at((k, t) if half else (k, t, "first half")))
                        for i in range(4):
                            last = nc.tensor.transpose(ps[:, 4 + 2 * t + half, i * P:(i + 1) * P],
                                                       xn[:, t, (4 * half + i) * P:(4 * half + i + 1) * P], ident)
                        last.then_inc(*S["norm_turned"].one((k, t, half)))

            def wait_split(k, t, halves=(0, 1)):
                for half in halves:
                    pe.wait_ge(*S["norm_low"].at((k, t, half)))

            def columns(layer, blocks, b, norm, first_bank=0):
                key, width = blocks[b]
                for half in range(2):
                    n = slot_of[((layer, key), half)]
                    pe.wait_ge(*weights_low(n))
                    wh, wl = used(whi, n), used(wlo, n)
                    for t in range(TT):
                        if b == 0:
                            wait_split(norm, t, (half,))
                        for k in range(4):
                            kt = 4 * half + k
                            last = three(ps[:, first_bank + 2 * (b % 2) + t, 0:width], xhi[:, kt, t * P:(t + 1) * P],
                                         xlo[:, kt, t * P:(t + 1) * P], wh[:, k, :], wl[:, k, :],
                                         kt == 0, kt == KT - 1)
                        if half and t == 0:
                            last.then_inc(*S["first_summed"].one(n))
                    last.then_inc(*S["weights_used"].one(n))

            def block_read(layer, blocks, b):
                rotated = blocks[b][0] in ROTATED
                for t in range(TT):
                    pe.wait_ge(*(S["rope_read"] if rotated else S["copied"]).at((layer, b, t)))

            def turn_block(layer, blocks, b, before):
                key = blocks[b][0]
                for t in range(TT):
                    pe.wait_ge(*(S["rotated"] if key in ROTATED else S["copied"]).at((layer, b, t)))
                    if before is not None:
                        pe.wait_ge(*S["turned_copied"].at((layer, before, t)))
                    for i in range(TURNED[key]):
                        last = nc.tensor.transpose(ps[:, 4 + t, i * P:(i + 1) * P],
                                                   temp[:, b % 2, t, i * P:(i + 1) * P], ident)
                    last.then_inc(*S["block_turned"].one((layer, b, t)))

            def index_scores():
                pe.wait_ge(*S["turned_copied"].at(("even", 0, 0)))
                pe.wait_ge(*S["turned_copied"].at(("even", 0, 1)))
                for u in range(8):
                    h, t = u // 2, u % 2
                    if u >= 2:
                        pe.wait_ge(*S["index_relu"].at(u - 2))
                    r = slice(base(h), base(h) + HD)
                    nc.tensor.matmul(ps[:, 6 + u % 2, 0:P * (t + 1)], fmi[r, h // 2, t * P:(t + 1) * P],
                                     fmi[r, 2, 0:P * (t + 1)], start=True, stop=True)\
                        .then_inc(*S["index_product"].one(u))

            def forget_sums():
                pe.wait_ge(consts_loaded, 16)
                pe.wait_ge(*S["gate_ready"].at())
                for h in range(8):
                    if h >= 2:
                        pe.wait_ge(*S["forget_bias"].at(h - 2))
                    for s in range(TT):
                        last = nc.tensor.matmul(ps[:, 6 + h % 2, 0:TOK],
                                                gate[:, 3, s * 8 + h:s * 8 + h + 1].broadcast_to([P, P]),
                                                C("upto")[:, s * TOK:(s + 1) * TOK], start=(s == 0), stop=(s == 1))
                    last.then_inc(*S["forget_sum"].one(h))

            def attend(layer, blocks):
                units = UNITS[layer]
                n = len(units)
                for b, (key, _) in enumerate(blocks):
                    for t in range(TT):
                        if key in TURNED:
                            pe.wait_ge(*S["turned_copied"].at((layer, b, t)))
                        else:
                            pe.wait_ge(*S["copied"].at((layer, b, t)))
                block_read(layer, blocks, len(blocks) - 2)
                block_read(layer, blocks, len(blocks) - 1)
                for h in range(2):
                    pe.wait_ge(*(S["index_relu"] if layer == "even" else S["forget_bias"]).at(6 + h))
                for u in range(-1, n + 3):
                    if u + 1 < n:
                        kind, h, t = units[u + 1]
                        if u >= 2:
                            pe.wait_ge(*S["logits"].at((layer, u - 2)))
                        q, k = qk_of(kind, h, t)
                        nc.tensor.matmul(ps[:, LOGIT_BANKS[(u + 1) % 3], 0:P * (t + 1)], q, k, start=True, stop=True)\
                            .then_inc(*S["products"].one((layer, u + 1)))
                    if 2 <= u < n + 2:
                        v = u - 2
                        kind, h, t = units[v]
                        pe.wait_ge(*S["probs"].at((layer, v)))
                        if v >= 2:
                            pe.wait_ge(*S["probs_copied"].at((layer, v - 2)))
                        for s in range(t + 1):
                            last = nc.tensor.transpose(ps[:, 2 + v % 2, s * P:(s + 1) * P],
                                                       prob[:, v % 3, s * P:(s + 1) * P], ident)
                        last.then_inc(*S["probs_turned"].one((layer, v)))
                    if u >= 3:
                        v = u - 3
                        kind, h, t = units[v]
                        pair = v // 4
                        pe.wait_ge(*S["probs_copied"].at((layer, v)))
                        if v % 4 == 0 and pair >= 2:
                            pe.wait_ge(*S["mixed_low"].at((layer, pair - 2)))
                        for s in range(t + 1):
                            last = nc.tensor.matmul(ps[base(h):base(h) + HD, 4 + pair % 2, t * P:(t + 1) * P],
                                                    v_of(kind, h, s), probT[:, v % 2, s * P:(s + 1) * P],
                                                    start=(s == 0), stop=(s == t))
                        last.then_inc(*S["values_done"].one((layer, v)))

            def down(key, tiles, a_hi, a_lo, ready):
                for i in range(tiles // 2):
                    n = slot_of[(key, i)]
                    pe.wait_ge(*weights_low(n))
                    wh = used(whi, n).rearrange("p (k c) -> p k c", k=2)
                    wl = used(wlo, n).rearrange("p (k c) -> p k c", k=2)
                    for k in range(2):
                        ready(2 * i + k)
                    for t in range(TT):
                        for half in range(2):
                            c = slice(half * 512, (half + 1) * 512)
                            for k in range(2):
                                kt = 2 * i + k
                                last = three(ps[:, 4 + 2 * t + half, :], a_hi[:, kt, t * P:(t + 1) * P],
                                             a_lo[:, kt, t * P:(t + 1) * P], wh[:, k, c], wl[:, k, c],
                                             kt == 0, kt == tiles - 1)
                        if t == 0 and i == tiles // 2 - 1:
                            last.then_inc(*S["first_summed"].one(n))
                    last.then_inc(*S["weights_used"].one(n))

            def half_slot(key, m, part):
                n, o = slot_of[key], ORDINAL[key]
                if m == 0 and part == 0:
                    pe.wait_ge(*weights_low(n))
                    if o >= 2:
                        pe.wait_ge(*slot_read(MIX_SLOTS[o - 2][0]))
                if key[0] == "z":
                    wh = used(whi, n).rearrange("p (k c) -> p k c", k=KT)
                    wl = used(wlo, n).rearrange("p (k c) -> p k c", k=KT)
                else:
                    wh = used(whi, n).rearrange("p (k m c) -> p k m c", k=KT, m=2)[:, :, m, :]
                    wl = used(wlo, n).rearrange("p (k m c) -> p k m c", k=KT, m=2)[:, :, m, :]
                for kt in range(part * KT // 2, (part + 1) * KT // 2):
                    if key == ("conv_out", 0) and m == 0 and kt % 2 == 0:
                        pe.wait_ge(*S["conv_low"].at(kt // 2))
                    if key[0] == "z":
                        width = wh.shape[2]
                        last = three(ps[:, o % 2, m * width:(m + 1) * width], xhi[:, kt, m * P:(m + 1) * P],
                                     xlo[:, kt, m * P:(m + 1) * P], wh[:, kt, :], wl[:, kt, :], kt == 0, kt == KT - 1)
                    else:
                        last = three(ps[:, o % 2, m * TOK:(m + 1) * TOK], wh[:, kt, :], wl[:, kt, :],
                                     xhi[:, kt, :], xlo[:, kt, :], kt == 0, kt == KT - 1)
                if m == 1 and part == 1:
                    last.then_inc(*S["weights_used"].one(n))

            def ab_channels():
                n = slot_of["ab"]
                pe.wait_ge(*weights_low(n))
                wh, wl = used(whi, n), used(wlo, n)
                for kt in range(KT):
                    if kt % 4 == 0:
                        for t in range(TT):
                            wait_split(5, t, (kt // 4,))
                    last = three(ps[0:32, 0, 0:TOK], wh[:, kt, :], wl[:, kt, :], xhi[:, kt, :], xlo[:, kt, :],
                                 kt == 0, kt == KT - 1)
                last.then_inc(*S["weights_used"].one(n))
                pe.wait_ge(*S["ab_copied"].at())
                for t in range(TT):
                    last = nc.tensor.transpose(ps[:, 0, TOK + t * 32:TOK + (t + 1) * 32], ab_feat[0:32, t * P:(t + 1) * P], ident[0:32, 0:32])
                last.then_inc(*S["ab_turned"].one())

            def decay_sums():
                pe.wait_ge(consts2_loaded, 16)
                pe.wait_ge(*S["decay_ready"].at())
                for t in range(TT):
                    for r in range(2):
                        g = decay[:, t, r * 8:r * 8 + 8]
                        c = t * 16 + r * 8
                        nc.tensor.matmul(ps[:, 7, c:c + 8], pair_of("cum", r), g, start=True, stop=True)
                        nc.tensor.matmul(ps[:, 7, 32 + c:40 + c], pair_of("tail", r), g, start=True, stop=True)
                    for q in range(2):
                        c = 64 + (2 * t + q) * 16
                        last = nc.tensor.matmul(ps[:, 7, c:c + 16], C("half")[:, q:q + 1].broadcast_to([P, P]), decay[:, t, :], start=True, stop=True)
                last.then_inc(*S["decay_summed"].one())

            def prepare(h, i):
                if h >= HEADS:
                    return
                if i == 3:
                    c = ORDINAL_OF_CONV[("qk", h)]
                    pe.wait_ge(*S["conv_gated"].at(("qk", h)))
                    if h:
                        pe.wait_ge(*S["ratio_started"].at(h - 1))
                    for m in range(2):
                        for t in range(TT):
                            last = nc.tensor.transpose(ps[:, 2, (2 * m + t) * P:(2 * m + t + 1) * P],
                                                       conv[:, c % 2, m, t * P:(t + 1) * P], ident)
                    last.then_inc(*S["qk_turned"].one(h))
                if i == 5:
                    pe.wait_ge(*S["qk_scaled"].at((h, 3)))
                    if h:
                        pe.wait_ge(*S["q_feat_made"].at(h - 1))
                    for m in range(2):
                        for t in range(TT):
                            last = nc.tensor.transpose(ps[:, 3, (2 * m + t) * P:(2 * m + t + 1) * P],
                                                       qk_tok[:, h % 2, m, t, :], ident)
                    last.then_inc(*S["qk_back"].one(h))
                    if h % 2 == 0:
                        c = ORDINAL_OF_CONV[("v", h // 2)]
                        pe.wait_ge(*S["conv_gated"].at(("v", h // 2)))
                        for m in range(2):
                            for t in range(TT):
                                last = nc.tensor.transpose(ps[:, 2, (2 * m + t) * P:(2 * m + t + 1) * P],
                                                           conv[:, c % 2, m, t * P:(t + 1) * P], ident)
                        last.then_inc(*S["v_turned"].one(h // 2))
                if i == 6:
                    if h % 2 == 0:
                        pe.wait_ge(*S["v_made"].at(h // 2))
                    for r in range(2):
                        for t in range(TT):
                            col = decay[:, t, r * 8 + h:r * 8 + h + 1]
                            last = nc.tensor.matmul(ps[:, 2, (2 * r + t) * P:(2 * r + t + 1) * P], col.broadcast_to([P, P]),
                                                    pair_of("cum", r), start=True, stop=True)
                    last.then_inc(*S["sums_spread"].one(h))
                    pe.wait_ge(*S["qk_feat_made"].at(h))
                    for m in range(2):
                        for t in range(TT):
                            last = nc.tensor.matmul(ps[:, 3, (2 * m + t) * P:(2 * m + t + 1) * P],
                                                    qk_feat[:, 1, t * P:(t + 1) * P], qk_feat[:, 1 - m, t * P:(t + 1) * P],
                                                    start=True, stop=True)
                    last.then_inc(*S["qk_products"].one(h))

            def level_first(h, i):
                if not 0 <= h < HEADS:
                    return
                if 1 <= i <= 5:
                    pe.wait_ge(*S["upper_rounded"].at(h))
                    pe.wait_ge(*(S["inverse_done"].at((h, i - 1)) if i > 1 else S["inverse_first"].at(h)))
                    for y in range(4):
                        last = nc.tensor.matmul(ps[:, 4, y * P:(y + 1) * P], upper_r[:, y, :], inv[:, y, :],
                                                start=True, stop=True)
                    last.then_inc(*S["join_product"].one((h, i)))
                if i == 2:
                    pe.wait_ge(*S["q_decayed_made"].at((h, 3)))
                    pe.wait_ge(*S["qk_ratio_made"].at(h))
                    for y in range(4):
                        last = nc.tensor.transpose(ps[:, 3, y * P:(y + 1) * P], q_decayed[:, y, :], ident)
                    last.then_inc(*S["q_decayed_turned"].one(h))
                if i == 6:
                    pe.wait_ge(*S["inverse_done"].at((h, 5)))
                    for y in range(4):
                        last = nc.tensor.matmul(ps[:, 4, y * P:(y + 1) * P], upper[:, y, :], inv[:, y, :].bitcast(F32),
                                                start=True, stop=True)
                    last.then_inc(*S["check_product"].one(h))
                if i == 7:
                    pe.wait_ge(*S["solution_sum"].at(h))
                    pe.wait_ge(*S["k_decayed_made"].at((h, 3)))
                    for y in range(4):
                        nc.tensor.matmul(ps[:, 4, y * P:(y + 1) * P], solved[:, y, :], v_tok[:, h % 4, y % 2, :],
                                         start=True, stop=True)
                    for y in range(4):
                        last = nc.tensor.matmul(ps[:, 5, y * P:(y + 1) * P], k_decayed[:, y, :], solved[:, y, :],
                                                start=True, stop=True)
                    last.then_inc(*S["solution"].one(h))

            def level_second(h, i):
                if not 0 <= h < HEADS:
                    return
                if i == 0:
                    pe.wait_ge(*S["inverse_begun"].at(h))
                    if h:
                        pe.wait_ge(*S["values_made"].at((h - 1, 3)))
                    for y in range(4):
                        last = nc.tensor.transpose(ps[:, 4, y * P:(y + 1) * P], inv_t[:, y, :].bitcast(F32), ident)
                    last.then_inc(*S["inverse_turned"].one(h))
                if 1 <= i <= 5:
                    pe.wait_ge(*S["prod_made"].at((h, i)))
                    if i >= 2:
                        pe.wait_ge(*S["inverse_t"].at((h, i)))
                    if i == 1 and h:
                        pe.wait_ge(*S["w_feat_made"].at(h - 1))
                    for y in range(4):
                        nc.tensor.matmul(ps[:, 5, y * P:(y + 1) * P], prod[:, y, :], inv_t[:, y, :], start=True, stop=True)
                    for y in range(4):
                        last = nc.tensor.matmul(ps[:, 4, y * P:(y + 1) * P], inv_t[:, y, :], prod[:, y, :],
                                                start=True, stop=True)
                    last.then_inc(*S["joined"].one((h, i)))
                if i == 6:
                    pe.wait_ge(*S["residual"].at(h))
                    pe.wait_ge(*S["inverse_t"].at((h, 6)))
                    for y in range(4):
                        last = nc.tensor.matmul(ps[:, 5, y * P:(y + 1) * P], prod[:, y, :], inv_t[:, y, :],
                                                start=True, stop=True)
                    last.then_inc(*S["correction"].one(h))

            def chain_first(h, i):
                if not (0 <= h < HEADS and 1 <= i < 4):
                    return
                for r in range(2):
                    t, b = chunk_of(i, r)
                    pe.wait_ge(*S["state_made"].at((h, i - 1, r)))
                    pe.wait_ge(*S["o_added"].at((h, i - 1, r)))
                    nc.tensor.matmul(ps[b:b + CHUNK, 6 + r, 0:P], w_feat[:, 2 * r + t, b:b + CHUNK], state[:, r, :],
                                     start=True, stop=True).then_inc(*S["recalled"].one((h, i, r)))

            def chain_second(h, i):
                if not (0 <= h < HEADS and i < 4):
                    return
                for r in range(2):
                    t, b = chunk_of(i, r)
                    y = 2 * r + t
                    if i:
                        pe.wait_ge(*S["values_new"].at((h, i, r)))
                    else:
                        pe.wait_ge(*S["values_made"].at((h, 3)))
                        pe.wait_ge(*S["w_feat_made"].at(h))
                        if h:
                            pe.wait_ge(*S["o_added"].at((h - 1, 3, r)))
                        elif r == 1:
                            pe.wait_ge(*S["exp_sums"].at())
                    out = ps[b:b + CHUNK, 6 + r, P:2 * P]
                    if i:
                        nc.tensor.matmul(out, q_feat[:, h % 2, y, b:b + CHUNK], state[:, r, :], start=True, stop=False)
                    nc.tensor.matmul(out, qk_ratio[:, h % 2, y, b:b + CHUNK], values[:, y, :], start=(i == 0), stop=True)\
                        .then_inc(*S["o_product"].one((h, i, r)))
                    if i < 3:
                        nc.tensor.matmul(ps[:, 6 + r, 2 * P:3 * P], k_rest[b:b + CHUNK, h % 2, y, :],
                                         values[b:b + CHUNK, y, :], start=True, stop=True)\
                            .then_inc(*S["state_product"].one((h, i, r)))

            def conv_norm(i):
                if i == 0:
                    pe.wait_ge(*S["taps31"].at((KT - 1, 31)))
                    for j in range(KT):
                        last = nc.tensor.matmul(ps[:, 2, 0:TOK], C("mean").broadcast_to([P, P]), cacc[:, j, :], start=(j == 0), stop=(j == KT - 1))
                    last.then_inc(*S["conv_mean"].one())
                if i == 1:
                    for q in range(4):
                        pe.wait_ge(*S["conv_squared"].at(q))
                        for j in range(2):
                            last = nc.tensor.matmul(ps[:, 2, TOK:2 * TOK], C("mean").broadcast_to([P, P]),
                                                    tanh[:, q % 2, j * TOK:(j + 1) * TOK],
                                                    start=(q == 0 and j == 0), stop=(q == 3 and j == 1))
                        last.then_inc(*S["conv_square_used"].one(q))
                if i == 2:
                    pe.wait_ge(*S["conv_rstd"].at())
                    for t in range(TT):
                        last = nc.tensor.matmul(ps[:, 2, t * P:(t + 1) * P], conv_rsd[:, t:t + 1].broadcast_to([P, P]), ident,
                                                start=True, stop=True)
                    last.then_inc(*S["conv_rstd_spread"].one())

            def turn_o():
                for t in range(TT):
                    pe.wait_ge(*S["o_final"].at((HEADS - 1, t)))
                    for half in range(2):
                        for i in range(4):
                            last = nc.tensor.transpose(ps[:, 4 + 2 * t + half, i * P:(i + 1) * P],
                                                       xn[:, t, (4 * half + i) * P:(4 * half + i + 1) * P], ident)
                        last.then_inc(*S["norm_turned"].one(("o", t, half)))

            def up(li, norm):
                for j in range(FT):
                    n = slot_of[(f"up{li}", j)]
                    pe.wait_ge(*weights_low(n))
                    if j >= 4:
                        pe.wait_ge(*(S["hidden"].at((li, j - 4)) if li == 2 else S["taps_done"].at((li, j - 4, 1))))
                    if li == 2 and j == 8:
                        pe.wait_ge(p_loaded, 32)
                        for kt in range(2):
                            for t in range(TT):
                                last = nc.tensor.transpose(ps[:, 4, kt * TOK + t * P:kt * TOK + (t + 1) * P],
                                                           p_tok[:, t, kt * P:(kt + 1) * P], ident)
                        last.then_inc(*S["p_turned"].one())
                    wh = used(whi, n).rearrange("p (k m c) -> p k m c", k=KT, m=2)
                    wl = used(wlo, n).rearrange("p (k m c) -> p k m c", k=KT, m=2)
                    for m in range(2):
                        for kt in range(KT):
                            if j + m == 0 and kt % 4 == 0:
                                for t in range(TT):
                                    wait_split(norm, t, (kt // 4,))
                            last = three(ps[:, j % 4, m * TOK:(m + 1) * TOK], wh[:, kt, m, :], wl[:, kt, m, :],
                                         xhi[:, kt, :], xlo[:, kt, :], kt == 0, kt == KT - 1)
                    last.then_inc(*S["weights_used"].one(n))

            pe.wait_ge(ident_loaded, 16)
            norm(0)
            for li, (layer, blocks) in enumerate(LAYERS):
                before = None
                for b in range(len(blocks)):
                    if b >= 2:
                        block_read(layer, blocks, b - 2)
                    columns(layer, blocks, b, 2 * li)
                    for c in turned_after(layer, b):
                        turn_block(layer, blocks, c, before)
                        before = c
                    if layer == "even" and b == 3:
                        index_scores()
                    if layer == "odd" and b == 2:
                        forget_sums()
                if blocks[-1][0] in TURNED:
                    turn_block(layer, blocks, len(blocks) - 1, before)
                attend(layer, blocks)
                for pair in range(8):
                    pe.wait_ge(*S["mixed_low"].at((layer, pair)))
                down(f"{layer}_out", KT, xhi, xlo, lambda kt: None)
                norm(2 * li + 1)
                up(li, 2 * li + 1)
                down(f"down{li}", FT, hhi, hlo, lambda kt: pe.wait_ge(*S["hidden_low"].at((li, kt))))
                if li == 0:
                    norm(2)

            norm(5)
            ab_channels()
            for r in range(len(ROUNDS)):
                for i in range(TICKS):
                    if r == 0 and i == 1:
                        decay_sums()
                    chain_first(r - 2, i)
                    level_first(r - 1, i)
                    if r == 9 and i == 0:
                        chain_second(r - 2, i)
                    if slot_at(r, i):
                        half_slot(slot_at(r, i), i % 2, 0)
                    if r < 9 or i:
                        chain_second(r - 2, i)
                    if i:
                        level_second(r - 1, i)
                    if slot_at(r, i):
                        half_slot(slot_at(r, i), i % 2, 1)
                    if i == 0:
                        level_second(r - 1, i)
                    prepare(r, i)
                    if r == 8:
                        conv_norm(i)
            turn_o()
            for t in range(TT):
                wait_split("o", t)
            for i in range(KT // 2):
                for m in range(2):
                    for part in range(2):
                        half_slot(("delta_out", i), m, part)
            for q in range(4):
                pe.wait_ge(*S["mix_low"].at(q))
            down("mix_out", KT, xhi, xlo, lambda kt: None)
            norm(6)
            up(2, 6)
            pe.wait_ge(*S["hidden"].at((2, FT - 1)))
            down("down2", FT, hhi2, hlo2, lambda kt: pe.wait_ge(*S["hidden_low"].at((2, kt))))
            pe.wait_ge(*S["p_low"].at())
            n = slot_of[("pl_proj", 0)]
            pe.wait_ge(*weights_low(n))
            wh = used(whi, n).rearrange("p (k c) -> p k c", k=2)
            wl = used(wlo, n).rearrange("p (k c) -> p k c", k=2)
            for t in range(TT):
                for half in range(2):
                    for kt in range(2):
                        c = slice(half * 512, (half + 1) * 512)
                        last = three(ps[:, 2 * t + half, :], phi[:, kt, t * P:(t + 1) * P], plo[:, kt, t * P:(t + 1) * P],
                                     wh[:, kt, c], wl[:, kt, c], kt == 0, kt == 1)
            last.then_inc(*S["weights_used"].one(n))
            norm(7)
            for t in range(TT):
                wait_split(7, t)
            for b in range(2):
                columns("gate", [(0, 512), (1, 512)], b, 7, 4)

        @block.scalar
        def _(act):
            split_to = [0]

            def split(last):
                while split_to[0] <= min(last, len(plan) - 1):
                    n = split_to[0]
                    act.wait_ge(weights_loaded[n % RAW], 16 * (n // RAW + 1))
                    if n >= RING:
                        act.wait_ge(*S["weights_used"].at(n - RING))
                    act.activation(used(whi, n), used(raw, n), ACT.Copy).then_inc(*S["weights_high"].one((n, 1)))
                    split_to[0] += 1

            def split_half(n, half):
                if half == 0:
                    act.wait_ge(weights_loaded[n % RAW], 16 * (n // RAW + 1))
                    act.wait_ge(*S["weights_used"].at(n - RING))
                c = slice(half * SLOT // 2, (half + 1) * SLOT // 2)
                act.activation(whi[:, n % RING, c], raw[:, n % RAW, c], ACT.Copy).then_inc(*S["weights_high"].one((n, half)))
                split_to[0] = n + 1

            def norm(k, turned=True):
                for t in range(TT):
                    if k == 0:
                        act.wait_ge(x_loaded[t], 16)
                    elif k == 5:
                        act.wait_ge(*S["normed"].at((4, t)))
                    else:
                        act.wait_ge(*S["x_added"].at((k, t, 1)))
                        if (k, t) == (4, TT - 1):
                            act.dma_start(gain_5, dram["gains"][5:6, :].broadcast_to([P, D])).then_inc(gain_5_loaded, 16)
                        act.wait_ge(*S["rstd_ready"].at((k - 1, t)))
                        act.wait_ge(*S["norm_turned"].at(("o" if k == 6 else k - 1, t, 1)))
                    act.activation(xn[:, t, :], x[:, t, :], ACT.Square, accum_out=sumsq[:, t:t + 1])\
                        .then_inc(*S["squared"].one((k, t)))
                if k == 0:
                    split(0)
                if k == 7:
                    split(slot_of[(("gate", 0), 1)])
                if turned:
                    round_turned(k)

            def round_turned(k):
                for t in range(TT):
                    for half in range(2):
                        act.wait_ge(*S["norm_turned"].at((k, t, half)))
                        act.activation(xhi[:, 4 * half:4 * half + 4, t * P:(t + 1) * P],
                                       ps[:, 4 + 2 * t + half, :].rearrange("p (i c) -> p i c", i=4), ACT.Copy)\
                            .then_inc(*S["norm_high"].one((k, t, half)))

            def copy_block(layer, blocks, b):
                key = blocks[b][0]
                n = slot_of[((layer, key), 1)]
                act.wait_ge(*S["weights_used"].at(n))
                for t in range(TT):
                    if key in TURNED:
                        dst = temp[:, b % 2, t, :]
                        if b >= 2 and blocks[b - 2][0] in TURNED:
                            act.wait_ge(*S["block_turned"].at((layer, b - 2, t)))
                    else:
                        dst = (v1 if key == "vb" else v0)[:, t, :]
                    act.activation(dst, ps[:, 2 * (b % 2) + t, :], ACT.Copy).then_inc(*S["copied"].one((layer, b, t)))

            def copy_turned(layer, blocks, b):
                key = blocks[b][0]
                tiles = TURNED[key]
                dst = fmi if key in ("idx", "kvf") else fm[:, FM_OF[key], :, :]
                for t in range(TT):
                    act.wait_ge(*S["block_turned"].at((layer, b, t)))
                    act.activation(dst[:, 0:tiles, t * P:(t + 1) * P],
                                   ps[:, 4 + t, 0:tiles * P].rearrange("p (i c) -> p i c", i=tiles), ACT.Copy)\
                        .then_inc(*S["turned_copied"].one((layer, b, t)))

            def index_relus():
                for u in range(8):
                    t = u % 2
                    act.wait_ge(*S["index_product"].at(u))
                    if u >= 2:
                        act.wait_ge(*S["index_sum"].at(u - 2))
                    act.activation(rel[:, u % 2, 0:P * (t + 1)], ps[:, 6 + u % 2, 0:P * (t + 1)], ACT.Relu)\
                        .then_inc(*S["index_relu"].one(u))

            def gate_logs():
                act.wait_ge(*S["gate_abs"].at())
                act.activation(gate[:, 2, :], gate[:, 1, :], ACT.Exp, scale=-1.0).then_inc(*S["gate_exp"].one())
                act.wait_ge(*S["gate_exp"].at())
                act.activation(gate[:, 3, :], gate[:, 2, :], ACT.Ln, bias=1.0).then_inc(*S["gate_ln"].one())

            def attend(layer):
                units = UNITS[layer]
                n = len(units)
                for u in range(n + 5):
                    if u < n:
                        kind, h, t = units[u]
                        act.wait_ge(*S["logits"].at((layer, u)))
                        act.activation(prob[:, u % 3, 0:P * (t + 1)], prob[:, u % 3, 0:P * (t + 1)], ACT.Exp,
                                       bias=lowest[:, u % 4:u % 4 + 1], scale=-1.0, accum_out=total[:, u % 4:u % 4 + 1])\
                            .then_inc(*S["exps"].one((layer, u)))
                        if kind == "D":
                            act.activation(sunk[:, u % 4:u % 4 + 1], nsink[:, h:h + 1], ACT.Exp,
                                           bias=lowest[:, u % 4:u % 4 + 1], scale=-1.0).then_inc(*S["sinks_done"].one(u))
                    if 2 <= u < n + 2:
                        v = u - 2
                        t = units[v][2]
                        act.wait_ge(*S["probs_turned"].at((layer, v)))
                        if v >= 2:
                            act.wait_ge(*S["values_done"].at((layer, v - 2)))
                        act.activation(probT[:, v % 2, 0:P * (t + 1)], ps[:, 2 + v % 2, 0:P * (t + 1)], ACT.Copy)\
                            .then_inc(*S["probs_copied"].one((layer, v)))
                    if u >= 4 and (u - 4) % 4 == 3:
                        pair = (u - 4) // 4
                        act.wait_ge(*S["values_done"].at((layer, u - 4)))
                        act.activation(xhi[:, SLOT_OF_PAIR[pair], :], ps[:, 4 + pair % 2, 0:TOK], ACT.Copy)\
                            .then_inc(*S["mixed_high"].one((layer, pair)))

            def up(li):
                act.wait_ge(params_loaded, 16)
                for j in range(FT + 2):
                    if j < FT:
                        n = slot_of[(f"up{li}", j)]
                        split(n + AHEAD)
                        act.wait_ge(*S["weights_used"].at(n))
                        if j >= 2:
                            act.wait_ge(*S["hidden"].at((li, j - 2)))
                        for m in range(2):
                            c = m * FT + j
                            act.activation(cv[:, j % 2, m, :], ps[:, j % 4, m * TOK:(m + 1) * TOK], ACT.Identity,
                                           bias=par_at(f"conv_b{li}", c), scale=par_at(f"conv_w{li}", 2 * 2 * FT + c))\
                                .then_inc(*S["conv_started"].one((li, j, m)))
                    if 1 <= j < FT + 1:
                        i = j - 1
                        act.wait_ge(*S["taps_done"].at((li, i, 0)))
                        act.activation(sg[:, i % 2, :], cv[:, i % 2, 0, :], ACT.Silu).then_inc(*S["gated"].one((li, i)))
                    if j >= 2:
                        i = j - 2
                        act.wait_ge(*S["hidden"].at((li, i)))
                        act.activation(hhi[:, i, :], hf[:, i % 2, :], ACT.Copy).then_inc(*S["hidden_high"].one((li, i)))

            def up2():
                for j in range(FT + 1):
                    if j == 9:
                        act.wait_ge(*S["p_turned"].at())
                        act.activation(phi[:, :, :], ps[:, 4, :].rearrange("p (k c) -> p k c", k=2), ACT.Copy)\
                            .then_inc(*S["p_high"].one())
                    if j < FT:
                        n = slot_of[("up2", j)]
                        split(n + AHEAD)
                        act.wait_ge(*S["weights_used"].at(n))
                        if j >= 2:
                            act.wait_ge(*S["hidden"].at((2, j - 2)))
                        act.activation(sg2[:, j % 2, :], ps[:, j % 4, 0:TOK], ACT.Silu).then_inc(*S["gated"].one((2, j)))
                    if j >= 1:
                        i = j - 1
                        act.wait_ge(*S["hidden"].at((2, i)))
                        act.activation(hhi2[:, i, :], hf2[:, i % 2, :], ACT.Copy).then_inc(*S["hidden_high"].one((2, i)))

            def evacuate(key):
                o, n = ORDINAL[key], slot_of[key]
                act.wait_ge(*S["weights_used"].at(n))
                src = ps[:, o % 2, :]
                if key[0] in ("qk", "v"):
                    c = ORDINAL_OF_CONV[key]
                    for m in range(2):
                        if c >= 2:
                            old = CONVS[c - 2]
                            act.wait_ge(*(S["qk_turned"] if old[0] == "qk" else S["v_turned"]).at(old[1]))
                        act.activation(conv[:, c % 2, m, :], src[:, m * TOK:(m + 1) * TOK], ACT.Copy,
                                       scale=par_at("taps5", 2 * 3 * HEADS + channel_tile(key, m)))\
                            .then_inc(*S["conv_begun"].one((key, m)))
                elif key[0] in ("glu", "z"):
                    if TANH_BEFORE[key]:
                        act.wait_ge(*tanh_free(TANH_BEFORE[key]))
                    if key[0] == "glu":
                        act.activation(tanh[:, TANH_OF[key], 0:TOK], src[:, TOK:2 * TOK], ACT.Tanh, scale=0.5)\
                            .then_inc(*S["tanh_made"].one(key))
                    else:
                        act.activation(tanh[:, TANH_OF[key], :], src, ACT.Tanh, scale=0.5).then_inc(*S["tanh_made"].one(key))
                elif key[0] == "gates":
                    act.activation(gts[:, :, key[1], :], src.rearrange("p (m c) -> p m c", m=2), ACT.Tanh, scale=0.5)\
                        .then_inc(*S["slot_read_act"].one(key))

            def conv_tanh(key):
                c = ORDINAL_OF_CONV[key]
                act.wait_ge(*S["taps5"].at((key, 1)))
                name = ("conv", key)
                if TANH_BEFORE[name]:
                    act.wait_ge(*tanh_free(TANH_BEFORE[name]))
                act.activation(tanh[:, TANH_OF[name], :].rearrange("p (m c) -> p m c", m=2), conv[:, c % 2, :, :], ACT.Tanh,
                               scale=0.5).then_inc(*S["tanh_made"].one(name))

            def prepare(h, i):
                if h >= HEADS:
                    return
                if i == 3:
                    act.wait_ge(*S["qk_turned"].at(h))
                    if h:
                        act.wait_ge(*S["qk_scaled"].at((h - 1, 3)))
                    for y in range(4):
                        if y == 0 and h:
                            act.wait_ge(*S["qk_ratio_made"].at(h - 1))
                        act.activation(ratio[:, y, :], ps[:, 2, y * P:(y + 1) * P], ACT.Square,
                                       accum_out=qk_sq[:, y:y + 1]).then_inc(*S["qk_squared"].one((h, y)))
                if i == 5:
                    act.wait_ge(*S["qk_back"].at(h))
                    if h:
                        act.wait_ge(*S["qk_products"].at(h - 1))
                    act.activation(qk_feat[:, :, :], ps[:, 3, :].rearrange("p (m c) -> p m c", m=2), ACT.Copy)\
                        .then_inc(*S["qk_feat_made"].one(h))
                    if h % 2 == 0:
                        act.wait_ge(*S["v_turned"].at(h // 2))
                        if h >= 4:
                            act.wait_ge(*S["solution"].at(h - 3))
                        act.activation(v_tok[:, h % 4:h % 4 + 2, :, :],
                                       ps[:, 2, :].rearrange("p (m t c) -> p m t c", m=2, t=2), ACT.Copy, scale=0.5)\
                            .then_inc(*S["v_made"].one(h // 2))
                if i == 6:
                    act.wait_ge(*S["ratio_started"].at(h))
                    for y in range(4):
                        r, t = y // 2, y % 2
                        act.activation(ratio[:, y, :], ratio[:, y, :], ACT.Exp,
                                       bias=neg_sum[:, t, r * 8 + h:r * 8 + h + 1]).then_inc(*S["ratio_made"].one((h, y)))

            def level(h, i):
                if not 0 <= h < HEADS:
                    return
                if i == 0:
                    act.wait_ge(*S["triangle_made"].at(h))
                    act.activation(upper_r[:, :, :], upper[:, :, :], ACT.Copy).then_inc(*S["upper_rounded"].one(h))

            def level_late(h, i):
                if not 0 <= h < HEADS:
                    return
                if i in (0, 1, 3):
                    for y in range(4):
                        r, t = y // 2, y % 2
                        column = t * 16 + r * 8 + h
                        if i == 0:
                            if y == 0 and h:
                                act.wait_ge(*S["q_decayed_turned"].at(h - 1))
                            act.activation(q_decayed[:, y, :], qk_tok[:, h % 2, 0, t, :], ACT.Copy,
                                           scale=exp_sum[:, column:column + 1]).then_inc(*S["q_decayed_made"].one((h, y)))
                        if i == 1:
                            act.activation(k_decayed[:, y, :], qk_tok[:, h % 2, 1, t, :], ACT.Copy,
                                           scale=exp_sum[:, column:column + 1]).then_inc(*S["k_decayed_made"].one((h, y)))
                        if i == 3:
                            act.activation(k_rest[:, h % 2, y, :], qk_tok[:, h % 2, 1, t, :], ACT.Copy,
                                           scale=exp_sum[:, 32 + column:33 + column])
                if i == 0:
                    act.wait_ge(*S["inverse_turned"].at(h))
                    act.activation(inv[:, :, :], ps[:, 4, :].rearrange("p (y c) -> p y c", y=4), ACT.Copy)\
                        .then_inc(*S["inverse_first"].one(h))
                if i == 2:
                    act.wait_ge(*S["q_decayed_turned"].at(h))
                    act.activation(q_feat[:, h % 2, :, :], ps[:, 3, :].rearrange("p (y c) -> p y c", y=4), ACT.Copy)\
                        .then_inc(*S["q_feat_made"].one(h))
                if 1 <= i <= 5:
                    act.wait_ge(*S["joined"].at((h, i)))
                    act.activation(inv[:, :, :], ps[:, 4, :].rearrange("p (y c) -> p y c", y=4), ACT.Copy)\
                        .then_inc(*S["inverse_done"].one((h, i)))
                    act.activation(inv_t[:, :, :], ps[:, 5, :].rearrange("p (y c) -> p y c", y=4), ACT.Copy)\
                        .then_inc(*S["inverse_t"].one((h, i + 1)))
                if i == 7:
                    act.wait_ge(*S["solution"].at(h))
                    if h:
                        act.wait_ge(*S["o_product"].at((h - 1, 3, 1)))
                    for y in range(4):
                        r, t = y // 2, y % 2
                        act.activation(values[:, y, :], ps[:, 4, y * P:(y + 1) * P], ACT.Copy,
                                       scale=beta[:, t, r * 8 + h:r * 8 + h + 1]).then_inc(*S["values_made"].one((h, y)))
                    act.activation(w_feat[:, :, :], ps[:, 5, :].rearrange("p (y c) -> p y c", y=4), ACT.Copy)\
                        .then_inc(*S["w_feat_made"].one(h))

            def finish(h, i):
                if not 0 <= h < HEADS:
                    return
                if i == 4:
                    act.wait_ge(*S["o_added"].at((h, 3, 1)))
                    for t in range(TT):
                        if h or t:
                            act.wait_ge(*S["o_squared"].at((h, t - 1) if t else (h - 1, TT - 1)))
                        act.activation(o_junk, o_tok[:, t, :], ACT.Square, accum_out=o_sq[:, t:t + 1])\
                            .then_inc(*S["o_squared"].one((h, t)))

            def conv_norm(i):
                if i == 1:
                    act.wait_ge(*S["conv_centered"].at())
                    for q in range(4):
                        act.wait_ge(*(S["conv_square_used"].at(q - 2) if q >= 2 else tanh_free(LAST_TANH[q])))
                        act.activation(tanh[:, q % 2, :].rearrange("p (m c) -> p m c", m=2), cacc[:, 2 * q:2 * q + 2, :],
                                       ACT.Square).then_inc(*S["conv_squared"].one(q))
                if i >= 6:
                    for q in range(2):
                        round_conv(2 * (i - 6) + q)
                if 3 <= i < 7:
                    q = i - 3
                    act.wait_ge(*S["conv_scaled"].at(q))
                    if q < 2:
                        act.wait_ge(*S["conv_square_used"].at(q + 2))
                    for m in range(2):
                        j = 2 * q + m
                        act.activation(cacc[:, j, :], cacc[:, j, :], ACT.Identity, scale=half_g[:, j:j + 1],
                                       bias=par_at("conv_ln_b_2", j)).then_inc(*S["conv_affine"].one(j))
                    act.wait_ge(*S["conv_affine"].at(2 * q + 1))
                    act.activation(tanh[:, q % 2, :].rearrange("p (m c) -> p m c", m=2), cacc[:, 2 * q:2 * q + 2, :],
                                   ACT.Tanh, scale=0.5).then_inc(*S["conv_tanh"].one(q))

            def round_conv(q):
                act.wait_ge(*S["conv_silu"].at(q))
                if q == 0:
                    act.wait_ge(*S["weights_used"].at(slot_of[("gates", KT - 1)]))
                act.activation(xhi[:, 2 * q:2 * q + 2, :], cacc[:, 2 * q:2 * q + 2, :], ACT.Copy).then_inc(*S["conv_high"].one(q))

            norm(0)
            split(AHEAD)
            for li, (layer, blocks) in enumerate(LAYERS):
                for b in range(len(blocks)):
                    split(slot_of[((layer, blocks[b][0]), 1)] + AHEAD)
                    if layer == "odd" and b == 0:
                        gate_logs()
                    if blocks[b][0] not in ROTATED:
                        copy_block(layer, blocks, b)
                    for c in turned_after(layer, b):
                        copy_turned(layer, blocks, c)
                    if layer == "even" and b == 3:
                        index_relus()
                if blocks[-1][0] in TURNED:
                    copy_turned(layer, blocks, len(blocks) - 1)
                attend(layer)
                for i in range(KT // 2):
                    split(slot_of[(f"{layer}_out", i)] + AHEAD - (i == KT // 2 - 1))
                norm(2 * li + 1)
                up(li)
                for i in range(FT // 2):
                    split(slot_of[(f"down{li}", i)] + AHEAD - (i == FT // 2 - 1))
                norm(2 * li + 2, turned=(li == 0))

            norm(5)
            split(slot_of["ab"] + AHEAD)
            act.wait_ge(*S["ab_abs"].at())
            act.activation(ab[:, 2, :, 0:16], ab[:, 1, :, 0:16], ACT.Exp, scale=-1.0).then_inc(*S["act_step"].one(0))
            act.activation(neg_rate[:, :], row_at["a_log_2"], ACT.Exp).then_inc(*S["act_step"].one(1))
            act.wait_ge(*S["act_step"].at(0))
            act.activation(ab[:, 3, :, 0:16], ab[:, 2, :, 0:16], ACT.Ln, bias=1.0).then_inc(*S["ab_ln"].one())
            act.activation(ab[:, 3, :, 16:32], ab[:, 0, :, 16:32], ACT.Tanh, scale=0.5).then_inc(*S["beta_tanh"].one())
            act.wait_ge(*S["decay_summed"].at())
            act.activation(exp_sum[:, :], ps[:, 7, 0:P], ACT.Exp).then_inc(*S["exp_sums"].one())
            act.wait_ge(*S["exp_sums"].at())
            act.wait_ge(*S["beta_ready"].at())
            for r in range(len(ROUNDS)):
                for i in range(TICKS):
                    level(r - 1, i)
                    if finished_slot(r, i):
                        evacuate(finished_slot(r, i))
                    if r < HEADS and i == 3:
                        conv_tanh(("qk", r))
                    if r < HEADS and r % 2 == 0 and i == 5:
                        conv_tanh(("v", r // 2))
                    if slot_at(r, i):
                        split_half(slot_of[slot_at(r, i)] + AHEAD, i % 2)
                    level_late(r - 1, i)
                    prepare(r, i)
                    finish(r - 2, i)
                    if r == 8:
                        conv_norm(i)
            act.wait_ge(*S["weights_used"].at(slot_of[("conv_out", 3)]))
            round_turned("o")
            for i in range(KT // 2):
                split(slot_of[("delta_out", i)] + AHEAD)
            for q in range(4):
                act.wait_ge(*S["mix_made"].at(q))
                act.wait_ge(*S["weights_used"].at(slot_of[("delta_out", 3)]))
                act.activation(xhi[:, 2 * q:2 * q + 2, :], gts[:, 0, 2 * q:2 * q + 2, :], ACT.Copy).then_inc(*S["mix_high"].one(q))
            for i in range(KT // 2):
                split(slot_of[("mix_out", i)] + AHEAD - (i == KT // 2 - 1))
            norm(6)
            up2()
            for i in range(FT // 2):
                split(slot_of[("down2", i)] + AHEAD - (i == FT // 2 - 1))
            norm(7)
            act.wait_ge(*S["weights_used"].at(slot_of[("pl_proj", 0)]))
            for t in range(TT):
                act.activation(pl[:, t, :], ps[:, 2 * t:2 * t + 2, :].rearrange("p a b -> p (a b)"), ACT.Copy)\
                    .then_inc(*S["pl_copied"].one(t))
            for t in range(TT):
                act.wait_ge(*S["pl_copied"].at(t))
                act.activation(pl_junk[:, t, :], pl[:, t, :], ACT.Square, accum_out=pl_sq[:, t:t + 1])\
                    .then_inc(*S["pl_squared"].one(t))
            for b in range(2):
                split(slot_of[(("gate", b), 1)] + AHEAD)
                for t in range(TT):
                    act.wait_ge(*summed(slot_of[(("gate", b), 1)], t))
                    if b:
                        act.wait_ge(*S["gate_tanh_used"].at((b - 1, t)))
                    act.activation(gate_tanh[:, t, :], ps[:, 4 + 2 * b + t, :], ACT.Tanh, scale=0.5)\
                        .then_inc(*S["gate_tanh_made"].one((b, t)))
            norm(8, turned=False)

        @block.vector
        def _(dve):
            steps, split_to = [0], [0]

            def link(ins):
                steps[0] += 1
                ins.then_inc(dve_step, 1)
                dve.wait_ge(dve_step, steps[0])

            def split(last):
                while split_to[0] <= min(last, len(plan) - 1):
                    n = split_to[0]
                    if n not in POOL_SLOTS:
                        dve.wait_ge(*S["weights_high"].at((n, 1)))
                        dve.tensor_tensor(used(wlo, n), used(raw, n), used(whi, n).bitcast(F32), ALU.subtract)\
                            .then_inc(*S["weights_low"].one((n, 1)))
                    split_to[0] += 1

            def split_half(n, half):
                if n not in POOL_SLOTS:
                    dve.wait_ge(*S["weights_high"].at((n, half)))
                    c = slice(half * SLOT // 2, (half + 1) * SLOT // 2)
                    dve.tensor_tensor(wlo[:, n % RING, c], raw[:, n % RAW, c], whi[:, n % RING, c].bitcast(F32),
                                      ALU.subtract).then_inc(*S["weights_low"].one((n, half)))
                split_to[0] = n + 1

            def normalize(k):
                if k == 5:
                    dve.wait_ge(gain_5_loaded, 16)
                else:
                    dve.wait_ge(gain_loaded, 16 * (k + 1 - (k > 5)))
                for t in range(TT):
                    dve.wait_ge(*S["rstd_ready"].at((k, t)))
                    for half in range(2):
                        c = slice(half * 512, (half + 1) * 512)
                        by = gain_5 if k == 5 else gain
                        dve.scalar_tensor_tensor((x if k == 4 else xn)[:, t, c], x[:, t, c], rstd[:, t:t + 1],
                                                 by[:, c], ALU.mult, ALU.mult)\
                            .then_inc(*S["normed"].one((k, t) if half else (k, t, "first half")))

            def norm(k):
                normalize(k)
                if k == 0:
                    split(0)
                if k == 7:
                    split(slot_of[(("gate", 0), 0)])
                lows(k)

            def lows(k):
                for t in range(TT):
                    for half in range(2):
                        dve.wait_ge(*S["norm_high"].at((k, t, half)))
                        at = (slice(None), slice(4 * half, 4 * half + 4), slice(t * P, (t + 1) * P))
                        dve.tensor_tensor(xlo[at], ps[:, 4 + 2 * t + half, :].rearrange("p (i c) -> p i c", i=4),
                                          xhi[at].bitcast(F32), ALU.subtract).then_inc(*S["norm_low"].one((k, t, half)))

            def add_quarter_to_x(k, n):
                for t in range(TT):
                    dve.wait_ge(*summed(n, t))
                    for half in range(2):
                        c = slice(half * 512, (half + 1) * 512)
                        dve.scalar_tensor_tensor(x[:, t, c], ps[:, 4 + 2 * t + half, :], 0.25, x[:, t, c], ALU.mult, ALU.add)\
                            .then_inc(*S["x_added"].one((k, t, half)))

            def add_to_x(k, n):
                for t in range(TT):
                    dve.wait_ge(*summed(n, t))
                    for half in range(2):
                        c = slice(half * 512, (half + 1) * 512)
                        dve.tensor_tensor(x[:, t, c], ps[:, 4 + 2 * t + half, :], x[:, t, c], ALU.add)\
                            .then_inc(*S["x_added"].one((k, t, half)))

            def rope(src, heads, t, dsts, read, done):
                cos = C("cos")[:, t * HD:(t + 1) * HD].unsqueeze(1)
                sin = C("sin")[:, t * HD:(t + 1) * HD].unsqueeze(1)
                a = rope_a[:, 0:heads * HD].rearrange("p (h d) -> p h d", h=heads)
                b = rope_b[:, 0:heads * HD].rearrange("p (h d) -> p h d", h=heads)
                dve.tensor_tensor(a, src, cos.broadcast_to([P, heads, HD]), ALU.mult)
                dve.tensor_tensor(b[:, :, 0:32], src[:, :, 32:64], sin[:, :, 0:32].broadcast_to([P, heads, 32]), ALU.mult)
                last = dve.tensor_tensor(b[:, :, 32:64], src[:, :, 0:32], sin[:, :, 32:64].broadcast_to([P, heads, 32]),
                                         ALU.mult)
                if read:
                    last.then_inc(*S["rope_read"].one(read))
                    dve.wait_ge(*S["rope_read"].at(read))
                else:
                    link(last)
                for i, dst in enumerate(dsts):
                    last = dve.tensor_tensor(dst, a, b, ALU.add)
                    if i < len(dsts) - 1 or not done:
                        link(last)
                    else:
                        last.then_inc(*S["rotated"].one(done))
                        dve.wait_ge(*S["rotated"].at(done))

            def heads_of(ap, n):
                return ap.rearrange("p (h d) -> p h d", h=n)

            def rope_block(layer, blocks, b):
                key = blocks[b][0]
                dve.wait_ge(*S["weights_used"].at(slot_of[((layer, key), 1)]))
                for t in range(TT):
                    src = ps[:, 2 * (b % 2) + t, :]
                    dst = temp[:, b % 2, t, :]
                    if b >= 2 and blocks[b - 2][0] in TURNED:
                        dve.wait_ge(*S["block_turned"].at((layer, b - 2, t)))
                    if key == "idx":
                        dve.tensor_copy(ks[:, 0, t, :], src[:, 256:320])
                        link(dve.tensor_copy(index_w[:, t, :], src[:, 320:324]))
                        rope(heads_of(src[:, 0:256], 4), 4, t, [heads_of(dst[:, 0:256], 4)], (layer, b, t), None)
                        if t:
                            split(slot_of[((layer, "ka"), 0)])
                        link(dve.tensor_reduce(key_mean[:, t:t + 1], ks[:, 0, t, :], AX.X, ALU.add))
                        link(dve.tensor_scalar(key_mean[:, t:t + 1], key_mean[:, t:t + 1], 1.0 / HD, None, ALU.mult))
                        link(dve.tensor_scalar(ks[:, 1, t, :], ks[:, 0, t, :], key_mean[:, t:t + 1], None, ALU.subtract))
                        dve.tensor_tensor_reduce(ks[:, 2, t, :], ks[:, 1, t, :], ks[:, 1, t, :], 1.0, 0.0, ALU.mult,
                                                 ALU.add, key_var[:, t:t + 1]).then_inc(*S["key_squares"].one(t))
                    elif key == "kvf":
                        dve.tensor_copy(v1[:, t, 0:P], src[:, P:2 * P])
                        dve.tensor_tensor(gate[:, 0, t * 8:t * 8 + 8], src[:, 256:264], row_at["forget_b"], ALU.add)
                        four = dst[:, 0:256].rearrange("p (g c d) -> p g c d", g=2, c=2)
                        rope(heads_of(src[:, 0:P], 2), 2, t, [four[:, :, 0, :], four[:, :, 1, :]], (layer, b, t), (layer, b, t))
                    else:
                        rope(heads_of(src, 8), 8, t, [heads_of(dst, 8)], (layer, b, t), (layer, b, t))
                if key == "idx":
                    dve.wait_ge(*S["key_rstd_ready"].at())
                    for t in range(TT):
                        dst = temp[:, b % 2, t, :]
                        link(dve.scalar_tensor_tensor(ks[:, 0, t, :], ks[:, 1, t, :], key_rstd[:, t:t + 1],
                                                      row_at["idx_k_ln_g"], ALU.mult, ALU.mult))
                        link(dve.tensor_tensor(ks[:, 1, t, :], ks[:, 0, t, :], row_at["idx_k_ln_b"], ALU.add))
                        rope(heads_of(ks[:, 1, t, :], 1), 1, t, [heads_of(dst[:, 256:320], 1), heads_of(dst[:, 320:384], 1)],
                             None, (layer, b, t))
                if key == "kvf":
                    link(dve.tensor_scalar(gate[:, 1, :], gate[:, 0, :], -1.0, None, ALU.mult))
                    dve.tensor_tensor(gate[:, 1, :], gate[:, 0, :], gate[:, 1, :], ALU.max).then_inc(*S["gate_abs"].one())

            def gate_finish():
                dve.wait_ge(*S["gate_ln"].at())
                link(dve.scalar_tensor_tensor(gate[:, 2, :], gate[:, 0, :], 0.0, gate[:, 3, :], ALU.min, ALU.subtract))
                dve.tensor_scalar(gate[:, 3, :], gate[:, 2, :], -8.0, None, ALU.mult).then_inc(*S["gate_ready"].one())
                dve.tensor_scalar(nsink[:, :], row_at["sinks"], -1.0, None, ALU.mult).then_inc(*S["nsink_ready"].one())

            def forget_biases():
                for h in range(8):
                    dve.wait_ge(*S["forget_sum"].at(h))
                    dve.tensor_tensor(bias[:, h, 0:P], ps[:, 6 + h % 2, 0:P], C("causal")[:, 0:P], ALU.add)
                    dve.tensor_tensor(bias[:, h, P:3 * P], ps[:, 6 + h % 2, 0:TOK], C("causal")[:, P:3 * P], ALU.add)\
                        .then_inc(*S["forget_bias"].one(h))
                dve.wait_ge(*S["forget_bias"].at(7))

            def index_sums():
                for u in range(8):
                    h, t = u // 2, u % 2
                    w = P * (t + 1)
                    dve.wait_ge(*S["index_relu"].at(u))
                    if h == 0:
                        last = dve.tensor_scalar(score[:, t, 0:w], rel[:, u % 2, 0:w], index_w[:, t, h:h + 1], None, ALU.mult)
                    else:
                        dve.wait_ge(*S["index_sum"].at(u - 2))
                        last = dve.scalar_tensor_tensor(score[:, t, 0:w], rel[:, u % 2, 0:w], index_w[:, t, h:h + 1],
                                                        score[:, t, 0:w], ALU.mult, ALU.add)
                    last.then_inc(*S["index_sum"].one(u))
                dve.wait_ge(*S["index_sum"].at(7))
                dve.memset(score[0:64, 0, 64:128], -1e30)
                link(dve.memset(score[0:64, 1, 192:256], -1e30))

            def take_top(rounds):
                for t in range(TT):
                    w = P * (t + 1)
                    for _ in range(rounds):
                        link(dve.max(top8[:, :], score[:, t, 0:w]))
                        link(dve.match_replace(score[:, t, 0:w], top8[:, :], score[:, t, 0:w], TAKEN))

            def pick():
                for t in range(TT):
                    w = P * (t + 1)
                    link(dve.tensor_scalar(picked[:, t, 0:w], score[:, t, 0:w], -2e38, MASKED, ALU.is_gt, ALU.mult))

            def attend(layer):
                units = UNITS[layer]
                n = len(units)
                for u in range(n + 6):
                    if u < n:
                        kind, h, t = units[u]
                        w = P * (t + 1)
                        dve.wait_ge(*S["products"].at((layer, u)))
                        if u >= 3:
                            dve.wait_ge(*S["probs_turned"].at((layer, u - 3)))
                        if kind == "B" and u < 2:
                            dve.wait_ge(*S["bias_ready"].at(1))
                        first = nsink[:, h:h + 1] if kind == "D" else 3e38
                        dve.tensor_tensor_reduce(prob[:, u % 3, 0:w], ps[:, LOGIT_BANKS[u % 3], 0:w], logit_bias(kind, h, t),
                                                 -0.125, first, ALU.add, ALU.min, lowest[:, u % 4:u % 4 + 1])\
                            .then_inc(*S["logits"].one((layer, u)))
                    if 1 <= u < n + 1:
                        v = u - 1
                        kind, h, t = units[v]
                        w = P * (t + 1)
                        sum_ = total[:, v % 4:v % 4 + 1]
                        dve.wait_ge(*S["exps"].at((layer, v)))
                        if kind == "D":
                            dve.wait_ge(*S["sinks_done"].at(v))
                            link(dve.tensor_tensor(sum_, sum_, sunk[:, v % 4:v % 4 + 1], ALU.add))
                        link(dve.reciprocal(inverse[:, v % 4:v % 4 + 1], sum_))
                        dve.tensor_scalar(prob[:, v % 3, 0:w], prob[:, v % 3, 0:w], inverse[:, v % 4:v % 4 + 1], None,
                                          ALU.mult).then_inc(*S["probs"].one((layer, v)))
                    if u >= 5 and (u - 5) % 4 == 3:
                        pair = (u - 5) // 4
                        kt = SLOT_OF_PAIR[pair]
                        dve.wait_ge(*S["mixed_high"].at((layer, pair)))
                        dve.tensor_tensor(xlo[:, kt, :], ps[:, 4 + pair % 2, 0:TOK], xhi[:, kt, :].bitcast(F32),
                                          ALU.subtract).then_inc(*S["mixed_low"].one((layer, pair)))

            def up(li):
                for j in range(FT + 2):
                    if j < FT:
                        split(slot_of[(f"up{li}", j)] + AHEAD)
                        for m in range(2):
                            dve.wait_ge(*S["conv_started"].at((li, j, 1)))
                            dve.scalar_tensor_tensor(cv[:, j % 2, m, 1:TOK], ps[:, j % 4, m * TOK:(m + 1) * TOK - 1],
                                                     par_at(f"conv_w{li}", 2 * FT + m * FT + j), cv[:, j % 2, m, 1:TOK],
                                                     ALU.mult, ALU.add).then_inc(*S["tap_one"].one((li, j, m)))
                        for m in range(2):
                            dve.wait_ge(*S["tap_one"].at((li, j, m)))
                            dve.scalar_tensor_tensor(cv[:, j % 2, m, 2:TOK], ps[:, j % 4, m * TOK:(m + 1) * TOK - 2],
                                                     par_at(f"conv_w{li}", m * FT + j), cv[:, j % 2, m, 2:TOK],
                                                     ALU.mult, ALU.add).then_inc(*S["taps_done"].one((li, j, m)))
                    if 1 <= j < FT + 1:
                        i = j - 1
                        dve.wait_ge(*S["gated"].at((li, i)))
                        dve.wait_ge(*S["taps_done"].at((li, i, 1)))
                        if i >= 2:
                            dve.wait_ge(*S["hidden_low"].at((li, i - 2)))
                        dve.tensor_tensor(hf[:, i % 2, :], sg[:, i % 2, :], cv[:, i % 2, 1, :], ALU.mult)\
                            .then_inc(*S["hidden"].one((li, i)))
                    if j >= 2:
                        i = j - 2
                        dve.wait_ge(*S["hidden_high"].at((li, i)))
                        dve.tensor_tensor(hlo[:, i, :], hf[:, i % 2, :], hhi[:, i, :].bitcast(F32), ALU.subtract)\
                            .then_inc(*S["hidden_low"].one((li, i)))

            def up2():
                for j in range(FT + 1):
                    if j == 9:
                        dve.wait_ge(*S["p_high"].at())
                        dve.tensor_tensor(plo[:, :, :], ps[:, 4, :].rearrange("p (k c) -> p k c", k=2),
                                          phi[:, :, :].bitcast(F32), ALU.subtract).then_inc(*S["p_low"].one())
                    if j < FT:
                        split(slot_of[("up2", j)] + AHEAD)
                        dve.wait_ge(*S["gated"].at((2, j)))
                        if j >= 2:
                            dve.wait_ge(*S["hidden_low"].at((2, j - 2)))
                        dve.tensor_tensor(hf2[:, j % 2, :], sg2[:, j % 2, :], ps[:, j % 4, TOK:2 * TOK], ALU.mult)\
                            .then_inc(*S["hidden"].one((2, j)))
                    if j >= 1:
                        i = j - 1
                        dve.wait_ge(*S["hidden_high"].at((2, i)))
                        dve.tensor_tensor(hlo2[:, i, :], hf2[:, i % 2, :], hhi2[:, i, :].bitcast(F32), ALU.subtract)\
                            .then_inc(*S["hidden_low"].one((2, i)))

            def decays():
                dve.wait_ge(*S["weights_used"].at(slot_of["ab"]))
                dve.tensor_copy(ab_feat[0:32, :], ps[0:32, 0, 0:TOK]).then_inc(*S["ab_copied"].one())
                split(slot_of["ab"] + AHEAD)
                dve.wait_ge(*S["ab_turned"].at())
                dve.wait_ge(params2_loaded, 16)
                link(dve.tensor_copy(ab[:, 0, :, :], ps[:, 0, TOK:TOK + 64].rearrange("p (t c) -> p t c", t=2)))
                dt = row_at["dt_bias_2"].unsqueeze(1).broadcast_to([P, TT, 16])
                link(dve.tensor_tensor(ab[:, 0, :, 0:16], ab[:, 0, :, 0:16], dt, ALU.add))
                link(dve.tensor_scalar(ab[:, 1, :, 0:16], ab[:, 0, :, 0:16], -1.0, None, ALU.mult))
                dve.tensor_tensor(ab[:, 1, :, 0:16], ab[:, 1, :, 0:16], ab[:, 0, :, 0:16], ALU.max).then_inc(*S["ab_abs"].one())
                dve.tensor_scalar(twice_b[:, :], par_at("conv_dw_b_2", 0, KT), 2.0, None, ALU.mult)
                dve.tensor_scalar(half_g[:, :], par_at("conv_ln_g_2", 0, KT), 0.5, None, ALU.mult)
                dve.wait_ge(*S["ab_ln"].at())
                link(dve.scalar_tensor_tensor(ab[:, 4, :, 0:16], ab[:, 0, :, 0:16], 0.0, ab[:, 3, :, 0:16], ALU.max, ALU.add))
                rate = neg_rate[:, :].unsqueeze(1).broadcast_to([P, TT, 16])
                dve.wait_ge(*S["act_step"].at(1))
                dve.scalar_tensor_tensor(decay[:, :, :], ab[:, 4, :, 0:16], -1.0, rate, ALU.mult, ALU.mult)\
                    .then_inc(*S["decay_ready"].one())
                dve.wait_ge(*S["beta_tanh"].at())
                link(dve.tensor_scalar(beta[:, :, :], ab[:, 3, :, 16:32], 0.5, 0.5, ALU.mult, ALU.add))
                dve.tensor_scalar(neg_beta[:, :, :], beta[:, :, :], -1.0, None, ALU.mult).then_inc(*S["beta_ready"].one())
                dve.wait_ge(*S["beta_ready"].at())
                dve.wait_ge(*S["exp_sums"].at())
                dve.tensor_scalar(neg_sum[:, :, :], ps[:, 7, 0:32].rearrange("p (t c) -> p t c", t=2), -1.0, None, ALU.mult)\
                    .then_inc(*S["neg_sum_made"].one())
                dve.wait_ge(*S["neg_sum_made"].at())

            def evacuate(key, part):
                if part and key[0] not in ("qk", "v"):
                    return
                o = ORDINAL[key]
                src = ps[:, o % 2, :]
                if key[0] in ("qk", "v"):
                    c = ORDINAL_OF_CONV[key]
                    for k in ((0, 1), (3, 4))[part]:
                        d = k - 2
                        for m in range(2):
                            if k == 0:
                                dve.wait_ge(*S["conv_begun"].at((key, 1)))
                            else:
                                dve.wait_ge(*S["tap5"].at((key, k_before[k], m)))
                            to, of = (slice(-d, TOK), slice(0, TOK + d)) if d < 0 else (slice(0, TOK - d), slice(d, TOK))
                            ins = dve.scalar_tensor_tensor(conv[:, c % 2, m, to], src[:, m * TOK:(m + 1) * TOK][:, of],
                                                           par_at("taps5", k * 3 * HEADS + channel_tile(key, m)),
                                                           conv[:, c % 2, m, to], ALU.mult, ALU.add)
                            ins.then_inc(*(S["taps5"].one((key, m)) if k == 4 else S["tap5"].one((key, k, m))))
                elif key[0] == "glu":
                    dve.wait_ge(*S["tanh_made"].at(key))
                    j = key[1]
                    if j == 0:
                        dve.wait_ge(*S["glu_cleared"].at())
                    if j >= 3:
                        dve.wait_ge(*S["taps31"].at((j - 3, 30)))
                    dve.scalar_tensor_tensor(glu_in[:, j % 3, 15:15 + TOK], tanh[:, TANH_OF[key], 0:TOK], 1.0, src[:, 0:TOK],
                                             ALU.add, ALU.mult).then_inc(*S["tanh_used"].one(key))
                elif key[0] == "z":
                    dve.wait_ge(*S["tanh_made"].at(key))
                    c = slice(key[1] * TOK, (key[1] + 1) * TOK)
                    dve.scalar_tensor_tensor(xn[:, :, c], tanh[:, TANH_OF[key], :].rearrange("p (t c) -> p t c", t=2), 1.0,
                                             src.rearrange("p (t c) -> p t c", t=2), ALU.add, ALU.mult)\
                        .then_inc(*S["tanh_used"].one(key))
                    dve.wait_ge(*S["tanh_used"].at(key))
                    view = xn[:, :, c].rearrange("p t (h c) -> p t h c", h=2)
                    for t in range(TT):
                        last = dve.tensor_tensor(view[:, t, :, :], view[:, t, :, :],
                                                 row_at["delta_norm_g_2"].unsqueeze(1).broadcast_to([P, 2, P]), ALU.mult)
                    last.then_inc(*S["z_made"].one(key[1]))
                elif key[0] == "conv_out":
                    dve.wait_ge(*S["weights_used"].at(slot_of[key]))
                    if key[1] == 0:
                        dve.wait_ge(*S["slot_read_act"].at(("gates", KT - 1)))
                    g = gts[:, 0, 2 * key[1]:2 * key[1] + 2, :]
                    dve.scalar_tensor_tensor(g, g, 1.0, src.rearrange("p (m c) -> p m c", m=2), ALU.add, ALU.mult)\
                        .then_inc(*S["conv_out_read"].one(key))
                elif key[0] == "delta_out":
                    dve.wait_ge(*S["weights_used"].at(slot_of[key]))
                    q = key[1]
                    g = gts[:, 1, 2 * q:2 * q + 2, :]
                    dve.scalar_tensor_tensor(g, g, 1.0, src.rearrange("p (m c) -> p m c", m=2), ALU.add, ALU.mult)\
                        .then_inc(*S["conv_out_read"].one(key))
                    dve.wait_ge(*S["conv_out_read"].at(key))
                    f = gts[:, 0, 2 * q:2 * q + 2, :]
                    dve.tensor_tensor(f, f, g, ALU.add).then_inc(*S["mix_made"].one(q))

            def conv_gate(key):
                c = ORDINAL_OF_CONV[key]
                name = ("conv", key)
                dve.wait_ge(*S["tanh_made"].at(name))
                dve.scalar_tensor_tensor(conv[:, c % 2, :, :], tanh[:, TANH_OF[name], :].rearrange("p (m c) -> p m c", m=2), 1.0,
                                         conv[:, c % 2, :, :], ALU.add, ALU.mult).then_inc(*S["conv_gated"].one(key))

            def long_taps(tick, part):
                taps = TAPS.get(tick, [])
                for j, k in taps[part * len(taps) // 2:(part + 1) * len(taps) // 2]:
                    src = glu_in[:, j % 3, k:k + TOK]
                    out = odd_taps[:, :] if k % 2 else cacc[:, j, :]
                    w = par_at("taps31", k * KT + j)
                    if k == 0:
                        dve.wait_ge(*S["tanh_used"].at(("glu", j)))
                        dve.tensor_scalar(out, src, w, twice_b[:, j:j + 1], ALU.mult, ALU.add)\
                            .then_inc(*S["taps31"].one((j, k)))
                    elif k == 1:
                        if j:
                            dve.wait_ge(*S["taps31"].at((j - 1, 31)))
                        dve.tensor_scalar(out, src, w, None, ALU.mult).then_inc(*S["taps31"].one((j, k)))
                    else:
                        dve.wait_ge(*S["taps31"].at((j, k - 2)))
                        dve.scalar_tensor_tensor(out, src, w, out, ALU.mult, ALU.add).then_inc(*S["taps31"].one((j, k)))
                    if k == 30:
                        dve.wait_ge(*S["taps31"].at((j, k)))
                        dve.tensor_tensor(out, out, odd_taps[:, :], ALU.add).then_inc(*S["taps31"].one((j, 31)))

            def prepare(h, i):
                if h >= HEADS:
                    return
                if i == 4:
                    dve.wait_ge(*S["qk_rstd_ready"].at(h))
                    for y in range(4):
                        scale = 0.5 * (P ** -0.5 if y < 2 else 1.0)
                        dve.tensor_scalar(qk_tok[:, h % 2, y // 2, y % 2, :], ps[:, 2, y * P:(y + 1) * P],
                                          qk_rstd[:, y:y + 1], scale, ALU.mult, ALU.mult).then_inc(*S["qk_scaled"].one((h, y)))
                if i == 6:
                    dve.wait_ge(*S["sums_spread"].at(h))
                    dve.tensor_tensor(four(ratio[:, :, :]), ps[:, 2, :].rearrange("p (r t c) -> p r t c", r=2, t=2),
                                      systems("off"), ALU.add).then_inc(*S["ratio_started"].one(h))
                if i == 7:
                    dve.wait_ge(*S["ratio_made"].at((h, 3)))
                    dve.wait_ge(*S["qk_products"].at(h))
                    kk = ps[:, 3, 0:TOK].rearrange("p (t c) -> p t c", t=2)
                    kq = ps[:, 3, TOK:2 * TOK].rearrange("p (t c) -> p t c", t=2)
                    if h:
                        dve.wait_ge(*S["check_product"].at(h - 1))
                    for y in range(4):
                        r, t = y // 2, y % 2
                        last = dve.scalar_tensor_tensor(upper[:, y, :], kk[:, t, :], beta[:, t, r * 8 + h:r * 8 + h + 1],
                                                        ratio[:, y, :], ALU.mult, ALU.mult)
                    last.then_inc(*S["upper_made"].one(h))
                    dve.wait_ge(*S["upper_made"].at(h))
                    dve.tensor_tensor(four(upper[:, :, :]), four(upper[:, :, :]), systems("strict"), ALU.mult)\
                        .then_inc(*S["strict_made"].one(h))
                    for r in range(2):
                        last = dve.tensor_tensor(qk_ratio[:, h % 2, 2 * r:2 * r + 2, :], kq, ratio[:, 2 * r:2 * r + 2, :],
                                                 ALU.mult)
                    last.then_inc(*S["qk_ratio_made"].one(h))

            def level_first(h, i):
                if not 0 <= h < HEADS:
                    return
                if 1 <= i <= 5:
                    dve.wait_ge(*S["join_product"].at((h, i)))
                    if i == 1 and h:
                        dve.wait_ge(*S["correction"].at(h - 1))
                    dve.tensor_tensor(four(prod[:, :, :]), ps[:, 4, :].rearrange("p (r t c) -> p r t c", r=2, t=2),
                                      systems(f"one_minus_join{LEVELS[i - 1]}"), ALU.mult)\
                        .then_inc(*S["prod_made"].one((h, i)))
                if i == 6:
                    dve.wait_ge(*S["check_product"].at(h))
                    dve.scalar_tensor_tensor(prod[:, :, :], ps[:, 4, :].rearrange("p (y c) -> p y c", y=4), -1.0,
                                             ident.unsqueeze(1).broadcast_to([P, 4, P]), ALU.mult, ALU.add).then_inc(*S["residual"].one(h))

            def level_second(h, i):
                if not 0 <= h < HEADS:
                    return
                if i == 6:
                    dve.wait_ge(*S["correction"].at(h))
                    dve.wait_ge(*S["inverse_t"].at((h, 6)))
                    dve.tensor_tensor(solved[:, :, :], ps[:, 5, :].rearrange("p (y c) -> p y c", y=4),
                                      inv_t[:, :, :].bitcast(F32), ALU.add).then_inc(*S["solution_sum"].one(h))

            def chain_first(h, i):
                if not (0 <= h < HEADS and 1 <= i < 4):
                    return
                for r in range(2):
                    t, b = chunk_of(i, r)
                    y = 2 * r + t
                    dve.wait_ge(*S["recalled"].at((h, i, r)))
                    dve.wait_ge(*S["values_made"].at((h, y)))
                    dve.scalar_tensor_tensor(values[b:b + CHUNK, y, :], ps[b:b + CHUNK, 6 + r, 0:P],
                                             neg_beta[b:b + CHUNK, t, r * 8 + h:r * 8 + h + 1], values[b:b + CHUNK, y, :],
                                             ALU.mult, ALU.add).then_inc(*S["values_new"].one((h, i, r)))

            def chain_second(h, i):
                if not (0 <= h < HEADS and i < 4):
                    return
                for r in range(2):
                    t, b = chunk_of(i, r)
                    if i < 3:
                        dve.wait_ge(*S["state_product"].at((h, i, r)))
                        new = ps[:, 6 + r, 2 * P:3 * P]
                        if i == 0:
                            last = dve.tensor_copy(state[:, r, :], new)
                        else:
                            column = 64 + (2 * t + b // CHUNK) * 16 + r * 8 + h
                            dve.wait_ge(*S["state_made"].at((h, i - 1, r)))
                            last = dve.scalar_tensor_tensor(state[:, r, :], state[:, r, :], exp_sum[:, column:column + 1],
                                                            new, ALU.mult, ALU.add)
                        last.then_inc(*S["state_made"].one((h, i, r)))
                    else:
                        dve.wait_ge(*S["o_product"].at((h, i, r)))
                    out = o_tok[b:b + CHUNK, t, :]
                    got = ps[b:b + CHUNK, 6 + r, P:2 * P]
                    if i < 2:
                        last = dve.tensor_copy(out, got)
                    else:
                        dve.wait_ge(*S["o_added"].at((h, 3 - i, 1 - r)))
                        last = dve.tensor_tensor(out, got, out, ALU.add)
                    last.then_inc(*S["o_added"].one((h, i, r)))

            def finish(h, i):
                if not 0 <= h < HEADS:
                    return
                if i == 5:
                    dve.wait_ge(*S["o_rstd_ready"].at(h))
                    dve.wait_ge(*S["z_made"].at(h // 2))
                    for t in range(TT):
                        at = xn[:, t, h * P:(h + 1) * P]
                        dve.scalar_tensor_tensor(at, o_tok[:, t, :], o_rstd[:, t:t + 1], at, ALU.mult, ALU.mult)\
                            .then_inc(*S["o_final"].one((h, t)))

            def conv_norm(i):
                if i == 0:
                    dve.wait_ge(*S["conv_mean"].at())
                    mean = ps[:, 2, 0:TOK].unsqueeze(1).broadcast_to([P, KT, TOK])
                    dve.tensor_tensor(cacc[:, :, :], cacc[:, :, :], mean, ALU.subtract).then_inc(*S["conv_centered"].one())
                if i == 1:
                    dve.wait_ge(*S["conv_square_used"].at(3))
                    for t in range(TT):
                        last = dve.tensor_tensor_reduce(glu_in[:, t, 0:P], ps[:, 2, TOK + t * P:TOK + (t + 1) * P], ident,
                                                        0.25, 1e-5, ALU.mult, ALU.add, conv_rsd[:, t:t + 1])
                    last.then_inc(*S["conv_var"].one())
                if 4 <= i < 8:
                    q = i - 4
                    at = cacc[:, 2 * q:2 * q + 2, :]
                    dve.wait_ge(*S["conv_tanh"].at(q))
                    dve.scalar_tensor_tensor(at, tanh[:, q % 2, :].rearrange("p (m c) -> p m c", m=2), 1.0, at,
                                             ALU.add, ALU.mult).then_inc(*S["conv_silu"].one(q))
                if 3 <= i < 7:
                    q = i - 3
                    if q == 0:
                        dve.wait_ge(*S["conv_rstd_spread"].at())
                    at = cacc[:, 2 * q:2 * q + 2, :]
                    dve.tensor_tensor(at, at, ps[:, 2, 0:TOK].unsqueeze(1).broadcast_to([P, 2, TOK]), ALU.mult)\
                        .then_inc(*S["conv_scaled"].one(q))
                if i >= 6:
                    for q in range(2):
                        low_conv(2 * (i - 6) + q)

            def low_conv(q):
                dve.wait_ge(*S["conv_high"].at(q))
                at = (slice(None), slice(2 * q, 2 * q + 2), slice(None))
                dve.tensor_tensor(xlo[at], cacc[at], xhi[at].bitcast(F32), ALU.subtract).then_inc(*S["conv_low"].one(q))

            norm(0)
            for li, (layer, blocks) in enumerate(LAYERS):
                for b in range(len(blocks)):
                    split(slot_of[((layer, blocks[b][0]), 1)] + AHEAD)
                    if layer == "even" and b >= 4:
                        take_top(TOP_ROUNDS[b - 4])
                    if layer == "odd" and b == 1:
                        gate_finish()
                    if layer == "even" and b == 0:
                        dve.wait_ge(consts_loaded, 16)
                        dve.wait_ge(rows_loaded, 16)
                    if blocks[b][0] in ROTATED:
                        rope_block(layer, blocks, b)
                    if layer == "even" and b == 3:
                        index_sums()
                    if layer == "odd" and b == 2:
                        forget_biases()
                if layer == "even":
                    pick()
                else:
                    dve.wait_ge(*S["nsink_ready"].at())
                attend(layer)
                for i in range(KT // 2):
                    split(slot_of[(f"{layer}_out", i)] + AHEAD - (i == KT // 2 - 1))
                add_to_x(2 * li + 1, slot_of[(f"{layer}_out", KT // 2 - 1)])
                norm(2 * li + 1)
                up(li)
                for i in range(FT // 2):
                    split(slot_of[(f"down{li}", i)] + AHEAD - (i == FT // 2 - 1))
                add_to_x(2 * li + 2, slot_of[(f"down{li}", FT // 2 - 1)])
                if li == 0:
                    norm(2)
            normalize(4)
            norm(5)
            split(slot_of["ab"])
            decays()
            for r in range(len(ROUNDS)):
                for i in range(TICKS):
                    chain_first(r - 2, i)
                    level_first(r - 1, i)
                    if i == 7:
                        prepare(r, i)
                    if finished_slot(r, i):
                        evacuate(finished_slot(r, i), 0)
                    if r < HEADS and i == 3:
                        conv_gate(("qk", r))
                    if r < HEADS and r % 2 == 0 and i == 5:
                        conv_gate(("v", r // 2))
                    long_taps(r * TICKS + i, 0)
                    chain_second(r - 2, i)
                    level_second(r - 1, i)
                    if i != 7:
                        prepare(r, i)
                    finish(r - 2, i)
                    if finished_slot(r, i):
                        evacuate(finished_slot(r, i), 1)
                    if slot_at(r, i):
                        split_half(slot_of[slot_at(r, i)] + AHEAD, i % 2)
                    long_taps(r * TICKS + i, 1)
                    if r == 8:
                        conv_norm(i)
            evacuate(("conv_out", KT // 2 - 1), 0)
            lows("o")
            for i in range(KT // 2):
                split(slot_of[("delta_out", i)] + AHEAD)
                evacuate(("delta_out", i), 0)
            for q in range(4):
                at = (slice(None), slice(2 * q, 2 * q + 2), slice(None))
                dve.wait_ge(*S["mix_high"].at(q))
                dve.tensor_tensor(xlo[at], gts[:, 0, 2 * q:2 * q + 2, :], xhi[at].bitcast(F32), ALU.subtract)\
                    .then_inc(*S["mix_low"].one(q))
            for i in range(KT // 2):
                split(slot_of[("mix_out", i)] + AHEAD - (i == KT // 2 - 1))
            add_quarter_to_x(6, slot_of[("mix_out", KT // 2 - 1)])
            norm(6)
            up2()
            for i in range(FT // 2):
                split(slot_of[("down2", i)] + AHEAD - (i == FT // 2 - 1))
            add_to_x(7, slot_of[("down2", FT // 2 - 1)])
            norm(7)
            split(slot_of[(("gate", 0), 1)])
            dve.wait_ge(*S["pl_rstd_ready"].at())
            for t in range(TT):
                dve.scalar_tensor_tensor(pl[:, t, :], pl[:, t, :], pl_rstd[:, t:t + 1], pl_gain[:, :], ALU.mult, ALU.mult)\
                    .then_inc(*S["pl_made"].one(t))
            for b in range(2):
                split(slot_of[(("gate", b), 1)] + AHEAD)
                for t in range(TT):
                    c = slice(b * 512, (b + 1) * 512)
                    dve.wait_ge(*S["gate_tanh_made"].at((b, t)))
                    dve.wait_ge(*S["pl_made"].at(t))
                    g = gate_tanh[:, t, :]
                    link(dve.scalar_tensor_tensor(g, g, 1.0, pl[:, t, c], ALU.add, ALU.mult))
                    last = dve.scalar_tensor_tensor(x[:, t, c], g, 0.5, x[:, t, c], ALU.mult, ALU.add)
                    last.then_inc(*(S["x_added"].one((8, t, 1)) if b else S["gate_tanh_used"].one((b, t))))
            normalize(NORMS - 1)
        return {name: event.values for name, event in S.items()}


FM_OF = {"qa": 0, "ka": 1, "qb": 2, "kb": 3, "qd": 0, "qc": 1, "kc": 2}


def pack_distances(inputs):
    q = np.arange(P)[:, None]
    distance = np.concatenate([t * P + q - np.arange(P * (t + 1))[None] for t in range(TT)], 1)
    return inputs["rel_bias"][0][:, distance + 256].transpose(1, 0, 2).reshape(P, -1)


def arrays(inputs):
    return {
        "x": inputs["x"][0], "p": inputs["p_2"][0, 0], "stream": pack_stream(inputs), "ident": np.eye(P, dtype=np.float32),
        "consts1": constants_1()[0], "consts2": constants_2()[0],
        "params1": pack_params_1(inputs)[0], "params2": pack_params_2(inputs)[0],
        "gains": pack_gains(inputs), "rows": pack_rows(inputs),
        "rel": pack_distances(inputs),
    }


def kernel(**inputs):
    import concourse.bacc as bacc
    from concourse.bass_utils import run_bass_kernel_spmd

    data = arrays({name: np.asarray(a) for name, a in inputs.items()})

    def make(counted):
        nc = bacc.Bacc("TRN2", target_bir_lowering=False, num_devices=1)
        dram = {name: nc.dram_tensor(f"in_{name}", a.shape, F32, kind="ExternalInput").ap() for name, a in data.items()}
        dram["out"] = nc.dram_tensor("out", [TOK, D], F32, kind="ExternalOutput").ap()
        return nc, build(nc, dram, counted)

    _, counted = make({})
    nc, _ = make(counted)
    r = run_bass_kernel_spmd(nc, [{f"in_{name}": a for name, a in data.items()}], core_ids=[0])
    return r.results[0]["out"].reshape(1, TOK, D)
```
